# Optimizing a Trainium2 kernel written in Bass

```python
import jax, jax.numpy as jnp
from jax import lax
import numpy as np

D_MODEL = 1024
BATCH = 1
SEQ = 512
DEPTH = 2

N_MIXERS = 2
N_MLA = (DEPTH + 1) // 2
N_HGRN = DEPTH // 2

MLA_HEADS = 8
MLA_Q_LORA = 512
MLA_KV_LORA = 256
MLA_NOPE = 128
MLA_ROPE = 64
MLA_V = 128
ROPE_BASE = 10000.0
ATTN_BLOCK = 128

HGRN_HEADS = 8
HGRN_DK = D_MODEL // HGRN_HEADS
HGRN_DV = D_MODEL // HGRN_HEADS
HGRN_CHUNK = 32

D_FF = 4 * D_MODEL

EPS = 1e-6


def rms_norm(x, g):
    xf = x.astype(jnp.float32)
    y = xf * lax.rsqrt(jnp.mean(xf * xf, axis=-1, keepdims=True) + EPS)
    return (y * g.astype(jnp.float32)).astype(x.dtype)

def rope_cos_sin(positions):
    inv_freq = jnp.power(ROPE_BASE, -jnp.arange(0, MLA_ROPE, 2, dtype=jnp.float32) / MLA_ROPE)
    ang = positions.astype(jnp.float32)[..., None] * inv_freq
    return jnp.cos(ang), jnp.sin(ang)

def apply_rope(t, cos, sin):
    tf = t.astype(jnp.float32)
    t1, t2 = jnp.split(tf, 2, axis=-1)
    return jnp.concatenate([t1 * cos - t2 * sin, t1 * sin + t2 * cos], axis=-1).astype(t.dtype)

def mla_mixer(h, cos, sin, w_in, q_norm, kv_norm, w_uq, w_ukv, w_o):
    B, S, _ = h.shape
    H = MLA_HEADS
    proj = h @ w_in
    c_q, c_kv, k_r = jnp.split(proj, [MLA_Q_LORA, MLA_Q_LORA + MLA_KV_LORA], axis=-1)
    q = (rms_norm(c_q, q_norm) @ w_uq).reshape(B, S, H, MLA_NOPE + MLA_ROPE)
    q_nope = q[..., :MLA_NOPE]
    q_rope = apply_rope(q[..., MLA_NOPE:], cos[:, :, None, :], sin[:, :, None, :])
    kv = (rms_norm(c_kv, kv_norm) @ w_ukv).reshape(B, S, H, MLA_NOPE + MLA_V)
    k_nope, v = kv[..., :MLA_NOPE], kv[..., MLA_NOPE:]
    k_rope = apply_rope(k_r, cos, sin)
    scale = (MLA_NOPE + MLA_ROPE) ** -0.5
    nb = S // ATTN_BLOCK
    qn_b = q_nope.reshape(B, nb, ATTN_BLOCK, H, MLA_NOPE).transpose(1, 0, 2, 3, 4)
    qr_b = q_rope.reshape(B, nb, ATTN_BLOCK, H, MLA_ROPE).transpose(1, 0, 2, 3, 4)
    k_pos = jnp.arange(S)

    def block(args):
        qn, qr, blk = args
        s = (jnp.einsum('bqhd,bkhd->bhqk', qn, k_nope)
             + jnp.einsum('bqhr,bkr->bhqk', qr, k_rope)).astype(jnp.float32) * scale
        q_pos = blk * ATTN_BLOCK + jnp.arange(ATTN_BLOCK)
        s = jnp.where(q_pos[:, None] >= k_pos[None, :], s, -jnp.inf)
        p = jax.nn.softmax(s, axis=-1).astype(v.dtype)
        return jnp.einsum('bhqk,bkhd->bqhd', p, v)

    o = lax.map(block, (qn_b, qr_b, jnp.arange(nb)))
    o = o.transpose(1, 0, 2, 3, 4).reshape(B, S, H * MLA_V)
    return o @ w_o

def hgrn2_mixer(h, lb, w_in, o_norm, w_o):
    B, S, _ = h.shape
    H, DK, DV, C = HGRN_HEADS, HGRN_DK, HGRN_DV, HGRN_CHUNK
    nc = S // C
    HK, HV = H * DK, H * DV
    proj = h @ w_in
    q_x, f_x, i_x, g_x = jnp.split(proj, [HK, 2 * HK, 2 * HK + HV], axis=-1)

    def heads(t, d):
        return t.astype(jnp.float32).reshape(B, nc, C, H, d).transpose(0, 3, 1, 2, 4)

    f = lb + (1.0 - lb) * jax.nn.sigmoid(f_x.astype(jnp.float32))
    q = heads(jax.nn.silu(q_x.astype(jnp.float32)), DK)
    k = heads(1.0 - f, DK)
    log_f = heads(jnp.log(f), DK)
    v = heads(i_x, DV)

    b = jnp.cumsum(log_f, axis=3)
    b_ref = b[:, :, :, C // 2:C // 2 + 1, :]
    b_last = b[:, :, :, -1:, :]
    q_rel = q * jnp.exp(b - b_ref)
    k_rel = k * jnp.exp(b_ref - b)
    causal = jnp.tril(jnp.ones((C, C), dtype=bool))
    a = jnp.where(causal, jnp.einsum('bhncd,bhnsd->bhncs', q_rel, k_rel), 0.0)
    o_intra = jnp.einsum('bhncs,bhnse->bhnce', a, v)

    q_dec = q * jnp.exp(b)
    k_dec = k * jnp.exp(b_last - b)
    chunk_decay = jnp.exp(b_last[:, :, :, 0, :])

    def step(state, xs):
        qd, kd, vc, dec = xs
        o_inter = jnp.einsum('bhcd,bhde->bhce', qd, state)
        state = dec[..., None] * state + jnp.einsum('bhcd,bhce->bhde', kd, vc)
        return state, o_inter

    mv = lambda t: jnp.moveaxis(t, 2, 0)
    s0 = jnp.zeros((B, H, DK, DV), jnp.float32)
    _, o_inter = lax.scan(step, s0, (mv(q_dec), mv(k_dec), mv(v), mv(chunk_decay)))
    o = o_intra + jnp.moveaxis(o_inter, 0, 2)
    o = o.transpose(0, 2, 3, 1, 4).reshape(B, S, H, DV)
    gate = jax.nn.silu(g_x.astype(jnp.float32)).reshape(B, S, H, DV)
    o = rms_norm(o, o_norm) * gate
    return o.reshape(B, S, HV).astype(h.dtype) @ w_o

def sq_relu_mlp(h, w1, w2):
    a = jax.nn.relu(h @ w1)
    return (a * a) @ w2

def first_inputs(seed: int = 0) -> dict:
    key = jax.random.key(seed)
    ks = jax.random.split(key, 16)
    f32 = jnp.float32
    nrm = lambda k, shape, fan_in: jax.random.normal(k, shape, f32) * (fan_in ** -0.5)
    mla_in_w = MLA_Q_LORA + MLA_KV_LORA + MLA_ROPE
    hgrn_in_w = 3 * HGRN_HEADS * HGRN_DK + HGRN_HEADS * HGRN_DV
    return {
        "x": jax.random.normal(ks[0], (BATCH, SEQ, D_MODEL), f32),
        "positions": jnp.broadcast_to(jnp.arange(SEQ, dtype=jnp.int32), (BATCH, SEQ)),
        "norm_gains": 1.0 + 0.1 * jax.random.normal(ks[1], (DEPTH, 4, D_MODEL), f32),
        "mla_w_in": nrm(ks[2], (N_MLA, D_MODEL, mla_in_w), D_MODEL),
        "mla_q_norm": 1.0 + 0.1 * jax.random.normal(ks[3], (N_MLA, MLA_Q_LORA), f32),
        "mla_kv_norm": 1.0 + 0.1 * jax.random.normal(ks[4], (N_MLA, MLA_KV_LORA), f32),
        "mla_w_uq": nrm(ks[5], (N_MLA, MLA_Q_LORA, MLA_HEADS * (MLA_NOPE + MLA_ROPE)), MLA_Q_LORA),
        "mla_w_ukv": nrm(ks[6], (N_MLA, MLA_KV_LORA, MLA_HEADS * (MLA_NOPE + MLA_V)), MLA_KV_LORA),
        "mla_w_o": nrm(ks[7], (N_MLA, MLA_HEADS * MLA_V, D_MODEL), MLA_HEADS * MLA_V),
        "hgrn_w_in": nrm(ks[8], (N_HGRN, D_MODEL, hgrn_in_w), D_MODEL),
        "hgrn_lb_logits": 0.1 * jax.random.normal(ks[9], (DEPTH, HGRN_HEADS * HGRN_DK), f32),
        "hgrn_o_norm": 1.0 + 0.1 * jax.random.normal(ks[10], (N_HGRN, HGRN_DV), f32),
        "hgrn_w_o": nrm(ks[11], (N_HGRN, HGRN_HEADS * HGRN_DV, D_MODEL), HGRN_HEADS * HGRN_DV),
        "mlp_w1": nrm(ks[12], (DEPTH, D_MODEL, D_FF), D_MODEL),
        "mlp_w2": nrm(ks[13], (DEPTH, D_FF, D_MODEL), D_FF),
    }

def first_block(x, positions, norm_gains, mla_w_in, mla_q_norm, mla_kv_norm, mla_w_uq, mla_w_ukv,
              mla_w_o, hgrn_w_in, hgrn_lb_logits, hgrn_o_norm, hgrn_w_o, mlp_w1, mlp_w2):
    cos, sin = rope_cos_sin(positions)
    p = jax.nn.softmax(hgrn_lb_logits.astype(jnp.float32), axis=0)
    lower_bounds = jnp.cumsum(p, axis=0) - p[0]
    h = x
    for layer in range(DEPTH):
        slot = layer // N_MIXERS
        a = rms_norm(h, norm_gains[layer, 0])
        if layer % N_MIXERS == 0:
            m = mla_mixer(a, cos, sin, mla_w_in[slot], mla_q_norm[slot], mla_kv_norm[slot],
                          mla_w_uq[slot], mla_w_ukv[slot], mla_w_o[slot])
        else:
            m = hgrn2_mixer(a, lower_bounds[layer], hgrn_w_in[slot], hgrn_o_norm[slot], hgrn_w_o[slot])
        h = h + rms_norm(m, norm_gains[layer, 1])
        a = rms_norm(h, norm_gains[layer, 2])
        h = h + rms_norm(sq_relu_mlp(a, mlp_w1[layer], mlp_w2[layer]), norm_gains[layer, 3])
    return h


CHUNK = 64
Q_BLOCK = 128
A_HEADS = 8
A_LAT = 128
IDX_HEADS = 8
IDX_DIM = 64
TOPK_MAX = 256
A_Q_COLS = A_HEADS * A_LAT
A_IN_COLS = A_Q_COLS + A_LAT + IDX_HEADS * IDX_DIM + IDX_DIM + IDX_HEADS
B_HEADS = D_MODEL // 256
B_DK = D_MODEL // B_HEADS
B_DV = 2 * B_DK
B_IN_COLS = 2 * D_MODEL + 2 * (B_HEADS * B_DV)
D_FF_2 = 2816
CONV_W = 3
N_A = (DEPTH + N_MIXERS - 1) // N_MIXERS
N_B = DEPTH // N_MIXERS


def rms_norm_2(x, g):
    xf = x.astype(jnp.float32)
    y = xf * lax.rsqrt(jnp.mean(xf * xf, axis=-1, keepdims=True) + EPS)
    return (y * g.astype(jnp.float32)).astype(x.dtype)

def dsa_mixer(h, w_in, q_g, k_g, iq_g, ik_g, w_out):
    bsz, seq, _ = h.shape
    topk = min(TOPK_MAX, seq // 4)
    proj = h @ w_in
    o1 = A_Q_COLS
    o2 = o1 + A_LAT
    o3 = o2 + IDX_HEADS * IDX_DIM
    o4 = o3 + IDX_DIM
    q = proj[..., :o1].reshape(bsz, seq, A_HEADS, A_LAT)
    c = proj[..., o1:o2]
    qi = proj[..., o2:o3].reshape(bsz, seq, IDX_HEADS, IDX_DIM)
    ki = rms_norm_2(proj[..., o3:o4], ik_g)
    wi = proj[..., o4:] * (IDX_HEADS ** -0.5 * IDX_DIM ** -0.5)
    q = rms_norm_2(q, q_g) * (A_LAT ** -0.5)
    k = rms_norm_2(c, k_g)
    qi = rms_norm_2(qi, iq_g)

    nb = seq // Q_BLOCK

    def to_blocks(a):
        return a.reshape(bsz, nb, Q_BLOCK, *a.shape[2:]).swapaxes(0, 1)

    t_blk = jnp.arange(seq, dtype=jnp.int32).reshape(nb, Q_BLOCK)
    key_pos = jnp.arange(seq, dtype=jnp.int32)
    gather = jax.vmap(lambda a, idx: a[idx])

    def block(args):
        qb, qib, wb, tb = args
        limit = (tb // CHUNK + 1) * CHUNK
        admissible = key_pos[None, :] < limit[:, None]
        rel = jax.nn.relu(jnp.einsum('bqhd,bsd->bqhs', qib, ki).astype(jnp.float32))
        score = jnp.einsum('bqhs,bqh->bqs', rel, wb.astype(jnp.float32))
        score = jnp.where(admissible[None], score, -jnp.inf)
        _, idx = lax.top_k(score, topk)
        valid = idx < limit[None, :, None]
        k_sel = gather(k, idx)
        v_sel = gather(c, idx)
        logits = jnp.einsum('bqhd,bqkd->bqhk', qb, k_sel).astype(jnp.float32)
        logits = jnp.where(valid[:, :, None, :], logits, -jnp.inf)
        p = jax.nn.softmax(logits, axis=-1).astype(v_sel.dtype)
        return jnp.einsum('bqhk,bqkd->bqhd', p, v_sel)

    o = lax.map(block, (to_blocks(q), to_blocks(qi), to_blocks(wi), t_blk))
    o = o.swapaxes(0, 1).reshape(bsz, seq, A_Q_COLS)
    return o @ w_out

def rotary(x):
    seq, d = x.shape[1], x.shape[-1]
    inv = 1.0 / (ROPE_BASE ** (jnp.arange(0, d, 2, dtype=jnp.float32) / d))
    ang = jnp.arange(seq, dtype=jnp.float32)[:, None] * inv[None, :]
    cos = jnp.cos(ang)[None, :, None, :]
    sin = jnp.sin(ang)[None, :, None, :]
    xf = x.astype(jnp.float32)
    x1, x2 = xf[..., : d // 2], xf[..., d // 2:]
    return jnp.concatenate([x1 * cos - x2 * sin, x1 * sin + x2 * cos], axis=-1)

def retention_mixer(h, w_in, out_g, w_out):
    bsz, seq, _ = h.shape
    nc = seq // CHUNK
    proj = h @ w_in
    dq = B_HEADS * B_DK
    dv = B_HEADS * B_DV
    q = rotary(proj[..., :dq].reshape(bsz, seq, B_HEADS, B_DK))
    k = rotary(proj[..., dq:2 * dq].reshape(bsz, seq, B_HEADS, B_DK)) * (B_DK ** -0.5)
    v = proj[..., 2 * dq:2 * dq + dv].reshape(bsz, seq, B_HEADS, B_DV).astype(jnp.float32)
    g = proj[..., 2 * dq + dv:]

    log_gamma = jnp.log1p(-(2.0 ** (-5.0 - jnp.arange(B_HEADS, dtype=jnp.float32))))
    pos = jnp.arange(CHUNK, dtype=jnp.float32)
    diff = pos[:, None] - pos[None, :]
    decay_intra = jnp.where(diff[None] >= 0,
                            jnp.exp(jnp.maximum(diff, 0.0)[None] * log_gamma[:, None, None]), 0.0)
    xi = jnp.exp((pos + 1.0)[:, None] * log_gamma[None, :])
    zeta = jnp.exp((CHUNK - 1.0 - pos)[:, None] * log_gamma[None, :])
    gamma_c = jnp.exp(CHUNK * log_gamma)

    qc = q.reshape(bsz, nc, CHUNK, B_HEADS, B_DK)
    kc = k.reshape(bsz, nc, CHUNK, B_HEADS, B_DK)
    vc = v.reshape(bsz, nc, CHUNK, B_HEADS, B_DV)
    s = jnp.einsum('bnqhd,bnkhd->bnhqk', qc, kc) * decay_intra[None, None]
    intra = jnp.einsum('bnhqk,bnkhe->bnqhe', s, vc)

    def step(state, inp):
        qn, kn, vn = inp
        cross = jnp.einsum('bqhd,bhde->bqhe', qn, state) * xi[None, :, :, None]
        state = state * gamma_c[None, :, None, None] + jnp.einsum(
            'bkhd,bkhe->bhde', kn * zeta[None, :, :, None], vn)
        return state, cross

    state0 = jnp.zeros((bsz, B_HEADS, B_DK, B_DV), jnp.float32)
    _, cross = lax.scan(step, state0, (qc.swapaxes(0, 1), kc.swapaxes(0, 1), vc.swapaxes(0, 1)))
    ret = (intra + cross.swapaxes(0, 1)).reshape(bsz, seq, B_HEADS, B_DV)
    ret = rms_norm_2(ret, out_g.reshape(B_HEADS, B_DV)).reshape(bsz, seq, dv)
    y = ret * jax.nn.silu(g.astype(jnp.float32))
    return y.astype(h.dtype) @ w_out

def conv_ffn(h, w_up, conv_w, conv_b, w_down):
    seq = h.shape[1]
    u = h @ w_up
    up = jnp.pad(u, ((0, 0), (CONV_W - 1, 0), (0, 0)))
    u = sum(up[:, j:j + seq] * conv_w[j] for j in range(CONV_W)) + conv_b
    a, b = u[..., :D_FF_2], u[..., D_FF_2:]
    return (jax.nn.silu(a) * b) @ w_down

def second_inputs(seed: int = 0) -> dict:
    key = jax.random.key(seed)
    ks = jax.random.split(key, 16)

    def nrm(k, shape, scale):
        return jax.random.normal(k, shape, jnp.float32) * scale

    return {
        'x': nrm(ks[0], (BATCH, SEQ, D_MODEL), 1.0),
        'norm_mix_g': 1.0 + nrm(ks[1], (DEPTH, D_MODEL), 0.02),
        'norm_ffn_g': 1.0 + nrm(ks[2], (DEPTH, D_MODEL), 0.02),
        'a_w_in': nrm(ks[3], (N_A, D_MODEL, A_IN_COLS), D_MODEL ** -0.5),
        'a_q_g': 1.0 + nrm(ks[4], (N_A, A_LAT), 0.02),
        'a_k_g': 1.0 + nrm(ks[5], (N_A, A_LAT), 0.02),
        'a_iq_g': 1.0 + nrm(ks[6], (N_A, IDX_DIM), 0.02),
        'a_ik_g': 1.0 + nrm(ks[7], (N_A, IDX_DIM), 0.02),
        'a_w_out': nrm(ks[8], (N_A, A_Q_COLS, D_MODEL), A_Q_COLS ** -0.5),
        'b_w_in': nrm(ks[9], (N_B, D_MODEL, B_IN_COLS), D_MODEL ** -0.5),
        'b_out_g': 1.0 + nrm(ks[10], (N_B, B_HEADS * B_DV), 0.02),
        'b_w_out': nrm(ks[11], (N_B, B_HEADS * B_DV, D_MODEL), (B_HEADS * B_DV) ** -0.5),
        'f_w_up': nrm(ks[12], (DEPTH, D_MODEL, 2 * D_FF_2), D_MODEL ** -0.5),
        'f_conv_w': nrm(ks[13], (DEPTH, CONV_W, 2 * D_FF_2), CONV_W ** -0.5),
        'f_conv_b': nrm(ks[14], (DEPTH, 2 * D_FF_2), 0.01),
        'f_w_down': nrm(ks[15], (DEPTH, D_FF_2, D_MODEL), D_FF_2 ** -0.5),
    }

def second_block(x, norm_mix_g, norm_ffn_g, a_w_in, a_q_g, a_k_g, a_iq_g, a_ik_g, a_w_out,
              b_w_in, b_out_g, b_w_out, f_w_up, f_conv_w, f_conv_b, f_w_down):
    for i in range(DEPTH):
        h = rms_norm_2(x, norm_mix_g[i])
        j = i // N_MIXERS
        if i % N_MIXERS == 0:
            x = x + dsa_mixer(h, a_w_in[j], a_q_g[j], a_k_g[j], a_iq_g[j], a_ik_g[j], a_w_out[j])
        else:
            x = x + retention_mixer(h, b_w_in[j], b_out_g[j], b_w_out[j])
        x = x + conv_ffn(rms_norm_2(x, norm_ffn_g[i]), f_w_up[i], f_conv_w[i], f_conv_b[i], f_w_down[i])
    return x


def setup_inputs(seed=0):
    out = dict(first_inputs(seed))
    for name, value in second_inputs(seed + 1).items():
        if name != "x":
            out[name + "_2"] = value
    return out


def reference(
    x, positions, norm_gains, mla_w_in, mla_q_norm, mla_kv_norm, mla_w_uq, mla_w_ukv, mla_w_o,
    hgrn_w_in, hgrn_lb_logits, hgrn_o_norm, hgrn_w_o, mlp_w1, mlp_w2, norm_mix_g_2,
    norm_ffn_g_2, a_w_in_2, a_q_g_2, a_k_g_2, a_iq_g_2, a_ik_g_2, a_w_out_2, b_w_in_2,
    b_out_g_2, b_w_out_2, f_w_up_2, f_conv_w_2, f_conv_b_2, f_w_down_2,
):
    x = first_block(
        x, positions, norm_gains, mla_w_in, mla_q_norm, mla_kv_norm, mla_w_uq, mla_w_ukv,
        mla_w_o, hgrn_w_in, hgrn_lb_logits, hgrn_o_norm, hgrn_w_o, mlp_w1, mlp_w2,
    )
    return second_block(
        x, norm_mix_g_2, norm_ffn_g_2, a_w_in_2, a_q_g_2, a_k_g_2, a_iq_g_2, a_ik_g_2,
        a_w_out_2, b_w_in_2, b_out_g_2, b_w_out_2, f_w_up_2, f_conv_w_2, f_conv_b_2, f_w_down_2,
    )


_drawn_inputs = setup_inputs


def setup_inputs(seed=0):
    import zlib

    import numpy as np

    out = dict(_drawn_inputs(seed))
    spreads = {}
    factors = {'hgrn_lb_logits': 7.977,
     'norm_mix_g_2': 3.666,
     'norm_ffn_g_2': 5.184,
     'a_q_g_2': 8.0,
     'a_k_g_2': 8.0,
     'a_iq_g_2': 8.0,
     'a_ik_g_2': 8.0,
     'b_out_g_2': 8.0,
     'f_conv_b_2': 8.0}
    for name, (base, spread) in spreads.items():
        noise = np.random.default_rng([zlib.crc32(name.encode()), seed]).standard_normal(out[name].shape)
        drawn = base * np.exp(spread * noise) if base else spread * noise
        out[name] = __import__('jax').numpy.asarray(drawn.astype(out[name].dtype))
    for name, factor in factors.items():
        out[name] = (out[name] * factor).astype(out[name].dtype)
    return out
```

```python
from contextlib import ExitStack

import numpy as np
import concourse.bass as bass
from concourse import mybir

F32 = mybir.dt.float32
F32R = mybir.dt.float32r
I32 = mybir.dt.int32
ALU = mybir.AluOpType
ACT = mybir.ActivationFunctionType

P = 128
T = 512
TB = T // P
D = 1024
DC = D // P
RING = 4
SLAB = 2048
EPS = 1e-6
NEG = -1e30
GONE = -3e38

MLA_HEADS, MLA_Q, MLA_KV, MLA_NOPE, MLA_ROPE, MLA_V = 8, 512, 256, 128, 64, 128
MLA_SCALE = (MLA_NOPE + MLA_ROPE) ** -0.5
FF = 4096
HG_HEADS, HG_CHUNK = 8, 32
HG_N = T // HG_CHUNK
HG_G = P // HG_CHUNK
DSA_HEADS, DSA_LAT, IDX_HEADS, IDX_DIM = 8, 128, 8, 64
DSA_CHUNK, TOPK = 64, 128
DSA_SCALE = DSA_LAT ** -0.5
IDX_SCALE = IDX_HEADS ** -0.5 * IDX_DIM ** -0.5
RET_HEADS, RET_DK, RET_DV = 4, 256, 512
FF2 = 2816
FF2C = FF2 // P
CONV_W = 3
ROPE_BASE = 10000.0

TWO_PI = [6.28125, 0.00193500518798828125, 3.0199159819e-7]
ROUND = 1.5 * 2.0 ** 23


def shape_tables():
    f32 = np.float32
    p = np.arange(P)[:, None]
    t = np.arange(T)[None, :]
    tabs = {}
    tabs["ident"] = np.eye(P, dtype=f32)
    tabs["ones"] = np.ones((P, P), f32)
    tabs["ones_half"] = (p // 64 == np.arange(P)[None, :] // 64).astype(f32)
    u = t - (T - P)
    tabs["causal"] = np.where(u <= p, 0.0, NEG).astype(f32)
    tabs["admissible"] = np.where(u < (p // DSA_CHUNK + 1) * DSA_CHUNK, 0.0, NEG).astype(f32)
    tabs["scan_keep"] = np.broadcast_to((t % HG_CHUNK != 0), (P, T)).astype(f32)
    inv = np.power(f32(ROPE_BASE), -np.arange(0, MLA_ROPE, 2, dtype=f32) / f32(MLA_ROPE)).astype(f32)
    half = (np.arange(P) % MLA_ROPE) // (MLA_ROPE // 2)
    tabs["small"] = np.stack([inv[np.arange(P) % (MLA_ROPE // 2)], np.where(half == 0, -1.0, 1.0),
                              np.full(P, EPS), np.zeros(P)], 1).astype(f32)
    inv2 = (f32(1.0) / np.power(f32(ROPE_BASE), np.arange(0, RET_DK, 2, dtype=f32) / f32(RET_DK))).astype(f32)
    ang = (np.arange(T, dtype=f32)[None, :] * inv2[:, None]).astype(f32)
    tabs["ret_cos"] = np.cos(ang.astype(np.float64)).astype(f32)
    tabs["ret_sin"] = np.sin(ang.astype(np.float64)).astype(f32)
    dec = []
    for h in range(RET_HEADS):
        lg = np.log1p(-(2.0 ** (-5.0 - h)))
        dec.append(np.where(t >= p, np.exp(np.maximum(t - p, 0) * lg) * RET_DK ** -0.5, 0.0))
    tabs["ret_decay"] = np.concatenate(dec, 1).astype(f32)
    a, b = np.arange(P)[:, None], np.arange(P)[None, :]
    hg = ((a // HG_CHUNK == b // HG_CHUNK) & (a <= b)).astype(np.int32)
    return tabs, hg


TABLE_WIDTH = {"ident": P, "ones": P, "ones_half": P, "causal": T, "admissible": T, "scan_keep": T, "small": 4,
               "ret_cos": T, "ret_sin": T, "ret_decay": RET_HEADS * T}


class Signal:

    def __init__(self, sem, per=1, credit=0):
        self.sem, self.per, self.credit = sem, per, credit

    def at(self, j, i=0):
        return self.sem, i * self.per + (j + 1 + self.credit)


class Slab:

    def __init__(self, kc, units, parts):
        self.kc, self.units, self.parts = kc, units, parts
        self.loads = len(parts(0))


class Stage:

    def __init__(self, before, turns, slabs):
        self.turns, self.slabs = turns, slabs
        self.per = sum(s.units for s in slabs)
        assert turns == 1 or (self.per % RING == 0 and len(slabs) % 2 == 0)
        self.base = before.end if before else 0
        self.end = self.base + turns * self.per
        self.slab_base = before.slab_end if before else 0
        self.slab_end = self.slab_base + turns * len(slabs)
        self.loads_base = before.loads_end if before else [0, 0]
        self.loads_per = [0, 0]
        self.first, at = [], 0
        self.loaded_at = []
        for q, s in enumerate(slabs):
            self.first.append(at)
            at += s.units
            self.loads_per[self.slot(q)] += s.loads
            self.loaded_at.append(self.loads_per[self.slot(q)])
        self.loads_end = [b + turns * n for b, n in zip(self.loads_base, self.loads_per)]
        self.before_last = before.slabs[-1].units if before else 0

    def slot(self, q):
        return (self.slab_base + q) % 2

    def bank(self, j):
        return (self.base + j) % RING

    def done(self, j, i=0):
        return i * self.per + (self.base + j + 1)

    def uses(self, j, i=0):
        return i * (self.per // RING) + (self.base + j) // RING

    def loaded(self, q, i=0):
        s = self.slot(q)
        return i * (16 * self.loads_per[s]) + 16 * (self.loads_base[s] + self.loaded_at[q])

    def raw_free(self, q, i=0):
        if q >= 2:
            return i * self.per + self.base + self.first[q - 1]
        if q == 1:
            return i * self.per + self.base
        last = min(self.before_last, self.slabs[-1].units) if self.turns > 1 else self.before_last
        return i * self.per + self.base - last


def turns(eng, n, body):
    if n == 1:
        body(0)
    else:
        with eng.Fori(0, n) as i:
            body(i)


def program(nc, x, positions, norm_gains, mla_w_in, mla_q_norm, mla_kv_norm, mla_w_uq, mla_w_ukv, mla_w_o, hgrn_w_in,
            hgrn_lb_logits, hgrn_o_norm, hgrn_w_o, mlp_w1, mlp_w2, norm_mix_g_2, norm_ffn_g_2, a_w_in_2, a_q_g_2,
            a_k_g_2, a_iq_g_2, a_ik_g_2, a_w_out_2, b_w_in_2, b_out_g_2, b_w_out_2, f_w_up_2, f_conv_w_2, f_conv_b_2,
            f_w_down_2, tables, hg_mask_dram, out):
    with ExitStack() as ctx:
        def sb(name, width, dt=F32, parts=P):
            return ctx.enter_context(nc.sbuf_tensor(name, [parts, width], dt))

        def sem(name):
            return ctx.enter_context(nc.semaphore(name))

        def signal(name, per=1, credit=0):
            return Signal(sem(name), per, credit)

        def plain_wait(dve):
            dve.memset(carrier[:], 0.0)

        shared_sems = {}

        def shared(name, per=1, turns=1):
            s, used = shared_sems.get(name) or (sem(name), 0)
            shared_sems[name] = s, used + per * turns
            return Signal(s, per, used)

        def tile(t, c, width=T):
            return t[:, bass.ds(c * width, width)]

        raw = [sb(f"raw{r}", SLAB) for r in range(2)]
        w_hi = [sb(f"w_hi{r}", DC * P, F32R) for r in range(RING)]
        w_lo = [sb(f"w_lo{r}", DC * P, F32R) for r in range(RING)]
        hT = sb("hT", DC * T)
        a_hi, a_lo = sb("a_hi", DC * T, F32R), sb("a_lo", DC * T, F32R)
        g_hi, g_lo = sb("g_hi", DC * T, F32R), sb("g_lo", DC * T, F32R)
        acc = sb("acc", DC * T)
        F = sb("F", 20 * T)
        cols = sb("cols", 128 + 16 + 4 * 88)
        tab = {k: sb(k, w) for k, w in TABLE_WIDTH.items() if not k.startswith("ret_")}
        ret_cos, ret_sin, ret_decay = sb("ret_cos", T), sb("ret_sin", T), sb("ret_decay", RET_HEADS * T)
        hg_mask = sb("hg_mask", P, I32)
        ident, ones, ones_half = tab["ident"], tab["ones"], tab["ones_half"]
        inv_freq, rope_sign, eps = (tab["small"][:, k:k + 1] for k in range(3))
        zero = tab["small"][:, 3:4]
        lb = sb("lb", 8 * DC)
        row_max, neg_max, row_sum, row_inv = (sb(n, 2) for n in ("row_max", "neg_max", "row_sum", "row_inv"))
        top8 = sb("top8", 8)
        carrier = sb("carrier", 1)
        wi_tok = sb("wi_tok", TB * IDX_HEADS)

        sq = [tile(F, 0), tile(F, 1)]
        log_ms, rstd = tile(F, 2), tile(F, 3)
        tmp = [tile(F, 4), tile(F, 5)]

        psum = [ctx.enter_context(nc.psum_tensor(f"proj{b}", [P, T], F32)) for b in range(RING)]
        aux = [ctx.enter_context(nc.psum_tensor(f"aux{b}", [P, T], F32)) for b in range(4)]

        def rows(ap, width=P):
            return ap.rearrange("(c p) -> c p", p=width)

        vec_rows = []
        where = {}
        at = 0

        def vec(name, n, src):
            nonlocal at
            where[name] = at
            vec_rows.append((at, n, 0, P, src))
            at += n

        vec("norm", 64, norm_gains.rearrange("l k (c p) -> (l k c) p", p=P))
        vec("mix", 16, norm_mix_g_2.rearrange("l (c p) -> (l c) p", p=P))
        vec("ffn", 16, norm_ffn_g_2.rearrange("l (c p) -> (l c) p", p=P))
        vec("ret_out", 16, b_out_g_2.rearrange("l (c p) -> (l c) p", p=P))
        vec("mla_q", 4, mla_q_norm.rearrange("l (c p) -> (l c) p", p=P))
        vec("mla_kv", 2, mla_kv_norm.rearrange("l (c p) -> (l c) p", p=P))
        vec("hg_o", 1, hgrn_o_norm)
        vec("dsa_q", 1, a_q_g_2)
        vec("dsa_k", 1, a_k_g_2)
        for name, src in (("dsa_iq", a_iq_g_2), ("dsa_ik", a_ik_g_2)):
            where[name] = at
            vec_rows.append((at, 1, 0, IDX_DIM, src))
            vec_rows.append((at, 1, IDX_DIM, IDX_DIM, src))
            at += 1
        VEC = at
        CONV0 = 144
        UC = 2 * FF2C
        row_tiles = [(tile(F, 6 + k, P), n, c0) for k, (n, c0) in
                     enumerate([(VEC, 0), (16, 128), (88, CONV0), (88, CONV0 + 88), (88, CONV0 + 176), (88, CONV0 + 264)])]
        row_loads = [(row_tiles[0][0][r:r + n, c:c + w], src) for r, n, c, w, src in vec_rows]
        row_loads.append((row_tiles[1][0][0:16, :], hgrn_lb_logits.rearrange("l (c p) -> (l c) p", p=P)))
        for l in range(2):
            w = f_conv_w_2[l].rearrange("k (c p) -> (k c) p", p=P)
            row_loads.append((row_tiles[2 + 2 * l][0][0:2 * UC, :], w[0:2 * UC, :]))
            row_loads.append((row_tiles[3 + 2 * l][0][0:UC, :], w[2 * UC:3 * UC, :]))
            row_loads.append((row_tiles[3 + 2 * l][0][UC:2 * UC, :], f_conv_b_2[l].rearrange("(c p) -> c p", p=P)))

        def gain(name, c, n=1):
            return cols[:, bass.ds(where[name] + c, n)]

        def conv_col(l, k, c):
            return cols[:, bass.ds(CONV0 + 176 * l + k * UC + c, 1)]

        def kpn(w):
            return w.rearrange("(k p) n -> p k n", p=P)

        def plain(w, k0=0, kc=DC, width=256, col=lambda i: 0):
            v = kpn(w)
            k = k0 if callable(k0) else (lambda i: k0)
            return Slab(kc, width // P, lambda i: [(0, width, v[:, bass.ds(k(i), kc), bass.ds(col(i), width)])])

        stages = []

        def stage(n, slabs):
            s = Stage(stages[-1] if stages else None, n, slabs)
            stages.append(s)
            return s

        w_in = kpn(mla_w_in[0])
        kr0 = MLA_Q + MLA_KV
        half = MLA_ROPE // 2
        st_mla_in = stage(1, [plain(mla_w_in[0], col=lambda i, c=c: c * 256) for c in range(3)] + [
            Slab(DC, 2, lambda i: [(64 * r, 64, w_in[:, :, kr0:kr0 + 64]) for r in range(2)]
                 + [(128 + 32 * r, 32, w_in[:, :, kr0 + 32 * (1 - r % 2):kr0 + 32 * (1 - r % 2) + 32]) for r in range(4)])])
        uq = kpn(mla_w_uq[0])
        QH = MLA_NOPE + MLA_ROPE

        def uq_parts(i):
            p = [(128 * h, 128, uq[:, :, bass.ds(i * (2 * QH) + h * QH, 128)]) for h in range(2)]
            p += [(256 + 64 * h, 64, uq[:, :, bass.ds(i * (2 * QH) + h * QH + MLA_NOPE, 64)]) for h in range(2)]
            p += [(384 + 64 * h + 32 * r, 32, uq[:, :, bass.ds(i * (2 * QH) + h * QH + MLA_NOPE + 32 * (1 - r), 32)])
                  for h in range(2) for r in range(2)]
            return p

        st_mla = stage(MLA_HEADS // 2, [Slab(MLA_Q // P, 4, uq_parts),
                                        plain(mla_w_ukv[0], kc=MLA_KV // P, width=512, col=lambda i: i * 512)])

        def square_out(w):
            return stage(1, [plain(w, col=lambda i, c=c: c * 256) for c in range(4)])

        st_mla_o = square_out(mla_w_o[0])

        def mlp_stage(l):
            return stage(FF // D, [plain(mlp_w1[l], col=lambda i, c=c: i * D + c * 256) for c in range(4)]
                         + [plain(mlp_w2[l], k0=lambda i: i * DC, col=lambda i, c=c: c * 256) for c in range(4)])

        st_mlp = [mlp_stage(0)]
        hg_w = kpn(hgrn_w_in[0])
        st_hg = stage(HG_HEADS, [Slab(DC, 2, lambda i, a=a: [(128 * r, 128, hg_w[:, :, bass.ds(i * P + (a + r) * D, P)])
                                                            for r in range(2)]) for a in (0, 2)])
        st_hg_o = square_out(hgrn_w_o[0])
        st_mlp.append(mlp_stage(1))

        dsa_w = kpn(a_w_in_2[0])
        o1 = DSA_HEADS * DSA_LAT
        o2 = o1 + DSA_LAT
        o3 = o2 + IDX_HEADS * IDX_DIM
        o4 = o3 + IDX_DIM
        st_dsa = stage(1, [plain(a_w_in_2[0], col=lambda i, c=c: o2 + 256 * c) for c in range(2)] + [
            Slab(DC, 2, lambda i: [(64 * r, 64, dsa_w[:, :, o3:o4]) for r in range(2)] + [(128, 128, dsa_w[:, :, o1:o2])]),
            Slab(DC, 1, lambda i: [(0, IDX_HEADS, dsa_w[:, :, o4:o4 + IDX_HEADS])])]
            + [plain(a_w_in_2[0], col=lambda i, c=c: 256 * c) for c in range(4)])
        st_dsa_o = square_out(a_w_out_2[0])

        def ffn_stages(l):
            up = kpn(f_w_up_2[l])

            def blocks(n, first, size):
                pairs = [Slab(DC, 2, lambda i, j=j: [(0, P, up[:, :, bass.ds(i * D + (first + j) * P, P)]),
                                                     (P, P, up[:, :, bass.ds(i * D + FF2 + (first + j) * P, P)])])
                         for j in range(size)]
                return stage(n, pairs + [plain(f_w_down_2[l], k0=lambda i: i * DC + first, kc=size,
                                               col=lambda i, c=c: c * 256) for c in range(4)])
            full = FF2C // DC
            return [(blocks(full, 0, DC), 0, DC), (blocks(1, full * DC, FF2C - full * DC), full * DC, FF2C - full * DC)]

        st_ffn = [ffn_stages(0)]
        dq, dv = RET_HEADS * RET_DK, RET_HEADS * RET_DV
        st_ret = stage(RET_HEADS, [plain(b_w_in_2[0], col=lambda i: i * RET_DK),
                                   plain(b_w_in_2[0], col=lambda i: i * RET_DK + dq)]
                       + [plain(b_w_in_2[0], col=lambda i, c=c: i * RET_DV + 2 * dq + 256 * c) for c in range(2)]
                       + [plain(b_w_in_2[0], col=lambda i, c=c: i * RET_DV + 2 * dq + dv + 256 * c) for c in range(2)]
                       + [plain(b_w_out_2[0], k0=lambda i: i * (RET_DV // P), kc=RET_DV // P, width=512,
                                col=lambda i, c=c: 512 * c) for c in range(2)])
        st_ffn.append(ffn_stages(1))

        loaded = [sem("loaded0"), sem("loaded1")]
        hi_split, lo_split = sem("hi_split"), sem("lo_split")
        unit_done = sem("unit_done")
        bank_free = [sem(f"bank_free{b}") for b in range(RING)]

        def raw_view(slot, s):
            return raw[slot][:, 0:s.kc * s.units * P].rearrange("p (k n) -> p k n", k=s.kc)

        tables_in, rows_in, x_in, pos_in = sem("tables_in"), sem("rows_in"), sem("x_in"), sem("pos_in")
        stored = sem("stored")
        turned = signal("turned")
        turned_out = signal("turned_out")
        x_turned, h_ready = signal("x_turned"), signal("h_ready")
        sq_ready, sq_used = signal("sq_ready"), signal("sq_used")
        log_ready, rstd_ready = signal("log_ready"), signal("rstd_ready")
        setup = signal("setup")
        lb_exp = signal("lb_exp")
        setup_lb_diff = (sem("lb_diff"), 1)

        class Norm:
            squares = groups_done = 0

            def __init__(self, chunks, turns=1, groups=1, matrix=ones, size=None, bank=aux[0]):
                self.chunks, self.per, self.gper = chunks, chunks * groups, groups
                self.matrix, self.bank, self.size = matrix, bank, size or chunks * P
                self.base, self.gbase = Norm.squares, Norm.groups_done
                Norm.squares += turns * self.per
                Norm.groups_done += turns * groups

            def square(self, act, src, c, g=0, i=0):
                m = self.base + g * self.chunks + c
                before = m - 1 if c >= 2 else m - c
                if before > 0:
                    act.wait_ge(sq_used.sem, i * self.per + before)
                act.activation(sq[c % 2], src, ACT.Square).then_inc(sq_ready.sem, 1)

            def sum(self, pe, c, g=0, i=0):
                m = self.base + g * self.chunks + c
                if c == 0 and self.gbase + g > 0:
                    pe.wait_ge(log_ready.sem, i * self.gper + self.gbase + g)
                pe.wait_ge(sq_ready.sem, i * self.per + m + 1)
                pe.matmul(self.bank[:], self.matrix[:], sq[c % 2], start=c == 0,
                          stop=c == self.chunks - 1).then_inc(sq_used.sem, 1)

            def root(self, act, g=0, i=0, users=None):
                n = self.gbase + g
                if n > 0:
                    act.wait_ge(rstd_ready.sem, i * self.gper + n)
                act.wait_ge(sq_used.sem, i * self.per + self.base + (g + 1) * self.chunks)
                act.activation(log_ms, self.bank[:], ACT.Ln, bias=eps, scale=1.0 / self.size).then_inc(log_ready.sem, 1)
                act.wait_ge(log_ready.sem, i * self.gper + n + 1)
                if users is not None:
                    act.wait_ge(*users)
                act.activation(rstd, log_ms, ACT.Exp, scale=-0.5).then_inc(rstd_ready.sem, 1)

            def ready(self, g=0, i=0):
                return rstd_ready.sem, i * self.gper + self.gbase + g + 1

        class Split:

            def __init__(self, per, turns=1):
                self.whole, self.high, self.low = (shared(f"split_{k}", per, turns) for k in ("whole", "hi", "lo"))

            def free(self, dve, c, i=0):
                sem, value = self.low.at(c - 2 if c >= 2 else -1, i)
                if not isinstance(value, int) or value > 0:
                    dve.wait_ge(sem, value)

            def round(self, act, dst, c, i=0):
                act.wait_ge(*self.whole.at(c, i))
                act.copy(dst, tmp[c % 2]).then_inc(self.high.sem, 1)

            def rest(self, dve, dst, hi, c, i=0):
                dve.wait_ge(*self.high.at(c, i))
                dve.tensor_tensor(dst, tmp[c % 2], hi.bitcast(F32), ALU.subtract).then_inc(self.low.sem, 1)

        def unit(pe, st, j, kc, hi, lo, i=0, k0=0, ready=None):
            pe.wait_ge(lo_split, st.done(j, i))
            if st.base + j >= RING:
                pe.wait_ge(bank_free[st.bank(j)], st.uses(j, i))
            r = st.bank(j)
            for k in range(kc):
                if ready:
                    pe.wait_ge(*ready(k))
                w = slice(k * P, k * P + P)
                xh, xl = tile(hi, k0 + k), tile(lo, k0 + k)
                pe.matmul(psum[r][:], w_hi[r][:, w], xh, start=k == 0, stop=False)
                pe.matmul(psum[r][:], w_hi[r][:, w], xl, start=False, stop=False)
                last = pe.matmul(psum[r][:], w_lo[r][:, w], xh, start=False, stop=k == kc - 1)
            last.then_inc(unit_done, 1)

        def arrived(eng, st, j, i=0):
            eng.wait_ge(unit_done, st.done(j, i))
            return psum[st.bank(j)]

        def taken(st, j):
            return bank_free[st.bank(j)], 1

        def emptied(eng, st, j, i=0):
            eng.wait_ge(bank_free[st.bank(j)], st.uses(j, i) + 1)

        class PreNorm:

            def __init__(self, gain_name, gain_at):
                self.norm = Norm(DC)
                self.split = Split(DC)
                self.gain = (gain_name, gain_at)

            def act(self, act, h_at):
                for c in range(DC):
                    act.wait_ge(*h_at(c))
                    self.norm.square(act, tile(hT, c), c)
                self.norm.root(act)
                for c in range(DC):
                    self.split.round(act, tile(a_hi, c), c)

            def pe(self, pe):
                for c in range(DC):
                    self.norm.sum(pe, c)

            def dve(self, dve):
                dve.wait_ge(*self.norm.ready())
                for c in range(DC + 1):
                    if c < DC:
                        self.split.free(dve, c)
                        dve.scalar_tensor_tensor(tmp[c % 2], tile(hT, c), gain(self.gain[0], self.gain[1] + c), rstd,
                                                 ALU.mult, ALU.mult).then_inc(self.split.whole.sem, 1)
                    if c >= 1:
                        self.split.rest(dve, tile(a_lo, c - 1), tile(a_hi, c - 1), c - 1)

            def ready(self, k):
                return self.split.low.at(k)

        class PostNorm:

            def __init__(self, gain_at):
                self.norm = Norm(DC)
                self.scaled, self.added = shared("post_scaled", DC), shared("post_added", DC)
                self.gain_at = gain_at

            def pe(self, pe):
                for c in range(DC):
                    self.norm.sum(pe, c)

            def dve(self, dve):
                dve.wait_ge(*self.norm.ready())
                for c in range(DC + 1):
                    if c < DC:
                        if c >= 2:
                            dve.wait_ge(*self.added.at(c - 2))
                        dve.scalar_tensor_tensor(tmp[c % 2], tile(acc, c), gain("norm", self.gain_at + c), rstd,
                                                 ALU.mult, ALU.mult).then_inc(self.scaled.sem, 1)
                    if c >= 1:
                        dve.wait_ge(*self.scaled.at(c - 1))
                        dve.tensor_tensor(tile(hT, c - 1), tile(hT, c - 1), tmp[(c - 1) % 2],
                                          ALU.add).then_inc(self.added.sem, 1)

        class Attention:

            def __init__(self, heads, turns, scale, sm, pr, pt):
                self.heads, self.scale, self.sm, self.pr, self.pt = heads, scale, sm, pr, pt
                n = heads * TB
                self.n = n
                s = lambda k: shared(f"attn_{k}", n, turns)
                self.scores, self.masked, self.negated, self.exped, self.inverted, self.normed, self.turned, \
                    self.turned_out = (s(k) for k in ("scores", "masked", "negated", "exped", "inverted", "normed",
                                                      "turned", "turned_out"))
                self.out = shared("attn_out", heads, turns)
                self.out_hi = shared("attn_out_hi", heads, turns)
                self.out_lo = shared("attn_out_lo", heads, turns)
                self.out_lo.credit += 1

            def keys(self, t):
                return (t % TB + 1) * P

            def pe(self, pe, i, score, values):
                for t in range(-1, self.n):
                    if t + 1 < self.n:
                        score(t + 1, aux[(t + 1) % 2], self.keys(t + 1)).then_inc(self.scores.sem, 1)
                    if t < 0:
                        continue
                    b = t % TB
                    pe.wait_ge(*self.normed.at(t, i))
                    for kb in range(b + 1):
                        last = pe.transpose(aux[2][:, kb * P:kb * P + P], self.pr[t % 2][:, kb * P:kb * P + P], ident[:])
                    last.then_inc(self.turned.sem, 1)
                    if b == 0:
                        pe.wait_ge(*self.out_lo.at(t // TB - 1, i))
                    pe.wait_ge(*self.turned_out.at(t, i))
                    for kb in range(b + 1):
                        last = pe.matmul(aux[3][:, b * P:b * P + P], values(t // TB, kb),
                                         self.pt[t % 2][:, kb * P:kb * P + P], start=kb == 0, stop=kb == b)
                    if b == TB - 1:
                        last.then_inc(self.out.sem, 1)

            def dve(self, dve, i, bias, out_lo, out_hi):
                for t in range(-1, self.n):
                    if t + 1 < self.n:
                        s, w = t + 1, self.keys(t + 1)
                        dve.wait_ge(*self.scores.at(s, i))
                        plain_wait(dve)
                        dve.tensor_tensor_reduce(self.sm[s % 2][:, 0:w], aux[s % 2][:, 0:w], bias(s), self.scale, GONE,
                                                 ALU.add, ALU.max, row_max[:, s % 2:s % 2 + 1]).then_inc(self.masked.sem, 1)
                        dve.wait_ge(*self.masked.at(s, i))
                        dve.tensor_scalar(neg_max[:, s % 2:s % 2 + 1], row_max[:, s % 2:s % 2 + 1], -1.0, None,
                                          ALU.mult).then_inc(self.negated.sem, 1)
                    if t < 0:
                        continue
                    w, r = self.keys(t), slice(t % 2, t % 2 + 1)
                    dve.wait_ge(*self.exped.at(t, i))
                    dve.reciprocal(row_inv[:, r], row_sum[:, r]).then_inc(self.inverted.sem, 1)
                    dve.wait_ge(*self.inverted.at(t, i))
                    dve.tensor_scalar(self.pr[t % 2][:, 0:w], self.pr[t % 2][:, 0:w], row_inv[:, r], None,
                                      ALU.mult).then_inc(self.normed.sem, 1)
                    if t % TB == TB - 1:
                        hh = t // TB
                        dve.wait_ge(*self.out_hi.at(hh, i))
                        dve.tensor_tensor(out_lo(hh), aux[3][:], out_hi(hh).bitcast(F32),
                                          ALU.subtract).then_inc(self.out_lo.sem, 1)

            def act(self, act, i, out_hi):
                for t in range(-1, self.n):
                    if t + 1 < self.n:
                        s, w, r = t + 1, self.keys(t + 1), slice((t + 1) % 2, (t + 1) % 2 + 1)
                        act.wait_ge(*self.negated.at(s, i))
                        act.activation(self.pr[s % 2][:, 0:w], self.sm[s % 2][:, 0:w], ACT.Exp, bias=neg_max[:, r],
                                       accum_out=row_sum[:, r]).then_inc(self.exped.sem, 1)
                    if t < 0:
                        continue
                    w = self.keys(t)
                    act.wait_ge(*self.turned.at(t, i))
                    act.copy(self.pt[t % 2][:, 0:w], aux[2][:, 0:w]).then_inc(self.turned_out.sem, 1)
                    if t % TB == TB - 1:
                        hh = t // TB
                        act.wait_ge(*self.out.at(hh, i))
                        act.copy(out_hi(hh), aux[3][:]).then_inc(self.out_hi.sem, 1)

        def causal(table, b):
            return tab[table][:, (TB - 1 - b) * P:T]


        def turn_block(pe, bank, src):
            for b in range(TB):
                last = pe.transpose(bank[:, b * P:b * P + P], src[:, b * P:b * P + P], ident[:])
            return last

        pre_mla = PreNorm("norm", 0)
        mla_c = [tile(F, 6 + c) for c in range(6)]
        k_rope, rope_cos, rope_sin = tile(F, 12), tile(F, 13), tile(F, 14)
        pos_i, pos_f, angle, cycles, reduced = (tile(F, 15 + k) for k in range(5))
        n_cq, n_ckv = Norm(MLA_Q // P), Norm(MLA_KV // P)
        s_c = Split(6)
        angle_ready, sin_ready = signal("angle_ready"), signal("sin_ready")
        rope_part, k_rope_ready = signal("rope_part"), signal("k_rope_ready")
        qn, q_rope, kn = [tile(F, 6), tile(F, 7)], tile(F, 8), [tile(F, 9), tile(F, 10)]
        vT, vtok = tile(F, 11), [tile(acc, 2), tile(acc, 3)]
        q_rope_ready = signal("q_rope_ready")
        v_turned, v_ready = signal("v_turned", 2), signal("v_ready", 2)
        at_mla = Attention(2, MLA_HEADS // 2, MLA_SCALE, [tile(F, 15), tile(F, 16)], [tile(F, 17), tile(F, 18)],
                           [tile(acc, 0), tile(acc, 1)])
        post_mla = PostNorm(8)

        class Mlp:

            def __init__(self, l):
                self.l, self.st = l, st_mlp[l]
                self.pre = PreNorm("norm", 32 * l + 16)
                self.split = Split(DC, self.st.turns)
                self.cleared = shared("mlp_cleared")
                self.post = PostNorm(32 * l + 24)
                self.relu = [tile(F, 6), tile(F, 7)]

            def pe(self, pe):
                self.pre.pe(pe)

                def block(i):
                    for j in range(DC):
                        unit(pe, self.st, j, DC, a_hi, a_lo, i, ready=self.pre.ready if j == 0 else None)
                    for m in range(DC):
                        unit(pe, self.st, DC + m, DC, g_hi, g_lo, i,
                             ready=(lambda k: self.split.low.at(k, i)) if m == 0 else None)
                turns(pe, self.st.turns, block)
                self.post.pe(pe)

            def act(self, act, h_at):
                self.pre.act(act, h_at)

                def block(i):
                    for j in range(DC + 1):
                        if j < DC:
                            bank = arrived(act, self.st, j, i)
                            act.activation(self.relu[j % 2], bank[:], ACT.Relu).then_inc(*taken(self.st, j))
                        if j >= 1:
                            self.split.round(act, tile(g_hi, j - 1), j - 1, i)
                turns(act, self.st.turns, block)
                for c in range(DC):
                    emptied(act, self.st, DC + c, self.st.turns - 1)
                    self.post.norm.square(act, tile(acc, c), c)
                self.post.norm.root(act)

            def dve(self, dve):
                self.pre.dve(dve)
                dve.memset(acc[:], 0.0).then_inc(self.cleared.sem, 1)
                dve.wait_ge(*self.cleared.at(0))

                def block(i):
                    for j in range(DC + 1):
                        if j < DC:
                            emptied(dve, self.st, j, i)
                            self.split.free(dve, j, i)
                            dve.tensor_tensor(tmp[j % 2], self.relu[j % 2], self.relu[j % 2],
                                              ALU.mult).then_inc(self.split.whole.sem, 1)
                        if j >= 1:
                            self.split.rest(dve, tile(g_lo, j - 1), tile(g_hi, j - 1), j - 1, i)
                    for m in range(DC):
                        bank = arrived(dve, self.st, DC + m, i)
                        dve.tensor_tensor(tile(acc, m), bank[:], tile(acc, m), ALU.add).then_inc(*taken(self.st, DC + m))
                turns(dve, self.st.turns, block)
                self.post.dve(dve)

        class OutProj:

            def __init__(self, st, hi, lo, post):
                self.st, self.hi, self.lo, self.post = st, hi, lo, post

            def pe(self, pe, ready):
                for m in range(DC + 1):
                    if m < DC:
                        unit(pe, self.st, m, DC, self.hi, self.lo, ready=ready if m == 0 else None)
                    if m >= 1:
                        self.post.norm.sum(pe, m - 1)

            def act(self, act):
                for m in range(DC):
                    bank = arrived(act, self.st, m)
                    self.post.norm.square(act, bank[:], m)
                    act.copy(tile(acc, m), bank[:]).then_inc(*taken(self.st, m))
                self.post.norm.root(act)

            def dve(self, dve):
                emptied(dve, self.st, DC - 1)
                self.post.dve(dve)

        out_mla = OutProj(st_mla_o, a_hi, a_lo, post_mla)
        mlp = [Mlp(0)]

        pre_hg = PreNorm("norm", 32)
        hg_sig, hg_q, hg_k, hg_f, hg_b, hg_logf = (tile(F, k) for k in (7, 9, 10, 11, 12, 13))
        hg_d, hg_d2 = tile(F, 11), tile(F, 8)
        hg_vT = tile(F, 14)
        hg_e = [tile(F, 15 + k) for k in range(4)]
        hg_qdec = tile(F, 19)
        hg_qrel, hg_krel, hg_dec, hg_kdec = hg_e
        hg_state, hg_v, hg_kT, hg_a, hg_gate = tile(acc, 0, 4 * T), tile(acc, 4), tile(acc, 5), tile(acc, 6), tile(acc, 7)
        hg_f_ready, hg_k_ready, hg_logf_ready, hg_b_ready, hg_d_ready, hg_d2_ready = (
            signal(f"hg_{n}_ready") for n in ("f", "k", "logf", "b", "d", "d2"))
        hg_e_ready = signal("hg_e_ready", 4)
        hg_rel_ready, hg_dec_ready = signal("hg_rel_ready", 2), signal("hg_dec_ready", 2)
        hg_cleared = signal("hg_cleared")
        hg_scores, hg_masked = signal("hg_scores"), signal("hg_masked")
        hg_v_turned, hg_v_ready, hg_k_turned, hg_kT_ready = (
            signal(f"hg_{n}") for n in ("v_turned", "v_ready", "k_turned", "kT_ready"))
        hg_u, hg_state_ready = signal("hg_u"), signal("hg_state_ready", HG_N - 1)
        hg_o, hg_y = signal("hg_o"), signal("hg_y")
        n_hg = Norm(1, turns=HG_HEADS, bank=aux[1])
        s_hg = Split(1, HG_HEADS)
        post_hg = PostNorm(40)
        out_hg = OutProj(st_hg_o, g_hi, g_lo, post_hg)
        mlp.append(Mlp(1))

        pre_dsa = PreNorm("mix", 0)
        idx_q, idx_k = [tile(F, 6 + c) for c in range(4)], tile(F, 10)
        dsa_cT, dsa_kT, dsa_c = tile(F, 11), tile(F, 12), tile(F, 13)
        dsa_bias = [tile(F, 14 + b) for b in range(TB)]
        idx_rel = [tile(F, 18), tile(F, 19)]
        wiT = tile(F, 19)
        dsa_q = tile(F, 18)
        NG = 6
        n_idx = Norm(1, groups=5, matrix=ones_half, size=IDX_DIM)
        n_key = Norm(1)
        idx_ready, key_ready = signal("idx_ready"), signal("key_ready")
        c_turned, c_ready = signal("c_turned"), signal("c_ready")
        wi_turned, wi_ready, wiT_ready = signal("wi_turned"), signal("wi_ready"), signal("wiT_ready")
        rel_ready, rel_taken, scored = signal("rel_ready"), signal("rel_taken"), signal("scored")
        dsa_bias_ready = signal("dsa_bias_ready")
        n_dq = Norm(1, turns=DSA_HEADS, bank=psum[0])
        dsa_q_ready = signal("dsa_q_ready")
        at_dsa = Attention(1, DSA_HEADS, DSA_SCALE, [tile(F, 6), tile(F, 7)], [tile(F, 8), tile(F, 9)],
                           [tile(F, 10), tile(F, 11)])
        REL = [(b, h) for b in range(1, TB) for h in range(IDX_HEADS)]
        Q0 = 7
        Q_AFTER = [range(0, 3), range(3, 6), range(6, 8)]

        class Ffn:

            def __init__(self, l):
                self.l = l
                self.pre = PreNorm("ffn", DC * l)
                self.u = [[tile(F, 6 + 2 * s + r) for r in range(2)] for s in range(2)]
                self.parts = []
                for k, (st, first, size) in enumerate(st_ffn[l]):
                    self.parts.append((st, first, size, Split(size, st.turns), shared("ffn_tap2", 2 * size, st.turns),
                                       shared("ffn_tap1", 2 * size, st.turns), shared("ffn_silu", size, st.turns)))
                self.last = st_ffn[l][-1]

            def h_at(self, c):
                st, _, size = self.last
                return bank_free[st.bank(2 * size + c)], st.uses(2 * size + c) + 1

            def pe(self, pe):
                self.pre.pe(pe)
                for k, (st, first, size, split, *_) in enumerate(self.parts):
                    def block(i):
                        for j in range(2 * size):
                            unit(pe, st, j, DC, a_hi, a_lo, i, ready=self.pre.ready if k == 0 and j == 0 else None)
                        for m in range(DC):
                            unit(pe, st, 2 * size + m, size, g_hi, g_lo, i,
                                 ready=(lambda c: split.low.at(c, i)) if m == 0 else None)
                    turns(pe, st.turns, block)

            def act(self, act, h_at):
                self.pre.act(act, h_at)
                l = self.l
                for st, first, size, split, tap2, tap1, silu in self.parts:
                    def block(i):
                        for j in range(size + 2):
                            if j >= 2:
                                split.round(act, tile(g_hi, j - 2), j - 2, i)
                            if j < size:
                                for s in range(2):
                                    c = i * DC + first + j + s * FF2C
                                    bank = arrived(act, st, 2 * j + s, i)
                                    act.activation(self.u[s][j % 2], bank[:], ACT.Identity, bias=conv_col(l, 3, c),
                                                   scale=conv_col(l, 2, c)).then_inc(tap2.sem, 1)
                            if 1 <= j <= size:
                                emptied(act, st, 2 * (j - 1), i)
                                u = self.u[0][(j - 1) % 2]
                                act.activation(u, u, ACT.Silu).then_inc(silu.sem, 1)
                    turns(act, st.turns, block)

            def dve(self, dve):
                self.pre.dve(dve)
                l = self.l
                for st, first, size, split, tap2, tap1, silu in self.parts:
                    def block(i):
                        for j in range(size + 2):
                            if j < size:
                                for k in (1, 0):
                                    for s in range(2):
                                        c = i * DC + first + j + s * FF2C
                                        u, back = self.u[s][j % 2], 2 - k
                                        dve.wait_ge(*(tap2 if k else tap1).at(2 * j + s, i))
                                        ins = dve.scalar_tensor_tensor(
                                            u[:, back:T], psum[st.bank(2 * j + s)][:, 0:T - back], conv_col(l, k, c),
                                            u[:, back:T], ALU.mult, ALU.add)
                                        if k:
                                            ins.then_inc(tap1.sem, 1)
                                        else:
                                            ins.then_inc(*taken(st, 2 * j + s))
                            if 1 <= j <= size:
                                dve.wait_ge(*silu.at(j - 1, i))
                                emptied(dve, st, 2 * (j - 1) + 1, i)
                                split.free(dve, j - 1, i)
                                dve.tensor_tensor(tmp[(j - 1) % 2], self.u[0][(j - 1) % 2], self.u[1][(j - 1) % 2],
                                                  ALU.mult).then_inc(split.whole.sem, 1)
                            if j >= 2:
                                split.rest(dve, tile(g_lo, j - 2), tile(g_hi, j - 2), j - 2, i)
                        for m in range(DC):
                            bank = arrived(dve, st, 2 * size + m, i)
                            dve.tensor_tensor(tile(hT, m), bank[:], tile(hT, m),
                                              ALU.add).then_inc(*taken(st, 2 * size + m))
                    turns(dve, st.turns, block)

        ffn = [Ffn(0)]

        pre_ret = PreNorm("mix", DC)
        ret_q, ret_k = [tile(F, 6), tile(F, 7)], [tile(F, 8), tile(F, 9)]
        ret_v = tile(F, 10, T)
        ret_vtok = F[:, 10 * T:14 * T]
        ret_gate = [tile(F, 14 + m) for m in range(4)]
        ret_vT = [tile(F, 18), tile(F, 19)]
        ret_s = [tile(acc, j) for j in range(TB)]
        ret_raw = [tile(acc, 4 + m) for m in range(4)]
        RV = RET_DV // P
        ret_part, ret_qk_ready = signal("ret_part", 4), signal("ret_qk_ready", 4)
        ret_v_turned, ret_v_ready = signal("ret_v_turned", RV), signal("ret_v_ready", RV)
        ret_scores, ret_s_ready = signal("ret_scores", TB), signal("ret_s_ready", TB)
        ret_o, ret_raw_ready, ret_y = signal("ret_o", RV), signal("ret_raw_ready", RV), signal("ret_y", RV)
        n_ret = Norm(RV, turns=RET_HEADS, size=RET_DV)
        s_ret = Split(RV, RET_HEADS)
        ffn.append(Ffn(1))

        out_turned, out_ready = signal("out_turned"), signal("out_ready")

        block = ctx.enter_context(nc.Block())

        @block.sync
        def _(sp):
            for st in stages:
                def load(i):
                    for q, s in enumerate(st.slabs):
                        if st.slab_base + q >= 2:
                            sp.wait_ge(lo_split, st.raw_free(q, i))
                        v = raw_view(st.slot(q), s)
                        for c, n, src in s.parts(i):
                            sp.dma_start(v[:, :, c:c + n], src).then_inc(loaded[st.slot(q)], 16)
                turns(sp, st.turns, load)
            for b in range(TB):
                sp.wait_ge(*out_ready.at(2 * b + 1))
                sp.dma_start(out.rearrange("a t d -> (a t) d")[b * P:b * P + P, :], acc[:, b * D:b * D + D]).then_inc(stored, 16)
            sp.wait_ge(stored, 16 * TB)

        @block.gpsimd
        def _(pool):
            pool.wait_ge(tables_in, 16 * (len(TABLE_WIDTH) + 1))
            for st in stages:
                def split(i):
                    for q, s in enumerate(st.slabs):
                        pool.wait_ge(loaded[st.slot(q)], st.loaded(q, i))
                        v = raw_view(st.slot(q), s)
                        for m in range(s.units):
                            j = st.first[q] + m
                            r = st.bank(j)
                            if st.base + j >= RING:
                                pool.wait_ge(unit_done, st.done(j - RING, i))
                            src = v[:, :, m * P:m * P + P]
                            hi = w_hi[r][:, 0:s.kc * P].rearrange("p (k n) -> p k n", k=s.kc)
                            lo = w_lo[r][:, 0:s.kc * P].rearrange("p (k n) -> p k n", k=s.kc)
                            pool.tensor_tensor(hi, src, zero.rearrange("p (a b) -> p a b", a=1).to_broadcast([P, s.kc, P]),
                                               ALU.subtract).then_inc(hi_split, 1)
                            pool.wait_ge(hi_split, st.done(j, i))
                            pool.tensor_tensor(lo, src, hi.bitcast(F32), ALU.subtract).then_inc(lo_split, 1)
                turns(pool, st.turns, split)

        @block.scalar
        def _(act):
            act.dma_start(acc[:].rearrange("p (t d) -> p t d", t=TB),
                          x.rearrange("a (t p) d -> p (a t) d", p=P)).then_inc(x_in, 16)
            for k in TABLE_WIDTH:
                dst = {"ret_cos": ret_cos, "ret_sin": ret_sin, "ret_decay": ret_decay}.get(k) or tab[k]
                act.dma_start(dst[:], tables[k]).then_inc(tables_in, 16)
            act.dma_start(hg_mask[:], hg_mask_dram).then_inc(tables_in, 16)
            act.dma_start(pos_i.bitcast(I32), positions.partition_broadcast(P)).then_inc(pos_in, 16)
            for dst, src in row_loads:
                act.dma_start(dst, src).then_inc(rows_in, 16)
            act.wait_ge(tables_in, 16 * (len(TABLE_WIDTH) + 1))

            for k, dst in enumerate((rope_sin, rope_cos)):
                act.wait_ge(*angle_ready.at(k))
                act.activation(dst, reduced, ACT.Sin).then_inc(sin_ready.sem, 1)
            act.wait_ge(*setup_lb_diff)
            act.activation(lb[:, DC:3 * DC], lb[:, DC:3 * DC], ACT.Exp).then_inc(lb_exp.sem, 1)

            pre_mla.act(act, lambda c: h_ready.at(c))

            def take_c(j):
                bank = arrived(act, st_mla_in, j)
                n, c = (n_cq, j) if j < 4 else (n_ckv, j - 4)
                n.square(act, bank[:], c)
                act.copy(mla_c[j], bank[:]).then_inc(*taken(st_mla_in, j))
            for j in range(5):
                take_c(j)
            n_cq.root(act)
            take_c(5)
            for c in range(4):
                s_c.round(act, tile(g_hi, c), c)
            n_ckv.root(act)
            for c in range(4, 6):
                s_c.round(act, tile(g_hi, c), c)

            def mla_heads(i):
                for j, dst in ((0, qn[0]), (1, qn[1]), (4, kn[0]), (5, vT), (6, kn[1])):
                    bank = arrived(act, st_mla, j, i)
                    act.copy(dst, bank[:]).then_inc(*taken(st_mla, j))
                for hh in range(2):
                    act.wait_ge(*v_turned.at(hh, i))
                    act.copy(vtok[hh], aux[2][:]).then_inc(v_ready.sem, 1)
                    if hh == 0:
                        bank = arrived(act, st_mla, 7, i)
                        act.copy(vT, bank[:]).then_inc(*taken(st_mla, 7))
                at_mla.act(act, i, lambda hh: tile(a_hi, i * 2 + hh))
            turns(act, st_mla.turns, mla_heads)
            out_mla.act(act)
            mlp[0].act(act, post_mla.added.at)

            pre_hg.act(act, mlp[0].post.added.at)

            def hg_head(i):
                for j, dst, f in ((0, hg_q, ACT.Silu), (1, hg_sig, ACT.Sigmoid), (2, hg_vT, ACT.Copy), (3, hg_gate, ACT.Silu)):
                    bank = arrived(act, st_hg, j, i)
                    act.activation(dst, bank[:], f).then_inc(*taken(st_hg, j))
                act.wait_ge(*hg_f_ready.at(0, i))
                act.activation(hg_logf, hg_f, ACT.Ln).then_inc(hg_logf_ready.sem, 1)
                act.wait_ge(*hg_d_ready.at(0, i))
                act.activation(hg_e[0], hg_d, ACT.Exp).then_inc(hg_e_ready.sem, 1)
                act.activation(hg_e[1], hg_d, ACT.Exp, scale=-1.0).then_inc(hg_e_ready.sem, 1)
                act.activation(hg_e[2], hg_b, ACT.Exp).then_inc(hg_e_ready.sem, 1)
                act.wait_ge(*hg_d2_ready.at(0, i))
                act.activation(hg_e[3], hg_d2, ACT.Exp).then_inc(hg_e_ready.sem, 1)
                act.wait_ge(*hg_v_turned.at(0, i))
                act.copy(hg_v, aux[1][:]).then_inc(hg_v_ready.sem, 1)
                act.wait_ge(*hg_k_turned.at(0, i))
                act.copy(hg_kT, aux[1][:]).then_inc(hg_kT_ready.sem, 1)
                act.wait_ge(*hg_o.at(0, i))
                n_hg.square(act, aux[0][:], 0, 0, i)
                n_hg.root(act, 0, i)
                s_hg.round(act, tile(g_hi, i), 0, i)
            turns(act, HG_HEADS, hg_head)
            out_hg.act(act)
            mlp[1].act(act, post_hg.added.at)

            pre_dsa.act(act, mlp[1].post.added.at)

            def root_of(g):
                if g < 5:
                    n_idx.root(act, g, users=idx_ready.at(g - 1) if g else None)
                else:
                    n_key.root(act, users=idx_ready.at(4))
            for g in range(NG):
                bank = arrived(act, st_dsa, g)
                n, k = (n_idx, g) if g < 5 else (n_key, 0)
                n.square(act, bank[:], 0, k)
                act.copy((idx_q + [idx_k, dsa_cT])[g], bank[:]).then_inc(*taken(st_dsa, g))
                if g:
                    root_of(g - 1)
            root_of(NG - 1)
            bank = arrived(act, st_dsa, NG)
            act.mul(wiT[0:IDX_HEADS, :], bank[0:IDX_HEADS, :], IDX_SCALE).then_inc(*taken(st_dsa, NG))
            act.wait_ge(*c_turned.at(0))
            act.copy(dsa_c, aux[2][:]).then_inc(c_ready.sem, 1)
            act.wait_ge(*wi_turned.at(0))
            act.copy(wi_tok[:], aux[3][:, 0:TB * IDX_HEADS]).then_inc(wi_ready.sem, 1)
            for r, (b, h) in enumerate(REL):
                w = (b + 1) * P
                act.wait_ge(*rel_ready.at(r))
                if r >= 2:
                    act.wait_ge(*scored.at(r - 2))
                act.activation(idx_rel[r % 2][:, 0:w], aux[r % 2][:, 0:w], ACT.Relu).then_inc(rel_taken.sem, 1)
                if h == IDX_HEADS - 1:
                    for q in Q_AFTER[b - 1]:
                        bank = arrived(act, st_dsa, Q0 + q)
                        act.copy(tile(acc, q), bank[:]).then_inc(*taken(st_dsa, Q0 + q))

            def dsa_head(i):
                if isinstance(i, int) or True:
                    act.wait_ge(bank_free[st_dsa.bank(Q0 + 7)], st_dsa.uses(Q0 + 7) + 1)
                n_dq.square(act, tile(acc, i), 0, 0, i)
                n_dq.root(act, 0, i)
                at_dsa.act(act, i, lambda hh: tile(g_hi, i))
            turns(act, DSA_HEADS, dsa_head)
            ffn[0].act(act, lambda c: (bank_free[st_dsa_o.bank(c)], st_dsa_o.uses(c) + 1))

            pre_ret.act(act, ffn[0].h_at)

            def ret_head(i):
                for m in range(RV + 1):
                    if m < RV:
                        bank = arrived(act, st_ret, 4 + m, i)
                        act.copy(ret_vT[m % 2], bank[:]).then_inc(*taken(st_ret, 4 + m))
                    if m >= 1:
                        act.wait_ge(*ret_v_turned.at(m - 1, i))
                        act.copy(ret_vtok.rearrange("p (b e) -> p b e", b=TB)[:, :, (m - 1) * P:m * P],
                                 aux[2 + (m - 1) % 2][:].rearrange("p (b e) -> p b e", b=TB)).then_inc(ret_v_ready.sem, 1)
                for m in range(RV):
                    bank = arrived(act, st_ret, 8 + m, i)
                    act.activation(ret_gate[m], bank[:], ACT.Silu).then_inc(*taken(st_ret, 8 + m))
                for m in range(RV):
                    act.wait_ge(*ret_o.at(m, i))
                    n_ret.square(act, aux[2 + m % 2][:], m, 0, i)
                    act.copy(ret_raw[m], aux[2 + m % 2][:]).then_inc(ret_raw_ready.sem, 1)
                n_ret.root(act, 0, i)
                for m in range(RV):
                    s_ret.round(act, tile(g_hi, m), m, i)
            turns(act, RET_HEADS, ret_head)
            ffn[1].act(act, lambda c: (bank_free[st_ret.bank(12 + c)], st_ret.uses(12 + c, RET_HEADS - 1) + 1))

        @block.vector
        def _(dve):
            count = 0

            def step(ins):
                nonlocal count
                count += 1
                ins.then_inc(setup.sem, 1)
                dve.wait_ge(setup.sem, count)

            dve.sem_inc(at_mla.out_lo.sem, 1)
            for c in range(DC):
                dve.wait_ge(*x_turned.at(c))
                dve.tensor_copy(tile(hT, c), aux[c % 2][:]).then_inc(h_ready.sem, 1)
            for k, (rows_t, n, c0) in enumerate(row_tiles):
                dve.wait_ge(*turned.at(k))
                dve.tensor_copy(cols[:, c0:c0 + n], aux[2 + k % 2][:, 0:n]).then_inc(turned_out.sem, 1)
            dve.wait_ge(*turned_out.at(5))
            dve.wait_ge(pos_in, 16)
            step(dve.tensor_copy(pos_f, pos_i.bitcast(I32)))
            step(dve.tensor_scalar(angle, pos_f, inv_freq, None, ALU.mult))
            for k, quarter in enumerate((0.0, 0.25)):
                step(dve.tensor_scalar(cycles, angle, 1.0 / (2 * np.pi), quarter, ALU.mult, ALU.add))
                step(dve.tensor_scalar(cycles, cycles, ROUND, None, ALU.add))
                step(dve.tensor_scalar(cycles, cycles, -ROUND, None, ALU.add))
                if k:
                    dve.wait_ge(*sin_ready.at(0))
                for n, part in enumerate(TWO_PI):
                    step(dve.scalar_tensor_tensor(reduced, cycles, -part, reduced if n else angle, ALU.mult, ALU.add))
                step(dve.tensor_scalar(reduced, reduced, quarter * 2 * np.pi, None, ALU.add))
                dve.tensor_scalar(reduced, reduced, 3.1415925, -3.1415925, ALU.min, ALU.max).then_inc(angle_ready.sem, 1)
            dve.wait_ge(*sin_ready.at(1))
            step(dve.tensor_scalar(rope_sin, rope_sin, rope_sign, None, ALU.mult))
            z = [lb[:, k * DC:k * DC + DC] for k in range(8)]
            l0, l1 = cols[:, 128:128 + DC], cols[:, 128 + DC:128 + 2 * DC]
            step(dve.tensor_tensor(z[0], l0, l1, ALU.max))
            dve.tensor_tensor(z[1], l0, z[0], ALU.subtract)
            dve.tensor_tensor(z[2], l1, z[0], ALU.subtract).then_inc(setup_lb_diff[0], 1)
            dve.wait_ge(*lb_exp.at(0))
            step(dve.tensor_tensor(z[3], z[1], z[2], ALU.add))
            step(dve.reciprocal(z[4], z[3]))
            step(dve.tensor_tensor(z[5], z[1], z[4], ALU.mult))
            step(dve.tensor_tensor(z[6], z[2], z[4], ALU.mult))
            step(dve.tensor_tensor(z[6], z[5], z[6], ALU.add))
            step(dve.tensor_tensor(z[6], z[6], z[5], ALU.subtract))
            step(dve.tensor_scalar(z[7], z[6], -1.0, 1.0, ALU.mult, ALU.add))

            pre_mla.dve(dve)

            def normed_c(n, gain_name, first, count_c):
                dve.wait_ge(*n.ready())
                for c in range(count_c + 1):
                    if c < count_c:
                        s_c.free(dve, first + c)
                        dve.scalar_tensor_tensor(tmp[(first + c) % 2], mla_c[first + c], gain(gain_name, c), rstd,
                                                 ALU.mult, ALU.mult).then_inc(s_c.whole.sem, 1)
                    if c >= 1:
                        k = first + c - 1
                        s_c.rest(dve, tile(g_lo, k), tile(g_hi, k), k)
            normed_c(n_cq, "mla_q", 0, 4)
            normed_c(n_ckv, "mla_kv", 4, 2)

            def rotate(st, j, i, dst, done):
                for k, table in ((0, rope_cos), (1, rope_sin)):
                    bank = arrived(dve, st, j + k, i)
                    dve.tensor_tensor(tmp[k], bank[:], table, ALU.mult).then_inc(*taken(st, j + k))
                emptied(dve, st, j + 1, i)
                dve.tensor_tensor(dst, tmp[0], tmp[1], ALU.add).then_inc(done.sem, 1)
            dve.wait_ge(*s_c.low.at(5))
            rotate(st_mla_in, 6, 0, k_rope, k_rope_ready)
            dve.wait_ge(*k_rope_ready.at(0))

            def mla_heads(i):
                rotate(st_mla, 2, i, q_rope, q_rope_ready)
                at_mla.dve(dve, i, lambda t: causal("causal", t % TB), lambda hh: tile(a_lo, i * 2 + hh),
                           lambda hh: tile(a_hi, i * 2 + hh))
            turns(dve, st_mla.turns, mla_heads)
            out_mla.dve(dve)
            mlp[0].dve(dve)

            pre_hg.dve(dve)
            dve.memset(hg_a, 0.0).then_inc(hg_cleared.sem, 1)
            dve.wait_ge(*hg_cleared.at(0))
            by_chunk = lambda t: t.rearrange("p (n c) -> p n c", n=HG_N)
            chunk_col = lambda t, c: by_chunk(t)[:, :, c:c + 1].to_broadcast([P, HG_N, HG_CHUNK])
            state = lambda n: hg_state[:, n * P:n * P + P]

            def hg_head(i):
                emptied(dve, st_hg, 1, i)
                dve.tensor_scalar(hg_f, hg_sig, lb[:, bass.ds(7 * DC + i, 1)], lb[:, bass.ds(6 * DC + i, 1)],
                                  ALU.mult, ALU.add).then_inc(hg_f_ready.sem, 1)
                dve.wait_ge(*hg_f_ready.at(0, i))
                dve.tensor_scalar(hg_k, hg_f, -1.0, 1.0, ALU.mult, ALU.add).then_inc(hg_k_ready.sem, 1)
                dve.wait_ge(*hg_logf_ready.at(0, i))
                dve.tensor_tensor_scan(hg_b, tab["scan_keep"][:], hg_logf, 0.0, ALU.mult, ALU.add).then_inc(hg_b_ready.sem, 1)
                dve.wait_ge(*hg_b_ready.at(0, i))
                dve.wait_ge(*hg_k_ready.at(0, i))
                dve.tensor_tensor(by_chunk(hg_d), by_chunk(hg_b), chunk_col(hg_b, HG_CHUNK // 2),
                                  ALU.subtract).then_inc(hg_d_ready.sem, 1)
                dve.tensor_tensor(by_chunk(hg_d2), chunk_col(hg_b, HG_CHUNK - 1), by_chunk(hg_b),
                                  ALU.subtract).then_inc(hg_d2_ready.sem, 1)
                emptied(dve, st_hg, 0, i)
                dve.wait_ge(*hg_e_ready.at(0, i))
                dve.tensor_tensor(hg_qrel, hg_e[0], hg_q, ALU.mult).then_inc(hg_rel_ready.sem, 1)
                dve.wait_ge(*hg_e_ready.at(1, i))
                dve.tensor_tensor(hg_krel, hg_e[1], hg_k, ALU.mult).then_inc(hg_rel_ready.sem, 1)
                dve.wait_ge(*hg_e_ready.at(2, i))
                dve.tensor_tensor(hg_qdec, hg_e[2], hg_q, ALU.mult).then_inc(hg_dec_ready.sem, 1)
                dve.wait_ge(*hg_e_ready.at(3, i))
                dve.tensor_tensor(hg_kdec, hg_e[3], hg_k, ALU.mult).then_inc(hg_dec_ready.sem, 1)
                dve.wait_ge(*hg_scores.at(0, i))
                plain_wait(dve)
                dve.copy_predicated(hg_a.rearrange("p (g c) -> p g c", g=TB),
                                    hg_mask[:].rearrange("p (a c) -> p a c", a=1).to_broadcast([P, TB, P]),
                                    aux[0][:].rearrange("p (g c) -> p g c", g=TB)).then_inc(hg_masked.sem, 1)
                for n in range(HG_N - 1):
                    u = aux[n % HG_G][:, n // HG_G * P:n // HG_G * P + P]
                    if n == 0:
                        dve.wait_ge(*hg_u.at(0, i))
                        dve.tensor_copy(state(1), u).then_inc(hg_state_ready.sem, 1)
                    else:
                        dve.wait_ge(*hg_state_ready.at(n - 1, i))
                        last = (n + 1) * HG_CHUNK - 1
                        dve.scalar_tensor_tensor(state(n + 1), state(n), hg_dec[:, last:last + 1], u,
                                                 ALU.mult, ALU.add).then_inc(hg_state_ready.sem, 1)
                dve.wait_ge(*n_hg.ready(0, i))
                dve.scalar_tensor_tensor(tmp[1], aux[0][:], gain("hg_o", 0), rstd, ALU.mult, ALU.mult).then_inc(hg_y.sem, 1)
                dve.wait_ge(*hg_y.at(0, i))
                emptied(dve, st_hg, 3, i)
                s_hg.free(dve, 0, i)
                dve.tensor_tensor(tmp[0], tmp[1], hg_gate, ALU.mult).then_inc(s_hg.whole.sem, 1)
                s_hg.rest(dve, tile(g_lo, i), tile(g_hi, i), 0, i)
            turns(dve, HG_HEADS, hg_head)
            out_hg.dve(dve)
            mlp[1].dve(dve)

            pre_dsa.dve(dve)
            for g in range(5):
                dst, name = (idx_q[g], "dsa_iq") if g < 4 else (idx_k, "dsa_ik")
                dve.wait_ge(*n_idx.ready(g))
                dve.scalar_tensor_tensor(dst, dst, gain(name, 0), rstd, ALU.mult, ALU.mult).then_inc(idx_ready.sem, 1)
            dve.wait_ge(*n_key.ready())
            dve.scalar_tensor_tensor(dsa_kT, dsa_cT, gain("dsa_k", 0), rstd, ALU.mult, ALU.mult).then_inc(key_ready.sem, 1)
            dve.wait_ge(*wi_ready.at(0))
            for r, (b, h) in enumerate(REL):
                w = (b + 1) * P
                score = dsa_bias[b][:, 0:w]
                dve.wait_ge(*rel_taken.at(r))
                if h:
                    dve.wait_ge(*scored.at(r - 1))
                dve.scalar_tensor_tensor(score, idx_rel[r % 2][:, 0:w], wi_tok[:, b * IDX_HEADS + h:b * IDX_HEADS + h + 1],
                                         score if h else causal("admissible", b), ALU.mult, ALU.add).then_inc(scored.sem, 1)
                if h < IDX_HEADS - 1:
                    continue
                dve.wait_ge(*scored.at(r))
                rounds = TOPK // 8
                with dve.Fori(0, rounds):
                    dve.max(top8[:], score)
                    dve.drain()
                    dve.match_replace(score, top8[:], score, GONE)
                    dve.drain()
                dve.tensor_scalar(score, score, GONE / 2, NEG, ALU.is_gt, ALU.mult).then_inc(dsa_bias_ready.sem, 1)
            dve.wait_ge(*dsa_bias_ready.at(TB - 2))

            def dsa_head(i):
                dve.wait_ge(*n_dq.ready(0, i))
                dve.scalar_tensor_tensor(dsa_q, tile(acc, i), gain("dsa_q", 0), rstd, ALU.mult,
                                         ALU.mult).then_inc(dsa_q_ready.sem, 1)
                at_dsa.dve(dve, i, lambda t: dsa_bias[t][:, 0:(t + 1) * P] if t else causal("admissible", 0),
                           lambda hh: tile(g_lo, i), lambda hh: tile(g_hi, i))
            turns(dve, DSA_HEADS, dsa_head)
            for m in range(DC):
                bank = arrived(dve, st_dsa_o, m)
                dve.tensor_tensor(tile(hT, m), bank[:], tile(hT, m), ALU.add).then_inc(*taken(st_dsa_o, m))
            ffn[0].dve(dve)

            pre_ret.dve(dve)

            def ret_head(i):
                s_ret.free(dve, 0, i)
                for s, dst in ((0, ret_q), (1, ret_k)):
                    if s:
                        dve.wait_ge(*ret_qk_ready.at(1, i))
                    p0, p1 = arrived(dve, st_ret, 2 * s, i), arrived(dve, st_ret, 2 * s + 1, i)
                    dve.tensor_tensor(dst[0], p0[:], ret_cos[:], ALU.mult).then_inc(ret_part.sem, 1)
                    dve.tensor_tensor(tmp[0], p1[:], ret_sin[:], ALU.mult).then_inc(ret_part.sem, 1)
                    dve.tensor_tensor(tmp[1], p0[:], ret_sin[:], ALU.mult).then_inc(*taken(st_ret, 2 * s))
                    dve.tensor_tensor(dst[1], p1[:], ret_cos[:], ALU.mult).then_inc(*taken(st_ret, 2 * s + 1))
                    dve.wait_ge(*ret_part.at(2 * s + 1, i))
                    dve.tensor_tensor(dst[0], dst[0], tmp[0], ALU.subtract).then_inc(ret_qk_ready.sem, 1)
                    emptied(dve, st_ret, 2 * s + 1, i)
                    dve.tensor_tensor(dst[1], tmp[1], dst[1], ALU.add).then_inc(ret_qk_ready.sem, 1)
                for j in range(TB):
                    w = T - j * P
                    dve.wait_ge(*ret_scores.at(j, i))
                    dve.tensor_tensor(ret_s[j][:, 0:w], aux[j % 2][:, 0:w], ret_decay[:, bass.ds(i * T, w)],
                                      ALU.mult).then_inc(ret_s_ready.sem, 1)
                dve.wait_ge(*n_ret.ready(0, i))
                for m in range(RV + 1):
                    if m < RV:
                        dve.scalar_tensor_tensor(ret_raw[m], ret_raw[m], gain("ret_out", i * RV + m), rstd, ALU.mult,
                                                 ALU.mult).then_inc(ret_y.sem, 1)
                        dve.wait_ge(*ret_y.at(m, i))
                        s_ret.free(dve, m, i)
                        dve.tensor_tensor(tmp[m % 2], ret_raw[m], ret_gate[m], ALU.mult).then_inc(s_ret.whole.sem, 1)
                    if m >= 1:
                        s_ret.rest(dve, tile(g_lo, m - 1), tile(g_hi, m - 1), m - 1, i)
                for m in range(DC):
                    bank = arrived(dve, st_ret, 12 + m, i)
                    dve.tensor_tensor(tile(hT, m), bank[:], tile(hT, m), ALU.add).then_inc(*taken(st_ret, 12 + m))
            turns(dve, RET_HEADS, ret_head)
            ffn[1].dve(dve)

            for k in range(2 * TB):
                dve.wait_ge(*out_turned.at(k))
                dve.tensor_copy(acc[:, k * T:k * T + T], aux[k % 4][:]).then_inc(out_ready.sem, 1)

        @block.tensor
        def _(pe):
            pe.wait_ge(tables_in, 16 * (len(TABLE_WIDTH) + 1))
            pe.wait_ge(x_in, 16)
            for c in range(DC):
                if c >= 2:
                    pe.wait_ge(*h_ready.at(c - 2))
                for b in range(TB):
                    last = pe.transpose(aux[c % 2][:, b * P:b * P + P], acc[:, b * D + c * P:b * D + c * P + P], ident[:])
                last.then_inc(x_turned.sem, 1)
            pe.wait_ge(rows_in, 16 * len(row_loads))
            for k, (rows_t, n, c0) in enumerate(row_tiles):
                if k >= 2:
                    pe.wait_ge(*turned_out.at(k - 2))
                pe.transpose(aux[2 + k % 2][:, 0:n], rows_t[0:n, :], ident[0:n, 0:n]).then_inc(turned.sem, 1)

            pe.wait_ge(*h_ready.at(DC - 1))
            pre_mla.pe(pe)
            for j in range(8):
                unit(pe, st_mla_in, j, DC, a_hi, a_lo, ready=pre_mla.ready if j == 0 else None)
                if 1 <= j <= 6:
                    n, c = (n_cq, j - 1) if j <= 4 else (n_ckv, j - 5)
                    n.sum(pe, c)

            def mla_heads(i):
                for j in range(4):
                    unit(pe, st_mla, j, MLA_Q // P, g_hi, g_lo, i, ready=s_c.low.at if j == 0 else None)
                for j in range(4, 8):
                    unit(pe, st_mla, j, MLA_KV // P, g_hi, g_lo, i, k0=4,
                         ready=(lambda k: s_c.low.at(4 + k)) if j == 4 else None)
                    if j >= 6:
                        hh = j - 6
                        emptied(pe, st_mla, 5 + 2 * hh, i)
                        if hh:
                            pe.wait_ge(*v_ready.at(0, i))
                        turn_block(pe, aux[2], vT).then_inc(v_turned.sem, 1)
                for j in (0, 1, 4, 6):
                    emptied(pe, st_mla, j, i)
                pe.wait_ge(*q_rope_ready.at(0, i))
                pe.wait_ge(*k_rope_ready.at(0))
                pe.wait_ge(*v_ready.at(1, i))

                def score(t, o, w):
                    hh, b = t // TB, t % TB
                    h0 = hh * MLA_ROPE
                    pe.matmul(o[:, 0:w], qn[hh][:, b * P:b * P + P], kn[hh][:, 0:w], start=True, stop=False)
                    return pe.matmul(o[:, 0:w], q_rope[h0:h0 + MLA_ROPE, b * P:b * P + P], k_rope[h0:h0 + MLA_ROPE, 0:w],
                                     start=False, stop=True)
                at_mla.pe(pe, i, score, lambda hh, kb: vtok[hh][:, kb * P:kb * P + P])
            turns(pe, st_mla.turns, mla_heads)
            out_mla.pe(pe, lambda k: at_mla.out_lo.at(k))
            mlp[0].pe(pe)

            pre_hg.pe(pe)

            def hg_units(js, i, ready=None):
                for j in js:
                    unit(pe, st_hg, j, DC, a_hi, a_lo, i, ready=ready if j == 0 else None)

            def hg_recur(i):
                pe.wait_ge(*hg_rel_ready.at(1, i))
                for g in range(TB):
                    s = slice(g * P, g * P + P)
                    last = pe.matmul(aux[0][:, s], hg_krel[:, s], hg_qrel[:, s], start=True, stop=True)
                last.then_inc(hg_scores.sem, 1)
                emptied(pe, st_hg, 2, i)
                turn_block(pe, aux[1], hg_vT).then_inc(hg_v_turned.sem, 1)
                pe.wait_ge(*hg_dec_ready.at(1, i))
                pe.wait_ge(*hg_v_ready.at(0, i))
                turn_block(pe, aux[1], hg_kdec).then_inc(hg_k_turned.sem, 1)
                pe.wait_ge(*hg_kT_ready.at(0, i))

                def outer(g):
                    for c in range(HG_G):
                        t = slice(c * HG_CHUNK, (c + 1) * HG_CHUNK)
                        s = slice(g * P, g * P + P)
                        last = pe.matmul(aux[c][:, s], hg_kT[t, s], hg_v[t, s], start=True, stop=True)
                    return last

                pe.wait_ge(*hg_masked.at(0, i))
                for g in range(TB):
                    last = outer(g)
                last.then_inc(hg_u.sem, 1)

            def hg_output(i):
                def output(g):
                    s = slice(g * P, g * P + P)
                    last = pe.matmul(aux[0][:, s], hg_v[:, s], hg_a[:, s], start=True, stop=True,
                                     skip_group_check=True)
                    for c in range(HG_G):
                        n = g * HG_G + c
                        if n == 0:
                            continue
                        t = slice(n * HG_CHUNK, (n + 1) * HG_CHUNK)
                        last = pe.matmul(aux[0][:, t], hg_state[:, n * P:n * P + P], hg_qdec[:, t], start=False,
                                         stop=True, skip_group_check=True)
                    return last
                pe.wait_ge(*hg_state_ready.at(HG_N - 2, i))
                for g in range(TB):
                    last = output(g)
                last.then_inc(hg_o.sem, 1)
                n_hg.sum(pe, 0, 0, i)
            hg_units(range(4), 0, pre_hg.ready)
            with pe.Fori(0, HG_HEADS - 1) as i:
                hg_units((0, 1), i + 1)
                hg_recur(i)
                hg_units((2, 3), i + 1)
                hg_output(i)
            hg_recur(HG_HEADS - 1)
            hg_output(HG_HEADS - 1)
            out_hg.pe(pe, lambda k: s_hg.low.at(0, k))
            mlp[1].pe(pe)

            pre_dsa.pe(pe)
            for j in range(NG + 1):
                unit(pe, st_dsa, j, DC, a_hi, a_lo, ready=pre_dsa.ready if j == 0 else None)
                if 1 <= j <= 5:
                    n_idx.sum(pe, 0, j - 1)
            n_key.sum(pe, 0)
            emptied(pe, st_dsa, 5)
            turn_block(pe, aux[2], dsa_cT).then_inc(c_turned.sem, 1)
            emptied(pe, st_dsa, NG)
            for b in range(TB):
                last = pe.transpose(aux[3][:, b * IDX_HEADS:(b + 1) * IDX_HEADS], wiT[0:IDX_HEADS, b * P:b * P + P],
                                    ident[0:IDX_HEADS, 0:IDX_HEADS])
            last.then_inc(wi_turned.sem, 1)
            pe.wait_ge(*idx_ready.at(4))
            pe.wait_ge(*key_ready.at(0))
            for r, (b, h) in enumerate(REL):
                if r >= 2:
                    pe.wait_ge(*rel_taken.at(r - 2))
                h0, w = h % 2 * IDX_DIM, (b + 1) * P
                pe.matmul(aux[r % 2][:, 0:w], idx_q[h // 2][h0:h0 + IDX_DIM, b * P:b * P + P], idx_k[h0:h0 + IDX_DIM, 0:w],
                          start=True, stop=True).then_inc(rel_ready.sem, 1)
                if h == IDX_HEADS - 1:
                    for q in Q_AFTER[b - 1]:
                        unit(pe, st_dsa, Q0 + q, DC, a_hi, a_lo)
            pe.wait_ge(*c_ready.at(0))

            def dsa_head(i):
                n_dq.sum(pe, 0, 0, i)
                pe.wait_ge(*dsa_q_ready.at(0, i))
                at_dsa.pe(pe, i, lambda t, o, w: pe.matmul(o[:, 0:w], dsa_q[:, t * P:t * P + P], dsa_kT[:, 0:w],
                                                           start=True, stop=True),
                          lambda hh, kb: dsa_c[:, kb * P:kb * P + P])
            turns(pe, DSA_HEADS, dsa_head)
            for m in range(DC):
                unit(pe, st_dsa_o, m, DC, g_hi, g_lo, ready=at_dsa.out_lo.at if m == 0 else None)
            ffn[0].pe(pe)

            pre_ret.pe(pe)

            def ret_head(i):
                for j in range(8):
                    unit(pe, st_ret, j, DC, a_hi, a_lo, i, ready=pre_ret.ready if j == 0 else None)
                    if j >= 5:
                        emptied(pe, st_ret, j - 1, i)
                        turn_block(pe, aux[2 + (j - 5) % 2], ret_vT[(j - 5) % 2]).then_inc(ret_v_turned.sem, 1)

                def scores(b):
                    w = T - b * P
                    pe.wait_ge(*ret_qk_ready.at(3, i))
                    if b >= 2:
                        pe.wait_ge(*ret_s_ready.at(b - 2, i))
                    for c in range(2):
                        last = pe.matmul(aux[b % 2][:, 0:w], ret_k[c][:, b * P:b * P + P], ret_q[c][:, b * P:T],
                                         start=c == 0, stop=c == 1)
                    last.then_inc(ret_scores.sem, 1)
                scores(0)
                scores(1)
                for m in range(RV):
                    unit(pe, st_ret, 8 + m, DC, a_hi, a_lo, i)
                    if m == 0:
                        emptied(pe, st_ret, 7, i)
                        pe.wait_ge(*ret_v_ready.at(1, i))
                        turn_block(pe, aux[3], ret_vT[1]).then_inc(ret_v_turned.sem, 1)
                    elif m <= 2:
                        scores(m + 1)
                pe.wait_ge(*ret_v_ready.at(RV - 1, i))
                for m in range(RV + 1):
                    if m < RV:
                        if m >= 2:
                            pe.wait_ge(*ret_raw_ready.at(m - 2, i))
                        for b in range(TB):
                            if m == 0:
                                pe.wait_ge(*ret_s_ready.at(b, i))
                            e = b * RET_DV + m * P
                            last = pe.matmul(aux[2 + m % 2][:, b * P:T], ret_vtok[:, e:e + P], ret_s[b][:, 0:T - b * P],
                                             start=b == 0, stop=b == TB - 1, skip_group_check=True)
                        last.then_inc(ret_o.sem, 1)
                    if m >= 1:
                        n_ret.sum(pe, m - 1, 0, i)
                for m in range(DC):
                    unit(pe, st_ret, 12 + m, RET_DV // P, g_hi, g_lo, i,
                         ready=(lambda k: s_ret.low.at(k, i)) if m == 0 else None)
            turns(pe, RET_HEADS, ret_head)
            ffn[1].pe(pe)

            for c in range(DC):
                pe.wait_ge(*ffn[1].h_at(c))
            for k in range(2 * TB):
                b = k // 2
                if k >= 4:
                    pe.wait_ge(*out_ready.at(k - 4))
                for q in range(4):
                    c = k % 2 * 4 + q
                    last = pe.transpose(aux[k % 4][:, q * P:q * P + P], hT[:, c * T + b * P:c * T + b * P + P], ident[:])
                last.then_inc(out_turned.sem, 1)


_INS = ["x", "positions", "norm_gains", "mla_w_in", "mla_q_norm", "mla_kv_norm", "mla_w_uq", "mla_w_ukv", "mla_w_o",
        "hgrn_w_in", "hgrn_lb_logits", "hgrn_o_norm", "hgrn_w_o", "mlp_w1", "mlp_w2", "norm_mix_g_2", "norm_ffn_g_2",
        "a_w_in_2", "a_q_g_2", "a_k_g_2", "a_iq_g_2", "a_ik_g_2", "a_w_out_2", "b_w_in_2", "b_out_g_2", "b_w_out_2",
        "f_w_up_2", "f_conv_w_2", "f_conv_b_2", "f_w_down_2"]


def kernel(**inputs):
    import concourse.bacc as bacc
    from concourse.bass_utils import run_bass_kernel_spmd as run

    nc = bacc.Bacc("TRN2", target_bir_lowering=False, num_devices=1)
    arrays = {}

    def given(name, a):
        arrays[name] = a
        return nc.dram_tensor(name, a.shape, mybir.dt.from_np(a.dtype), kind="ExternalInput").ap()

    args = [given(f"in_{name}", np.ascontiguousarray(inputs[name])) for name in _INS]
    tabs, hg = shape_tables()
    tables = {k: given(f"table_{k}", np.ascontiguousarray(v)) for k, v in tabs.items()}
    hg_mask = given("table_hg_mask", hg)
    out = nc.dram_tensor("out_0", (1, T, D), F32, kind="ExternalOutput").ap()
    program(nc, *args, tables, hg_mask, out)
    r = run(nc, [arrays], core_ids=[0])
    return r.results[0]["out_0"]
```

```python
from contextlib import ExitStack

import numpy as np
import concourse.bass as bass
from concourse import mybir

F32 = mybir.dt.float32
F32R = mybir.dt.float32r
I32 = mybir.dt.int32
ALU = mybir.AluOpType
ACT = mybir.ActivationFunctionType

P = 128
T = 512
TB = T // P
D = 1024
DC = D // P
RING = 4
SLAB = 2048
EPS = 1e-6
NEG = -1e30
GONE = -3e38

MLA_HEADS, MLA_Q, MLA_KV, MLA_NOPE, MLA_ROPE, MLA_V = 8, 512, 256, 128, 64, 128
MLA_SCALE = (MLA_NOPE + MLA_ROPE) ** -0.5
FF = 4096
HG_HEADS, HG_CHUNK = 8, 32
HG_N = T // HG_CHUNK
HG_G = P // HG_CHUNK
DSA_HEADS, DSA_LAT, IDX_HEADS, IDX_DIM = 8, 128, 8, 64
DSA_CHUNK, TOPK = 64, 128
DSA_SCALE = DSA_LAT ** -0.5
IDX_SCALE = IDX_HEADS ** -0.5 * IDX_DIM ** -0.5
RET_HEADS, RET_DK, RET_DV = 4, 256, 512
FF2 = 2816
FF2C = FF2 // P
CONV_W = 3
ROPE_BASE = 10000.0

TWO_PI = [6.28125, 0.00193500518798828125, 3.0199159819e-7]
ROUND = 1.5 * 2.0 ** 23


def shape_tables():
    f32 = np.float32
    p = np.arange(P)[:, None]
    t = np.arange(T)[None, :]
    tabs = {}
    tabs["ident"] = np.eye(P, dtype=f32)
    tabs["ones"] = np.ones((P, P), f32)
    tabs["ones_half"] = (p // 64 == np.arange(P)[None, :] // 64).astype(f32)
    u = t - (T - P)
    tabs["causal"] = np.where(u <= p, 0.0, NEG).astype(f32)
    tabs["admissible"] = np.where(u < (p // DSA_CHUNK + 1) * DSA_CHUNK, 0.0, NEG).astype(f32)
    tabs["scan_keep"] = np.broadcast_to((t % HG_CHUNK != 0), (P, T)).astype(f32)
    inv = np.power(f32(ROPE_BASE), -np.arange(0, MLA_ROPE, 2, dtype=f32) / f32(MLA_ROPE)).astype(f32)
    half = (np.arange(P) % MLA_ROPE) // (MLA_ROPE // 2)
    tabs["small"] = np.stack([inv[np.arange(P) % (MLA_ROPE // 2)], np.where(half == 0, -1.0, 1.0),
                              np.full(P, EPS), np.zeros(P)], 1).astype(f32)
    inv2 = (f32(1.0) / np.power(f32(ROPE_BASE), np.arange(0, RET_DK, 2, dtype=f32) / f32(RET_DK))).astype(f32)
    ang = (np.arange(T, dtype=f32)[None, :] * inv2[:, None]).astype(f32)
    tabs["ret_cos"] = np.cos(ang.astype(np.float64)).astype(f32)
    tabs["ret_sin"] = np.sin(ang.astype(np.float64)).astype(f32)
    dec = []
    for h in range(RET_HEADS):
        lg = np.log1p(-(2.0 ** (-5.0 - h)))
        dec.append(np.where(t >= p, np.exp(np.maximum(t - p, 0) * lg) * RET_DK ** -0.5, 0.0))
    tabs["ret_decay"] = np.concatenate(dec, 1).astype(f32)
    a, b = np.arange(P)[:, None], np.arange(P)[None, :]
    hg = ((a // HG_CHUNK == b // HG_CHUNK) & (a <= b)).astype(np.int32)
    return tabs, hg


TABLE_WIDTH = {"ident": P, "ones": P, "ones_half": P, "causal": T, "admissible": T, "scan_keep": T, "small": 4,
               "ret_cos": T, "ret_sin": T, "ret_decay": RET_HEADS * T}


class Signal:

    def __init__(self, sem, per=1, credit=0):
        self.sem, self.per, self.credit = sem, per, credit

    def at(self, j, i=0):
        return self.sem, i * self.per + (j + 1 + self.credit)


class Slab:

    def __init__(self, kc, units, parts):
        self.kc, self.units, self.parts = kc, units, parts
        self.loads = len(parts(0))


class Stage:

    def __init__(self, before, turns, slabs):
        self.turns, self.slabs = turns, slabs
        self.per = sum(s.units for s in slabs)
        assert turns == 1 or (self.per % RING == 0 and len(slabs) % 2 == 0)
        self.base = before.end if before else 0
        self.end = self.base + turns * self.per
        self.slab_base = before.slab_end if before else 0
        self.slab_end = self.slab_base + turns * len(slabs)
        self.loads_base = before.loads_end if before else [0, 0]
        self.loads_per = [0, 0]
        self.first, at = [], 0
        self.loaded_at = []
        for q, s in enumerate(slabs):
            self.first.append(at)
            at += s.units
            self.loads_per[self.slot(q)] += s.loads
            self.loaded_at.append(self.loads_per[self.slot(q)])
        self.loads_end = [b + turns * n for b, n in zip(self.loads_base, self.loads_per)]
        self.before_last = before.slabs[-1].units if before else 0

    def slot(self, q):
        return (self.slab_base + q) % 2

    def bank(self, j):
        return (self.base + j) % RING

    def done(self, j, i=0):
        return i * self.per + (self.base + j + 1)

    def uses(self, j, i=0):
        return i * (self.per // RING) + (self.base + j) // RING

    def loaded(self, q, i=0):
        s = self.slot(q)
        return i * (16 * self.loads_per[s]) + 16 * (self.loads_base[s] + self.loaded_at[q])

    def raw_free(self, q, i=0):
        if q >= 2:
            return i * self.per + self.base + self.first[q - 1]
        if q == 1:
            return i * self.per + self.base
        last = min(self.before_last, self.slabs[-1].units) if self.turns > 1 else self.before_last
        return i * self.per + self.base - last


def turns(eng, n, body):
    if n == 1:
        body(0)
    else:
        with eng.Fori(0, n) as i:
            body(i)


def turns_from(eng, n, body):
    body(0, True)
    if n == 2:
        body(1, False)
    elif n > 2:
        with eng.Fori(1, n) as i:
            body(i, False)


def program(nc, x, positions, norm_gains, mla_w_in, mla_q_norm, mla_kv_norm, mla_w_uq, mla_w_ukv, mla_w_o, hgrn_w_in,
            hgrn_lb_logits, hgrn_o_norm, hgrn_w_o, mlp_w1, mlp_w2, norm_mix_g_2, norm_ffn_g_2, a_w_in_2, a_q_g_2,
            a_k_g_2, a_iq_g_2, a_ik_g_2, a_w_out_2, b_w_in_2, b_out_g_2, b_w_out_2, f_w_up_2, f_conv_w_2, f_conv_b_2,
            f_w_down_2, tables, hg_mask_dram, out):
    with ExitStack() as ctx:
        def sb(name, width, dt=F32, parts=P):
            return ctx.enter_context(nc.sbuf_tensor(name, [parts, width], dt))

        def sem(name):
            return ctx.enter_context(nc.semaphore(name))

        def signal(name, per=1, credit=0):
            return Signal(sem(name), per, credit)

        def plain_wait(dve, s=0):
            dve.memset(carrier[:, s:s + 1], 0.0)

        shared_sems = {}

        def shared(name, per=1, turns=1):
            s, used = shared_sems.get(name) or (sem(name), 0)
            shared_sems[name] = s, used + per * turns
            return Signal(s, per, used)

        def tile(t, c, width=T):
            return t[:, bass.ds(c * width, width)]

        raw = [sb(f"raw{r}", SLAB) for r in range(2)]
        w_hi = [sb(f"w_hi{r}", DC * P, F32R) for r in range(RING)]
        w_lo = [sb(f"w_lo{r}", DC * P, F32R) for r in range(RING)]
        hT = sb("hT", DC * T)
        a_hi, a_lo = sb("a_hi", DC * T, F32R), sb("a_lo", DC * T, F32R)
        g_hi, g_lo = sb("g_hi", DC * T, F32R), sb("g_lo", DC * T, F32R)
        acc = sb("acc", DC * T)
        F = sb("F", 20 * T)
        cols = sb("cols", 128 + 16 + 4 * 88)
        tab = {k: sb(k, w) for k, w in TABLE_WIDTH.items() if not k.startswith("ret_")}
        ret_cos, ret_sin, ret_decay = sb("ret_cos", T), sb("ret_sin", T), sb("ret_decay", RET_HEADS * T)
        hg_mask = sb("hg_mask", P, I32)
        ident, ones, ones_half = tab["ident"], tab["ones"], tab["ones_half"]
        inv_freq, rope_sign, eps = (tab["small"][:, k:k + 1] for k in range(3))
        zero = tab["small"][:, 3:4]
        lb = sb("lb", 8 * DC)
        row_min, row_bias, row_sum, row_inv = (sb(n, 3) for n in ("row_min", "row_bias", "row_sum", "row_inv"))
        top8 = sb("top8", 8)
        carrier = sb("carrier", 3)
        wi_tok = sb("wi_tok", TB * IDX_HEADS)
        q_log, q_rstds = sb("q_log", DSA_HEADS * TB), sb("q_rstds", DSA_HEADS * TB)
        q_rstd, q_rstd_neg = sb("q_rstd", DSA_HEADS * TB // 2), sb("q_rstd_neg", DSA_HEADS * TB // 2)
        qk_gain = sb("qk_gain", 1)

        sq = [tile(F, 0), tile(F, 1)]
        log_ms, rstd = tile(F, 2), tile(F, 3)
        tmp = [tile(F, 4), tile(F, 5)]

        psum = [ctx.enter_context(nc.psum_tensor(f"proj{b}", [P, T], F32)) for b in range(RING)]
        aux = [ctx.enter_context(nc.psum_tensor(f"aux{b}", [P, T], F32)) for b in range(4)]

        def rows(ap, width=P):
            return ap.rearrange("(c p) -> c p", p=width)

        vec_rows = []
        where = {}
        at = 0

        def vec(name, n, src):
            nonlocal at
            where[name] = at
            vec_rows.append((at, n, 0, P, src))
            at += n

        vec("norm", 64, norm_gains.rearrange("l k (c p) -> (l k c) p", p=P))
        vec("mix", 16, norm_mix_g_2.rearrange("l (c p) -> (l c) p", p=P))
        vec("ffn", 16, norm_ffn_g_2.rearrange("l (c p) -> (l c) p", p=P))
        vec("ret_out", 16, b_out_g_2.rearrange("l (c p) -> (l c) p", p=P))
        vec("mla_q", 4, mla_q_norm.rearrange("l (c p) -> (l c) p", p=P))
        vec("mla_kv", 2, mla_kv_norm.rearrange("l (c p) -> (l c) p", p=P))
        vec("hg_o", 1, hgrn_o_norm)
        vec("dsa_q", 1, a_q_g_2)
        vec("dsa_k", 1, a_k_g_2)
        for name, src in (("dsa_iq", a_iq_g_2), ("dsa_ik", a_ik_g_2)):
            where[name] = at
            vec_rows.append((at, 1, 0, IDX_DIM, src))
            vec_rows.append((at, 1, IDX_DIM, IDX_DIM, src))
            at += 1
        VEC = at
        CONV0 = 144
        UC = 2 * FF2C
        row_tiles = [(tile(F, 6 + k, P), n, c0) for k, (n, c0) in
                     enumerate([(VEC, 0), (16, 128), (88, CONV0), (88, CONV0 + 88), (88, CONV0 + 176), (88, CONV0 + 264)])]
        row_loads = [(row_tiles[0][0][r:r + n, c:c + w], src) for r, n, c, w, src in vec_rows]
        row_loads.append((row_tiles[1][0][0:16, :], hgrn_lb_logits.rearrange("l (c p) -> (l c) p", p=P)))
        for l in range(2):
            w = f_conv_w_2[l].rearrange("k (c p) -> (k c) p", p=P)
            row_loads.append((row_tiles[2 + 2 * l][0][0:2 * UC, :], w[0:2 * UC, :]))
            row_loads.append((row_tiles[3 + 2 * l][0][0:UC, :], w[2 * UC:3 * UC, :]))
            row_loads.append((row_tiles[3 + 2 * l][0][UC:2 * UC, :], f_conv_b_2[l].rearrange("(c p) -> c p", p=P)))

        def gain(name, c, n=1):
            return cols[:, bass.ds(where[name] + c, n)]

        def conv_col(l, k, c):
            return cols[:, bass.ds(CONV0 + 176 * l + k * UC + c, 1)]

        def kpn(w):
            return w.rearrange("(k p) n -> p k n", p=P)

        def plain(w, k0=0, kc=DC, width=256, col=lambda i: 0):
            v = kpn(w)
            k = k0 if callable(k0) else (lambda i: k0)
            return Slab(kc, width // P, lambda i: [(0, width, v[:, bass.ds(k(i), kc), bass.ds(col(i), width)])])

        stages = []

        def stage(n, slabs):
            s = Stage(stages[-1] if stages else None, n, slabs)
            stages.append(s)
            return s

        w_in = kpn(mla_w_in[0])
        kr0 = MLA_Q + MLA_KV
        half = MLA_ROPE // 2
        st_mla_in = stage(1, [plain(mla_w_in[0], col=lambda i, c=c: c * 256) for c in range(3)] + [
            Slab(DC, 2, lambda i: [(64 * r, 64, w_in[:, :, kr0:kr0 + 64]) for r in range(2)]
                 + [(128 + 32 * r, 32, w_in[:, :, kr0 + 32 * (1 - r % 2):kr0 + 32 * (1 - r % 2) + 32]) for r in range(4)])])
        uq = kpn(mla_w_uq[0])
        QH = MLA_NOPE + MLA_ROPE

        MLA_TURN = 4

        def uq_parts(i, a):
            c0 = lambda h: i * (MLA_TURN * QH) + (a + h) * QH
            p = [(128 * h, 128, uq[:, :, bass.ds(c0(h), 128)]) for h in range(2)]
            p += [(256 + 64 * h, 64, uq[:, :, bass.ds(c0(h) + MLA_NOPE, 64)]) for h in range(2)]
            p += [(384 + 64 * h + 32 * r, 32, uq[:, :, bass.ds(c0(h) + MLA_NOPE + 32 * (1 - r), 32)])
                  for h in range(2) for r in range(2)]
            return p

        KVH = MLA_NOPE + MLA_V
        st_mla = stage(MLA_HEADS // MLA_TURN, [
            s for a in range(0, MLA_TURN, 2) for s in (
                Slab(MLA_Q // P, 4, lambda i, a=a: uq_parts(i, a)),
                plain(mla_w_ukv[0], kc=MLA_KV // P, width=2 * KVH, col=lambda i, a=a: i * (MLA_TURN * KVH) + a * KVH))])

        def square_out(w):
            return stage(1, [plain(w, col=lambda i, c=c: c * 256) for c in range(4)])

        st_mla_o = square_out(mla_w_o[0])

        def mlp_stage(l):
            return stage(FF // D, [plain(mlp_w1[l], col=lambda i, c=c: i * D + c * 256) for c in range(4)]
                         + [plain(mlp_w2[l], k0=lambda i: i * DC, col=lambda i, c=c: c * 256) for c in range(4)])

        st_mlp = [mlp_stage(0)]
        hg_w = kpn(hgrn_w_in[0])
        st_hg = stage(HG_HEADS, [Slab(DC, 2, lambda i, a=a: [(128 * r, 128, hg_w[:, :, bass.ds(i * P + (a + r) * D, P)])
                                                            for r in range(2)]) for a in (0, 2)])
        st_hg_o = square_out(hgrn_w_o[0])
        st_mlp.append(mlp_stage(1))

        dsa_w = kpn(a_w_in_2[0])
        o1 = DSA_HEADS * DSA_LAT
        o2 = o1 + DSA_LAT
        o3 = o2 + IDX_HEADS * IDX_DIM
        o4 = o3 + IDX_DIM
        st_dsa = stage(1, [plain(a_w_in_2[0], col=lambda i, c=c: o2 + 256 * c) for c in range(2)] + [
            Slab(DC, 2, lambda i: [(64 * r, 64, dsa_w[:, :, o3:o4]) for r in range(2)] + [(128, 128, dsa_w[:, :, o1:o2])]),
            Slab(DC, 1, lambda i: [(0, IDX_HEADS, dsa_w[:, :, o4:o4 + IDX_HEADS])])]
            + [plain(a_w_in_2[0], col=lambda i, c=c: 256 * c) for c in range(4)])
        st_dsa_o = square_out(a_w_out_2[0])

        def ffn_stages(l):
            up = kpn(f_w_up_2[l])

            def blocks(n, first, size):
                pairs = [Slab(DC, 2, lambda i, j=j: [(0, P, up[:, :, bass.ds(i * D + (first + j) * P, P)]),
                                                     (P, P, up[:, :, bass.ds(i * D + FF2 + (first + j) * P, P)])])
                         for j in range(size)]
                return stage(n, pairs + [plain(f_w_down_2[l], k0=lambda i: i * DC + first, kc=size,
                                               col=lambda i, c=c: c * 256) for c in range(4)])
            full = FF2C // DC
            return [(blocks(full, 0, DC), 0, DC), (blocks(1, full * DC, FF2C - full * DC), full * DC, FF2C - full * DC)]

        st_ffn = [ffn_stages(0)]
        dq, dv = RET_HEADS * RET_DK, RET_HEADS * RET_DV

        def ret_slabs(part, h):
            w, v0 = b_w_in_2[0], 2 * dq
            if part == "qk":
                return [plain(w, col=lambda i, c=c: h(i) * RET_DK + c) for c in (0, dq)]
            if part == "out":
                return [plain(b_w_out_2[0], k0=lambda i: h(i) * (RET_DV // P), kc=RET_DV // P, width=512,
                              col=lambda i, c=c: 512 * c) for c in range(2)]
            c0 = v0 if part == "v" else v0 + dv
            return [plain(w, col=lambda i, c=c: h(i) * RET_DV + c0 + 256 * c) for c in range(2)]

        this, following, final = (lambda i: i), (lambda i: i + 1), (lambda i: RET_HEADS - 1)
        st_ret_qk = stage(1, ret_slabs("qk", this))
        st_ret = stage(RET_HEADS - 1, ret_slabs("v", this) + ret_slabs("g", this) + ret_slabs("qk", following)
                       + ret_slabs("out", this))
        st_ret_end = stage(1, ret_slabs("v", final) + ret_slabs("g", final) + ret_slabs("out", final))
        st_ffn.append(ffn_stages(1))

        loaded = [sem("loaded0"), sem("loaded1")]
        hi_split, lo_split = sem("hi_split"), sem("lo_split")
        unit_done = sem("unit_done")
        bank_free = [sem(f"bank_free{b}") for b in range(RING)]

        def raw_view(slot, s):
            return raw[slot][:, 0:s.kc * s.units * P].rearrange("p (k n) -> p k n", k=s.kc)

        tables_in, rows_in, x_in, pos_in = sem("tables_in"), sem("rows_in"), sem("x_in"), sem("pos_in")
        stored = sem("stored")
        turned = signal("turned")
        turned_out = signal("turned_out")
        x_turned, h_ready = signal("x_turned"), signal("h_ready")
        sq_ready, sq_used = signal("sq_ready"), signal("sq_used")
        log_ready, rstd_ready = signal("log_ready"), signal("rstd_ready")
        setup = signal("setup")
        lb_exp = signal("lb_exp")
        setup_lb_diff = (sem("lb_diff"), 1)

        class Norm:
            squares = groups_done = 0

            def __init__(self, chunks, turns=1, groups=1, matrix=ones, size=None, bank=aux[0]):
                self.chunks, self.per, self.gper = chunks, chunks * groups, groups
                self.matrix, self.bank, self.size = matrix, bank, size or chunks * P
                self.base, self.gbase = Norm.squares, Norm.groups_done
                Norm.squares += turns * self.per
                Norm.groups_done += turns * groups

            def square(self, act, src, c, g=0, i=0):
                m, n = self.base + g * self.chunks + c, len(sq)
                before = m - n + 1 if c >= n else m - c
                if before > 0:
                    act.wait_ge(sq_used.sem, i * self.per + before)
                act.activation(sq[c % n], src, ACT.Square).then_inc(sq_ready.sem, 1)

            def sum(self, pe, c, g=0, i=0):
                m = self.base + g * self.chunks + c
                if c == 0 and self.gbase + g > 0:
                    pe.wait_ge(log_ready.sem, i * self.gper + self.gbase + g)
                pe.wait_ge(sq_ready.sem, i * self.per + m + 1)
                pe.matmul(self.bank[:], self.matrix[:], sq[c % len(sq)], start=c == 0,
                          stop=c == self.chunks - 1).then_inc(sq_used.sem, 1)

            def sum_tokens(self, pe, c):
                m = self.base + c
                if c == 0:
                    pe.wait_ge(log_ready.sem, self.gbase)
                pe.wait_ge(sq_ready.sem, m + 1)
                for b in range(TB):
                    k = c * TB + b
                    last = pe.matmul(self.bank[:, k:k + 1], sq[c % 2][:, b * P:b * P + P], ones[:, 0:1], start=True, stop=True)
                last.then_inc(sq_used.sem, 1)

            def root_tokens(self, act, log, dst):
                act.wait_ge(sq_used.sem, self.base + self.chunks)
                act.activation(log, self.bank[:, 0:self.chunks * TB], ACT.Ln, bias=eps,
                               scale=1.0 / self.size).then_inc(log_ready.sem, 1)
                act.wait_ge(log_ready.sem, self.gbase + 1)
                act.activation(dst, log, ACT.Exp, scale=-0.5).then_inc(rstd_ready.sem, 1)

            def root(self, act, g=0, i=0, users=None):
                n = self.gbase + g
                if n > 0:
                    act.wait_ge(rstd_ready.sem, i * self.gper + n)
                act.wait_ge(sq_used.sem, i * self.per + self.base + (g + 1) * self.chunks)
                act.activation(log_ms, self.bank[:], ACT.Ln, bias=eps, scale=1.0 / self.size).then_inc(log_ready.sem, 1)
                act.wait_ge(log_ready.sem, i * self.gper + n + 1)
                if users is not None:
                    act.wait_ge(*users)
                act.activation(rstd, log_ms, ACT.Exp, scale=-0.5).then_inc(rstd_ready.sem, 1)

            def ready(self, g=0, i=0):
                return rstd_ready.sem, i * self.gper + self.gbase + g + 1

        class AddedNorm(Norm):

            def __init__(self, chunks, total):
                super().__init__(chunks)
                self.total = total

            def square(self, act, src, c):
                n = len(sq)
                if self.base > 0 and c == 0:
                    act.wait_ge(sq_used.sem, self.base)
                if c > n:
                    act.wait_ge(sq_used.sem, self.base + c - n)
                act.activation(sq[c % n] if c else self.total, src, ACT.Square).then_inc(sq_ready.sem, 1)

            def add(self, dve, c):
                dve.wait_ge(sq_ready.sem, self.base + c + 1)
                if c >= 2:
                    dve.wait_ge(sq_used.sem, self.base + c - 1)
                dve.tensor_tensor(self.total, self.total, sq[c % len(sq)], ALU.add).then_inc(sq_used.sem, 1)

            def sum(self, pe):
                if self.gbase > 0:
                    pe.wait_ge(log_ready.sem, self.gbase)
                pe.wait_ge(sq_used.sem, self.base + self.chunks - 1)
                pe.matmul(self.bank[:], ones[:], self.total, start=True, stop=True).then_inc(sq_used.sem, 1)

        class Split:

            def __init__(self, per, turns=1):
                self.whole, self.high, self.low = (shared(f"split_{k}", per, turns) for k in ("whole", "hi", "lo"))

            def free(self, dve, c, i=0):
                sem, value = self.low.at(c - 2 if c >= 2 else -1, i)
                if not isinstance(value, int) or value > 0:
                    dve.wait_ge(sem, value)

            def round(self, act, dst, c, i=0):
                act.wait_ge(*self.whole.at(c, i))
                act.copy(dst, tmp[c % 2]).then_inc(self.high.sem, 1)

            def rest(self, dve, dst, hi, c, i=0):
                dve.wait_ge(*self.high.at(c, i))
                dve.tensor_tensor(dst, tmp[c % 2], hi.bitcast(F32), ALU.subtract).then_inc(self.low.sem, 1)

        def open_unit(pe, st, j, i):
            pe.wait_ge(lo_split, st.done(j, i))
            if st.base + j >= RING:
                pe.wait_ge(bank_free[st.bank(j)], st.uses(j, i))

        def unit_chunk(pe, st, j, k, kc, hi, lo, k0=0):
            r = st.bank(j)
            w = slice(k * P, k * P + P)
            xh, xl = tile(hi, k0 + k), tile(lo, k0 + k)
            pe.matmul(psum[r][:], w_hi[r][:, w], xh, start=k == 0, stop=False)
            pe.matmul(psum[r][:], w_hi[r][:, w], xl, start=False, stop=False)
            last = pe.matmul(psum[r][:], w_lo[r][:, w], xh, start=False, stop=k == kc - 1)
            if k == kc - 1:
                last.then_inc(unit_done, 1)

        def unit(pe, st, j, kc, hi, lo, i=0, k0=0, ready=None):
            open_unit(pe, st, j, i)
            for k in range(kc):
                if ready:
                    pe.wait_ge(*ready(k))
                unit_chunk(pe, st, j, k, kc, hi, lo, k0)

        def unit_pair(pe, st, j, kc, hi, lo, i, ready):
            for u in (j, j + 1):
                open_unit(pe, st, u, i)
                for k in range(kc - 1):
                    if u == j:
                        pe.wait_ge(*ready(k))
                    unit_chunk(pe, st, u, k, kc, hi, lo)
            pe.wait_ge(*ready(kc - 1))
            for u in (j, j + 1):
                unit_chunk(pe, st, u, kc - 1, kc, hi, lo)

        def arrived(eng, st, j, i=0):
            eng.wait_ge(unit_done, st.done(j, i))
            return psum[st.bank(j)]

        def taken(st, j):
            return bank_free[st.bank(j)], 1

        def emptied(eng, st, j, i=0):
            eng.wait_ge(bank_free[st.bank(j)], st.uses(j, i) + 1)

        class PreNorm:

            def __init__(self, gain_name, gain_at):
                self.norm = Norm(DC)
                self.split = Split(DC)
                self.gain = (gain_name, gain_at)

            def act(self, act, h_at):
                for c in range(DC):
                    act.wait_ge(*h_at(c))
                    self.norm.square(act, tile(hT, c), c)
                self.norm.root(act)
                for c in range(DC):
                    self.split.round(act, tile(a_hi, c), c)

            def pe(self, pe):
                for c in range(DC):
                    self.norm.sum(pe, c)

            def dve(self, dve):
                dve.wait_ge(*self.norm.ready())
                for c in range(DC + 1):
                    if c < DC:
                        self.split.free(dve, c)
                        dve.scalar_tensor_tensor(tmp[c % 2], tile(hT, c), gain(self.gain[0], self.gain[1] + c), rstd,
                                                 ALU.mult, ALU.mult).then_inc(self.split.whole.sem, 1)
                    if c >= 1:
                        self.split.rest(dve, tile(a_lo, c - 1), tile(a_hi, c - 1), c - 1)

            def ready(self, k):
                return self.split.low.at(k)

        class LateNorm:

            def __init__(self, gain_name, gain_at, total):
                self.norm = AddedNorm(DC, total)
                self.high, self.low = shared("late_hi", DC), shared("late_lo", DC)
                self.gain = (gain_name, gain_at)

            def column(self, c):
                return gain(self.gain[0], self.gain[1] + c)

            def act(self, act, h_at):
                for c in range(DC):
                    act.wait_ge(*h_at(c))
                    act.activation(tile(a_hi, c), tile(hT, c), ACT.Identity, bias=zero,
                                   scale=self.column(c)).then_inc(self.high.sem, 1)
                for c in range(DC):
                    self.norm.square(act, tile(hT, c), c)
                self.norm.root(act)

            def rest(self, dve, c):
                dve.wait_ge(*self.high.at(c))
                dve.scalar_tensor_tensor(tile(a_lo, c), tile(hT, c), self.column(c), tile(a_hi, c).bitcast(F32),
                                         ALU.mult, ALU.subtract).then_inc(self.low.sem, 1)

            def adds(self, dve):
                for c in range(1, DC):
                    self.norm.add(dve, c)
                dve.wait_ge(*self.norm.ready())

        class PostNorm:

            def __init__(self, gain_at, total):
                self.norm = AddedNorm(DC, total)
                self.scaled, self.added = shared("post_scaled", DC), shared("post_added", DC)
                self.gain_at = gain_at

            def dve(self, dve, then=None):
                dve.wait_ge(*self.norm.ready())
                for c in range(DC + 2):
                    if c < DC:
                        if c >= 2:
                            dve.wait_ge(*self.added.at(c - 2))
                        dve.scalar_tensor_tensor(tmp[c % 2], tile(acc, c), gain("norm", self.gain_at + c), rstd,
                                                 ALU.mult, ALU.mult).then_inc(self.scaled.sem, 1)
                    if 1 <= c <= DC:
                        dve.wait_ge(*self.scaled.at(c - 1))
                        dve.tensor_tensor(tile(hT, c - 1), tile(hT, c - 1), tmp[(c - 1) % 2],
                                          ALU.add).then_inc(self.added.sem, 1)
                    if c >= 2 and then:
                        then.rest(dve, c - 2)

        class Attention:

            def __init__(self, heads, turns, scale, pr, pt, row_scale=None):
                self.heads, self.scale, self.pr, self.pt, self.row_scale = heads, scale, pr, pt, row_scale
                self.n = n = heads * TB
                s = lambda k: shared(f"attn_{k}", n, turns)
                self.scores, self.masked, self.exped, self.inverted, self.normed, self.turned, self.turned_out = (
                    s(k) for k in ("scores", "masked", "exped", "inverted", "normed", "turned", "turned_out"))
                self.biased = s("biased") if row_scale else self.masked
                self.out = shared("attn_out", heads, turns)
                self.out_hi = shared("attn_out_hi", heads, turns)
                self.out_lo = shared("attn_out_lo", heads, turns)
                self.s_bank = [aux[0], aux[1], psum[2]]
                self.t_bank, self.o_bank = [aux[2], psum[0]], [aux[3], psum[1]]

            def keys(self, t):
                return (t % TB + 1) * P

            def pe(self, pe, i, score, values):
                for s in range(self.n + 3):
                    if s < self.n:
                        score(s, self.s_bank[s % 3], self.keys(s)).then_inc(self.scores.sem, 1)
                    t = s - 2
                    if 0 <= t < self.n:
                        pe.wait_ge(*self.normed.at(t, i))
                        for kb in range(t % TB + 1):
                            k = slice(kb * P, kb * P + P)
                            last = pe.transpose(self.t_bank[t % 2][:, k], self.pr[t % 3][:, k], ident[:])
                        last.then_inc(self.turned.sem, 1)
                    t = s - 3
                    if t >= 0:
                        hh, b = t // TB, t % TB
                        if b == 0 and hh >= 2:
                            pe.wait_ge(*self.out_lo.at(hh - 2, i))
                        pe.wait_ge(*self.turned_out.at(t, i))
                        for kb in range(b + 1):
                            last = pe.matmul(self.o_bank[hh % 2][:, b * P:b * P + P], values(hh, kb),
                                             self.pt[t % 2][:, kb * P:kb * P + P], start=kb == 0, stop=kb == b)
                        if b == TB - 1:
                            last.then_inc(self.out.sem, 1)
                pe.wait_ge(*self.out_lo.at(self.heads - 1, i))

            def dve(self, dve, i, bias, out_lo, out_hi):
                for s in range(self.n + 5):
                    if s < self.n:
                        w, r = self.keys(s), slice(s % 3, s % 3 + 1)
                        dve.wait_ge(*self.scores.at(s, i))
                        plain_wait(dve, s % 3)
                        dve.tensor_tensor_reduce(self.pr[s % 3][:, 0:w], self.s_bank[s % 3][:, 0:w], bias(s), -self.scale,
                                                 -GONE, ALU.add, ALU.min, row_min[:, r]).then_inc(self.masked.sem, 1)
                        if self.row_scale:
                            dve.wait_ge(*self.masked.at(s, i))
                            dve.tensor_scalar(row_bias[:, r], row_min[:, r], self.row_scale(s)[0], None,
                                              ALU.mult).then_inc(self.biased.sem, 1)
                    t = s - 1
                    if 0 <= t < self.n:
                        w, r = self.keys(t), slice(t % 3, t % 3 + 1)
                        dve.wait_ge(*self.exped.at(t, i))
                        dve.reciprocal(row_inv[:, r], row_sum[:, r]).then_inc(self.inverted.sem, 1)
                        dve.wait_ge(*self.inverted.at(t, i))
                        dve.tensor_scalar(self.pr[t % 3][:, 0:w], self.pr[t % 3][:, 0:w], row_inv[:, r], None,
                                          ALU.mult).then_inc(self.normed.sem, 1)
                    hh = (s - 5) // TB
                    if s >= 5 and s - 5 == hh * TB + TB - 1:
                        dve.wait_ge(*self.out_hi.at(hh, i))
                        dve.tensor_tensor(out_lo(hh), self.o_bank[hh % 2][:], out_hi(hh).bitcast(F32),
                                          ALU.subtract).then_inc(self.out_lo.sem, 1)

            def act(self, act, i, out_hi):
                for s in range(self.n + 4):
                    if s < self.n:
                        w, r = self.keys(s), slice(s % 3, s % 3 + 1)
                        act.wait_ge(*self.biased.at(s, i))
                        act.activation(self.pr[s % 3][:, 0:w], self.pr[s % 3][:, 0:w], ACT.Exp,
                                       bias=(row_bias if self.row_scale else row_min)[:, r],
                                       scale=self.row_scale(s)[1] if self.row_scale else -1.0,
                                       accum_out=row_sum[:, r]).then_inc(self.exped.sem, 1)
                    t = s - 2
                    if 0 <= t < self.n:
                        w = self.keys(t)
                        act.wait_ge(*self.turned.at(t, i))
                        act.copy(self.pt[t % 2][:, 0:w], self.t_bank[t % 2][:, 0:w]).then_inc(self.turned_out.sem, 1)
                    hh = (s - 4) // TB
                    if s >= 4 and s - 4 == hh * TB + TB - 1:
                        act.wait_ge(*self.out.at(hh, i))
                        act.copy(out_hi(hh), self.o_bank[hh % 2][:]).then_inc(self.out_hi.sem, 1)

        def causal(table, b):
            return tab[table][:, (TB - 1 - b) * P:T]


        def turn_block(pe, bank, src):
            for b in range(TB):
                last = pe.transpose(bank[:, b * P:b * P + P], src[:, b * P:b * P + P], ident[:])
            return last

        pre_mla = PreNorm("norm", 0)
        mla_c = [tile(F, 6 + c) for c in range(6)]
        k_rope, rope_cos, rope_sin = tile(F, 12), tile(F, 13), tile(F, 14)
        pos_i, pos_f, angle, cycles, reduced = (tile(F, 15 + k) for k in range(5))
        n_cq, n_ckv = Norm(MLA_Q // P), Norm(MLA_KV // P)
        s_c = Split(6)
        angle_ready, sin_ready = signal("angle_ready"), signal("sin_ready")
        rope_part, k_rope_ready = signal("rope_part"), signal("k_rope_ready")
        qn, q_rope, kn = [tile(F, 6 + k) for k in range(4)], [tile(F, 10), tile(F, 11)], [tile(F, 15 + k) for k in range(4)]
        vT, vtok = [tile(F, 19), tile(acc, 7)], [tile(acc, k) for k in range(4)]
        q_rope_ready = signal("q_rope_ready", 2)
        v_turned, v_ready = signal("v_turned", MLA_TURN), signal("v_ready", MLA_TURN)
        V_AFTER = {6: 0, 8: 1, 14: 2, 15: 3}
        at_mla = Attention(MLA_TURN, MLA_HEADS // MLA_TURN, MLA_SCALE, [tile(acc, 4 + k) for k in range(3)], sq)
        post_mla = PostNorm(8, tile(F, 6))

        class Mlp:

            def __init__(self, l):
                self.l, self.st = l, st_mlp[l]
                self.pre = LateNorm("norm", 32 * l + 16, tile(F, 8))
                self.split = Split(DC, self.st.turns)
                self.cleared = shared("mlp_cleared")
                self.post = PostNorm(32 * l + 24, tile(F, 9))
                self.relu = [tile(F, 6), tile(F, 7)]

            def pe(self, pe):
                def block(i, first):
                    for j in range(DC):
                        unit(pe, self.st, j, DC, a_hi, a_lo, i, ready=self.pre.low.at if first and j == 0 else None)
                        if first and j == 1:
                            self.pre.norm.sum(pe)
                    for m in range(DC):
                        unit(pe, self.st, DC + m, DC, g_hi, g_lo, i,
                             ready=(lambda k: self.split.low.at(k, i)) if m == 0 else None)
                turns_from(pe, self.st.turns, block)
                self.post.norm.sum(pe)

            def act(self, act, h_at):
                self.pre.act(act, h_at)

                def block(i):
                    for j in range(DC):
                        self.split.round(act, tile(g_hi, j), j, i)
                turns(act, self.st.turns, block)
                for c in range(DC):
                    emptied(act, self.st, DC + c, self.st.turns - 1)
                    self.post.norm.square(act, tile(acc, c), c)
                self.post.norm.root(act)

            def dve(self, dve, then=None):
                dve.memset(acc[:], 0.0).then_inc(self.cleared.sem, 1)
                dve.wait_ge(*self.cleared.at(0))
                self.pre.adds(dve)

                def block(i, last):
                    for j in range(DC + 1):
                        if j < DC:
                            bank = arrived(dve, self.st, j, i)
                            dve.scalar_tensor_tensor(self.relu[j % 2], bank[:], 0.0, rstd, ALU.max,
                                                     ALU.mult).then_inc(*taken(self.st, j))
                            emptied(dve, self.st, j, i)
                            self.split.free(dve, j, i)
                            dve.tensor_tensor(tmp[j % 2], self.relu[j % 2], self.relu[j % 2],
                                              ALU.mult).then_inc(self.split.whole.sem, 1)
                        if j >= 1:
                            self.split.rest(dve, tile(g_lo, j - 1), tile(g_hi, j - 1), j - 1, i)
                    for m in range(DC):
                        bank = arrived(dve, self.st, DC + m, i)
                        dve.tensor_tensor(tile(acc, m), bank[:], tile(acc, m), ALU.add).then_inc(*taken(self.st, DC + m))
                        if last and m >= 2:
                            self.post.norm.add(dve, m - 1)
                with dve.Fori(0, self.st.turns - 1) as i:
                    block(i, False)
                block(self.st.turns - 1, True)
                self.post.norm.add(dve, DC - 1)
                self.post.dve(dve, then)

        class OutProj:

            def __init__(self, st, hi, lo, post):
                self.st, self.hi, self.lo, self.post = st, hi, lo, post

            def pe(self, pe, ready):
                for m in range(DC):
                    unit(pe, self.st, m, DC, self.hi, self.lo, ready=ready if m == 0 else None)
                self.post.norm.sum(pe)

            def act(self, act):
                for m in range(DC):
                    bank = arrived(act, self.st, m)
                    self.post.norm.square(act, bank[:], m)
                    act.copy(tile(acc, m), bank[:]).then_inc(*taken(self.st, m))
                self.post.norm.root(act)

            def dve(self, dve, then):
                for m in range(1, DC):
                    self.post.norm.add(dve, m)
                emptied(dve, self.st, DC - 1)
                self.post.dve(dve, then)

        out_mla = OutProj(st_mla_o, a_hi, a_lo, post_mla)
        mlp = [Mlp(0)]

        pre_hg = PreNorm("norm", 32)
        hg_sig, hg_q, hg_k, hg_f, hg_b, hg_logf = (tile(F, k) for k in (7, 9, 10, 11, 12, 13))
        hg_d, hg_d2 = tile(F, 11), tile(F, 8)
        hg_vT = tile(F, 14)
        hg_e = [tile(F, 15 + k) for k in range(4)]
        hg_qdec = tile(F, 19)
        hg_qrel, hg_krel, hg_dec, hg_kdec = hg_e
        hg_state, hg_v, hg_kT, hg_a, hg_gate = tile(acc, 0, 4 * T), tile(acc, 4), tile(acc, 5), tile(acc, 6), tile(acc, 7)
        hg_f_ready, hg_k_ready, hg_logf_ready, hg_b_ready, hg_d_ready, hg_d2_ready = (
            signal(f"hg_{n}_ready") for n in ("f", "k", "logf", "b", "d", "d2"))
        hg_e_ready = signal("hg_e_ready", 4)
        hg_rel_ready, hg_dec_ready = signal("hg_rel_ready", 2), signal("hg_dec_ready", 2)
        hg_cleared = signal("hg_cleared")
        hg_scores, hg_masked = signal("hg_scores"), signal("hg_masked")
        hg_v_turned, hg_v_ready, hg_k_turned, hg_kT_ready = (
            signal(f"hg_{n}") for n in ("v_turned", "v_ready", "k_turned", "kT_ready"))
        hg_u, hg_state_ready = signal("hg_u"), signal("hg_state_ready", HG_N - 1)
        hg_o, hg_y = signal("hg_o"), signal("hg_y", credit=1)
        n_hg = Norm(1, turns=HG_HEADS, bank=aux[1])
        s_hg = Split(1, HG_HEADS)
        post_hg = PostNorm(40, tile(F, 6))
        out_hg = OutProj(st_hg_o, g_hi, g_lo, post_hg)
        mlp.append(Mlp(1))

        pre_dsa = PreNorm("mix", 0)
        idx_q, idx_k = [tile(F, 6 + c) for c in range(4)], tile(F, 10)
        dsa_cT, dsa_kT, dsa_c = tile(F, 11), tile(F, 12), tile(F, 13)
        dsa_bias = [tile(F, 14 + b) for b in range(TB)]
        idx_rel = [tile(F, 18), tile(F, 19)]
        wiT = tile(F, 19)
        dsa_q = tile(F, 18)
        NG = 6
        n_idx = Norm(1, groups=5, matrix=ones_half, size=IDX_DIM)
        n_key = Norm(1)
        idx_ready, key_ready = signal("idx_ready"), signal("key_ready")
        c_turned, c_ready = signal("c_turned"), signal("c_ready")
        wi_turned, wi_ready, wiT_ready = signal("wi_turned"), signal("wi_ready"), signal("wiT_ready")
        rel_ready, rel_taken, scored = signal("rel_ready"), signal("rel_taken"), signal("scored")
        dsa_bias_ready = signal("dsa_bias_ready")
        n_dq = Norm(DSA_HEADS, size=DSA_LAT, bank=aux[2])
        DSA_TURN = 4
        dsa_q = [tile(F, 6 + k) for k in range(DSA_TURN)]
        dsa_q_ready = signal("dsa_q_ready", DSA_TURN)
        q_rstd_turn = signal("q_rstd_turn", 2)
        at_dsa = Attention(DSA_TURN, DSA_HEADS // DSA_TURN, DSA_SCALE, [tile(F, 10), tile(F, 18), tile(F, 19)], sq,
                           lambda t: (q_rstd[:, t:t + 1], q_rstd_neg[:, t:t + 1]))
        REL = [(b, h) for b in range(1, TB) for h in range(IDX_HEADS)]
        Q0 = 7
        Q_AFTER = [range(0, 3), range(3, 6), range(6, 8)]

        class Ffn:

            def __init__(self, l):
                self.l = l
                self.pre = LateNorm("ffn", DC * l, tile(F, 14))
                self.u = [[tile(F, 6 + 2 * s + r) for r in range(2)] for s in range(2)]
                self.x = [[tile(F, 10 + 2 * s + r) for r in range(2)] for s in range(2)]
                self.parts = []
                for k, (st, first, size) in enumerate(st_ffn[l]):
                    self.parts.append((st, first, size, Split(size, st.turns), shared("ffn_tap2", 2 * size, st.turns),
                                       shared("ffn_tap1", 2 * size, st.turns), shared("ffn_tap0", 2 * size, st.turns),
                                       shared("ffn_silu", size, st.turns)))
                self.last = st_ffn[l][-1]

            def h_at(self, c):
                st, _, size = self.last
                return bank_free[st.bank(2 * size + c)], st.uses(2 * size + c) + 1

            def pe(self, pe):
                for st, first, size, split, *_ in self.parts:
                    def block(i, start):
                        start = start and first == 0
                        for j in range(2 * size):
                            unit(pe, st, j, DC, a_hi, a_lo, i, ready=self.pre.low.at if start and j == 0 else None)
                            if start and j == 1:
                                self.pre.norm.sum(pe)
                        unit_pair(pe, st, 2 * size, size, g_hi, g_lo, i, lambda c: split.low.at(c, i))
                        for m in range(2, DC):
                            unit(pe, st, 2 * size + m, size, g_hi, g_lo, i)
                    turns_from(pe, st.turns, block)

            def act(self, act, h_at):
                self.pre.act(act, h_at)
                l = self.l
                for st, first, size, split, tap2, tap1, tap0, silu in self.parts:
                    def block(i):
                        for j in range(size + 2):
                            if j >= 2:
                                split.round(act, tile(g_hi, j - 2), j - 2, i)
                            if j < size:
                                for s in range(2):
                                    c = i * DC + first + j + s * FF2C
                                    emptied(act, st, 2 * j + s, i)
                                    act.activation(self.u[s][j % 2], self.x[s][j % 2], ACT.Identity, bias=conv_col(l, 3, c),
                                                   scale=conv_col(l, 2, c)).then_inc(tap2.sem, 1)
                            if 1 <= j <= size:
                                act.wait_ge(*tap0.at(2 * (j - 1), i))
                                u = self.u[0][(j - 1) % 2]
                                act.activation(u, u, ACT.Silu).then_inc(silu.sem, 1)
                    turns(act, st.turns, block)

            def dve(self, dve):
                for c in range(DC):
                    self.pre.rest(dve, c)
                self.pre.adds(dve)
                l = self.l
                for st, first, size, split, tap2, tap1, tap0, silu in self.parts:
                    def block(i):
                        for j in range(size + 2):
                            if j < size:
                                for s in range(2):
                                    bank = arrived(dve, st, 2 * j + s, i)
                                    dve.tensor_tensor(self.x[s][j % 2], bank[:], rstd, ALU.mult).then_inc(*taken(st, 2 * j + s))
                            if 1 <= j <= size:
                                dve.wait_ge(*silu.at(j - 1, i))
                                dve.wait_ge(*tap0.at(2 * (j - 1) + 1, i))
                                split.free(dve, j - 1, i)
                                dve.tensor_tensor(tmp[(j - 1) % 2], self.u[0][(j - 1) % 2], self.u[1][(j - 1) % 2],
                                                  ALU.mult).then_inc(split.whole.sem, 1)
                            if j >= 2:
                                split.rest(dve, tile(g_lo, j - 2), tile(g_hi, j - 2), j - 2, i)
                            if j < size:
                                for k in (1, 0):
                                    for s in range(2):
                                        c = i * DC + first + j + s * FF2C
                                        u, back = self.u[s][j % 2], 2 - k
                                        dve.wait_ge(*(tap1 if k == 0 else tap2).at(2 * j + s, i))
                                        dve.scalar_tensor_tensor(
                                            u[:, back:T], self.x[s][j % 2][:, 0:T - back], conv_col(l, k, c),
                                            u[:, back:T], ALU.mult, ALU.add).then_inc((tap1 if k else tap0).sem, 1)
                        for m in range(DC):
                            bank = arrived(dve, st, 2 * size + m, i)
                            dve.tensor_tensor(tile(hT, m), bank[:], tile(hT, m),
                                              ALU.add).then_inc(*taken(st, 2 * size + m))
                    turns(dve, st.turns, block)

        ffn = [Ffn(0)]

        pre_ret = LateNorm("mix", DC, tile(F, 14))
        ret_factor = tab["scan_keep"]
        ret_factors = signal("ret_factors", 3)
        ret_q, ret_k = [tile(F, 6), tile(F, 7)], [tile(F, 8), tile(F, 9)]
        ret_vtok = F[:, 10 * T:14 * T]
        ret_gate = [tile(F, 14 + m) for m in range(4)]
        ret_vT = [tile(F, 18), tile(F, 19)]
        ret_s = [tile(acc, j) for j in range(TB)]
        ret_raw = [tile(acc, 4 + m) for m in range(4)]
        RV = RET_DV // P
        ret_part, ret_qk_ready = signal("ret_part", 4), signal("ret_qk_ready", 4)
        ret_v_turned, ret_v_ready = signal("ret_v_turned", RV), signal("ret_v_ready", RV)
        ret_scores, ret_s_ready = signal("ret_scores", TB), signal("ret_s_ready", TB)
        ret_o, ret_raw_ready, ret_y = signal("ret_o", RV), signal("ret_raw_ready", RV, credit=1), signal("ret_y", RV)
        n_ret = Norm(RV, turns=RET_HEADS, size=RET_DV)
        s_ret = Split(RV, RET_HEADS)
        ffn.append(Ffn(1))

        out_turned, out_ready = signal("out_turned"), signal("out_ready")

        block = ctx.enter_context(nc.Block())

        @block.sync
        def _(sp):
            for st in stages:
                def load(i):
                    for q, s in enumerate(st.slabs):
                        if st.slab_base + q >= 2:
                            sp.wait_ge(lo_split, st.raw_free(q, i))
                        v = raw_view(st.slot(q), s)
                        for c, n, src in s.parts(i):
                            sp.dma_start(v[:, :, c:c + n], src).then_inc(loaded[st.slot(q)], 16)
                turns(sp, st.turns, load)
            for b in range(TB):
                sp.wait_ge(*out_ready.at(2 * b + 1))
                sp.dma_start(out.rearrange("a t d -> (a t) d")[b * P:b * P + P, :], acc[:, b * D:b * D + D]).then_inc(stored, 16)
            sp.wait_ge(stored, 16 * TB)

        @block.gpsimd
        def _(pool):
            pool.wait_ge(tables_in, 16 * (len(TABLE_WIDTH) + 1))
            for st in stages:
                def split(i):
                    for q, s in enumerate(st.slabs):
                        pool.wait_ge(loaded[st.slot(q)], st.loaded(q, i))
                        v = raw_view(st.slot(q), s)
                        for m in range(s.units):
                            j = st.first[q] + m
                            r = st.bank(j)
                            if st.base + j >= RING:
                                pool.wait_ge(unit_done, st.done(j - RING, i))
                            src = v[:, :, m * P:m * P + P]
                            hi = w_hi[r][:, 0:s.kc * P].rearrange("p (k n) -> p k n", k=s.kc)
                            lo = w_lo[r][:, 0:s.kc * P].rearrange("p (k n) -> p k n", k=s.kc)
                            pool.tensor_tensor(hi, src, zero.rearrange("p (a b) -> p a b", a=1).to_broadcast([P, s.kc, P]),
                                               ALU.subtract).then_inc(hi_split, 1)
                            pool.wait_ge(hi_split, st.done(j, i))
                            pool.tensor_tensor(lo, src, hi.bitcast(F32), ALU.subtract).then_inc(lo_split, 1)
                turns(pool, st.turns, split)

        @block.scalar
        def _(act):
            act.dma_start(acc[:].rearrange("p (t d) -> p t d", t=TB),
                          x.rearrange("a (t p) d -> p (a t) d", p=P)).then_inc(x_in, 16)
            for k in TABLE_WIDTH:
                dst = {"ret_cos": ret_cos, "ret_sin": ret_sin, "ret_decay": ret_decay}.get(k) or tab[k]
                act.dma_start(dst[:], tables[k]).then_inc(tables_in, 16)
            act.dma_start(hg_mask[:], hg_mask_dram).then_inc(tables_in, 16)
            act.dma_start(pos_i.bitcast(I32), positions.partition_broadcast(P)).then_inc(pos_in, 16)
            for dst, src in row_loads:
                act.dma_start(dst, src).then_inc(rows_in, 16)
            act.wait_ge(tables_in, 16 * (len(TABLE_WIDTH) + 1))

            for k, dst in enumerate((rope_sin, rope_cos)):
                act.wait_ge(*angle_ready.at(k))
                act.activation(dst, reduced, ACT.Sin).then_inc(sin_ready.sem, 1)
            act.wait_ge(*setup_lb_diff)
            act.activation(lb[:, DC:3 * DC], lb[:, DC:3 * DC], ACT.Exp).then_inc(lb_exp.sem, 1)

            pre_mla.act(act, lambda c: h_ready.at(c))

            def take_c(j):
                bank = arrived(act, st_mla_in, j)
                n, c = (n_cq, j) if j < 4 else (n_ckv, j - 4)
                n.square(act, bank[:], c)
                act.copy(mla_c[j], bank[:]).then_inc(*taken(st_mla_in, j))
            for j in range(5):
                take_c(j)
            n_cq.root(act)
            take_c(5)
            for c in range(4):
                s_c.round(act, tile(g_hi, c), c)
            n_ckv.root(act)
            for c in range(4, 6):
                s_c.round(act, tile(g_hi, c), c)

            def mla_heads(i):
                for a in range(2):
                    for j, dst in ((0, qn[2 * a]), (1, qn[2 * a + 1]), (4, kn[2 * a]), (5, vT[0]), (6, kn[2 * a + 1]), (7, vT[1])):
                        j += 8 * a
                        bank = arrived(act, st_mla, j, i)
                        act.copy(dst, bank[:]).then_inc(*taken(st_mla, j))
                        if j in V_AFTER:
                            hh = V_AFTER[j]
                            act.wait_ge(*v_turned.at(hh, i))
                            act.copy(vtok[hh], aux[2 + hh % 2][:]).then_inc(v_ready.sem, 1)
                at_mla.act(act, i, lambda hh: tile(a_hi, i * MLA_TURN + hh))
            turns(act, st_mla.turns, mla_heads)
            out_mla.act(act)
            mlp[0].act(act, post_mla.added.at)

            pre_hg.act(act, mlp[0].post.added.at)

            def hg_evacuate(i, js):
                for j in js:
                    dst, f = ((hg_q, ACT.Silu), (hg_sig, ACT.Sigmoid), (hg_vT, ACT.Copy), (hg_gate, ACT.Silu))[j]
                    bank = arrived(act, st_hg, j, i)
                    act.activation(dst, bank[:], f).then_inc(*taken(st_hg, j))

            def hg_gates(i):
                act.wait_ge(*hg_f_ready.at(0, i))
                act.activation(hg_logf, hg_f, ACT.Ln).then_inc(hg_logf_ready.sem, 1)
                act.wait_ge(*hg_d_ready.at(0, i))
                act.activation(hg_e[0], hg_d, ACT.Exp).then_inc(hg_e_ready.sem, 1)
                act.activation(hg_e[1], hg_d, ACT.Exp, scale=-1.0).then_inc(hg_e_ready.sem, 1)
                act.activation(hg_e[2], hg_b, ACT.Exp).then_inc(hg_e_ready.sem, 1)
                act.wait_ge(*hg_d2_ready.at(0, i))
                act.activation(hg_e[3], hg_d2, ACT.Exp).then_inc(hg_e_ready.sem, 1)

            def hg_turned(i):
                act.wait_ge(*hg_v_turned.at(0, i))
                act.copy(hg_v, aux[1][:]).then_inc(hg_v_ready.sem, 1)
                act.wait_ge(*hg_k_turned.at(0, i))
                act.copy(hg_kT, aux[1][:]).then_inc(hg_kT_ready.sem, 1)

            def hg_normed(i):
                act.wait_ge(*hg_o.at(0, i))
                n_hg.square(act, aux[0][:], 0, 0, i)
                n_hg.root(act, 0, i)
                s_hg.round(act, tile(g_hi, i), 0, i)
            hg_evacuate(0, (0, 1, 2))
            hg_gates(0)
            hg_evacuate(0, (3,))
            with act.Fori(0, HG_HEADS - 1) as i:
                hg_turned(i)
                hg_evacuate(i + 1, (0, 1, 2))
                hg_gates(i + 1)
                hg_normed(i)
                hg_evacuate(i + 1, (3,))
            hg_turned(HG_HEADS - 1)
            hg_normed(HG_HEADS - 1)
            out_hg.act(act)
            mlp[1].act(act, post_hg.added.at)

            pre_dsa.act(act, mlp[1].post.added.at)

            def root_of(g):
                if g < 5:
                    n_idx.root(act, g, users=idx_ready.at(g - 1) if g else None)
                else:
                    n_key.root(act, users=idx_ready.at(4))
            for g in range(NG):
                bank = arrived(act, st_dsa, g)
                n, k = (n_idx, g) if g < 5 else (n_key, 0)
                n.square(act, bank[:], 0, k)
                act.copy((idx_q + [idx_k, dsa_cT])[g], bank[:]).then_inc(*taken(st_dsa, g))
                if g:
                    root_of(g - 1)
            root_of(NG - 1)
            bank = arrived(act, st_dsa, NG)
            act.mul(wiT[0:IDX_HEADS, :], bank[0:IDX_HEADS, :], IDX_SCALE).then_inc(*taken(st_dsa, NG))
            act.wait_ge(*c_turned.at(0))
            act.copy(dsa_c, aux[2][:]).then_inc(c_ready.sem, 1)
            act.wait_ge(*wi_turned.at(0))
            act.copy(wi_tok[:], aux[3][:, 0:TB * IDX_HEADS]).then_inc(wi_ready.sem, 1)
            for r, (b, h) in enumerate(REL):
                w = (b + 1) * P
                act.wait_ge(*rel_ready.at(r))
                if r >= 2:
                    act.wait_ge(*scored.at(r - 2))
                act.activation(idx_rel[r % 2][:, 0:w], aux[r % 2][:, 0:w], ACT.Relu).then_inc(rel_taken.sem, 1)
                if h == IDX_HEADS - 1:
                    for q in Q_AFTER[b - 1]:
                        bank = arrived(act, st_dsa, Q0 + q)
                        n_dq.square(act, bank[:], q)
                        act.copy(tile(acc, q), bank[:]).then_inc(*taken(st_dsa, Q0 + q))
            n_dq.root_tokens(act, q_log[:], q_rstds[:])
            emptied(act, st_dsa, Q0 + DSA_HEADS - 1)

            def dsa_heads(i):
                for hh in range(DSA_TURN):
                    act.copy(dsa_q[hh], tile(acc, i * DSA_TURN + hh)).then_inc(dsa_q_ready.sem, 1)
                at_dsa.act(act, i, lambda hh: tile(g_hi, i * DSA_TURN + hh))
            turns(act, DSA_HEADS // DSA_TURN, dsa_heads)
            ffn[0].act(act, lambda c: (bank_free[st_dsa_o.bank(c)], st_dsa_o.uses(c) + 1))

            pre_ret.act(act, ffn[0].h_at)

            def ret_head(st, i, h):
                for m in range(RV):
                    act.wait_ge(*ret_v_turned.at(m, h))
                    act.copy(ret_vtok.rearrange("p (b e) -> p b e", b=TB)[:, :, m * P:(m + 1) * P],
                             aux[2 + m % 2][:].rearrange("p (b e) -> p b e", b=TB)).then_inc(ret_v_ready.sem, 1)
                for m in range(RV):
                    emptied(act, st, 4 + m, i)
                    act.activation(ret_gate[m], ret_gate[m], ACT.Silu)
                for m in range(RV):
                    act.wait_ge(*ret_o.at(m, h))
                    n_ret.square(act, aux[2 + m % 2][:], m, 0, h)
                    act.copy(ret_raw[m], aux[2 + m % 2][:]).then_inc(ret_raw_ready.sem, 1)
                n_ret.root(act, 0, h)
                for m in range(RV):
                    s_ret.round(act, tile(g_hi, m), m, h)
            with act.Fori(0, RET_HEADS - 1) as i:
                ret_head(st_ret, i, i)
            ret_head(st_ret_end, 0, RET_HEADS - 1)
            ffn[1].act(act, lambda c: (bank_free[st_ret_end.bank(8 + c)], st_ret_end.uses(8 + c) + 1))

        @block.vector
        def _(dve):
            count = 0

            def step(ins):
                nonlocal count
                count += 1
                ins.then_inc(setup.sem, 1)
                dve.wait_ge(setup.sem, count)

            dve.sem_inc(hg_y.sem, 1)
            dve.sem_inc(ret_raw_ready.sem, 1)
            for c in range(DC):
                dve.wait_ge(*x_turned.at(c))
                dve.tensor_copy(tile(hT, c), aux[c % 2][:]).then_inc(h_ready.sem, 1)
            for k, (rows_t, n, c0) in enumerate(row_tiles):
                dve.wait_ge(*turned.at(k))
                dve.tensor_copy(cols[:, c0:c0 + n], aux[2 + k % 2][:, 0:n]).then_inc(turned_out.sem, 1)
            dve.wait_ge(*turned_out.at(5))
            dve.wait_ge(pos_in, 16)
            step(dve.tensor_copy(pos_f, pos_i.bitcast(I32)))
            step(dve.tensor_scalar(angle, pos_f, inv_freq, None, ALU.mult))
            for k, quarter in enumerate((0.0, 0.25)):
                step(dve.tensor_scalar(cycles, angle, 1.0 / (2 * np.pi), quarter, ALU.mult, ALU.add))
                step(dve.tensor_scalar(cycles, cycles, ROUND, None, ALU.add))
                step(dve.tensor_scalar(cycles, cycles, -ROUND, None, ALU.add))
                if k:
                    dve.wait_ge(*sin_ready.at(0))
                for n, part in enumerate(TWO_PI):
                    step(dve.scalar_tensor_tensor(reduced, cycles, -part, reduced if n else angle, ALU.mult, ALU.add))
                step(dve.tensor_scalar(reduced, reduced, quarter * 2 * np.pi, None, ALU.add))
                dve.tensor_scalar(reduced, reduced, 3.1415925, -3.1415925, ALU.min, ALU.max).then_inc(angle_ready.sem, 1)
            dve.wait_ge(*sin_ready.at(1))
            step(dve.tensor_scalar(rope_sin, rope_sin, rope_sign, None, ALU.mult))
            z = [lb[:, k * DC:k * DC + DC] for k in range(8)]
            l0, l1 = cols[:, 128:128 + DC], cols[:, 128 + DC:128 + 2 * DC]
            step(dve.tensor_tensor(z[0], l0, l1, ALU.max))
            dve.tensor_tensor(z[1], l0, z[0], ALU.subtract)
            dve.tensor_tensor(z[2], l1, z[0], ALU.subtract).then_inc(setup_lb_diff[0], 1)
            dve.wait_ge(*lb_exp.at(0))
            step(dve.tensor_tensor(z[3], z[1], z[2], ALU.add))
            step(dve.reciprocal(z[4], z[3]))
            step(dve.tensor_tensor(z[5], z[1], z[4], ALU.mult))
            step(dve.tensor_tensor(z[6], z[2], z[4], ALU.mult))
            step(dve.tensor_tensor(z[6], z[5], z[6], ALU.add))
            step(dve.tensor_tensor(z[6], z[6], z[5], ALU.subtract))
            step(dve.tensor_scalar(z[7], z[6], -1.0, 1.0, ALU.mult, ALU.add))
            step(dve.tensor_tensor(qk_gain[:], gain("dsa_q", 0), gain("dsa_k", 0), ALU.mult))

            pre_mla.dve(dve)

            def normed_c(n, gain_name, first, count_c):
                dve.wait_ge(*n.ready())
                for c in range(count_c + 1):
                    if c < count_c:
                        s_c.free(dve, first + c)
                        dve.scalar_tensor_tensor(tmp[(first + c) % 2], mla_c[first + c], gain(gain_name, c), rstd,
                                                 ALU.mult, ALU.mult).then_inc(s_c.whole.sem, 1)
                    if c >= 1:
                        k = first + c - 1
                        s_c.rest(dve, tile(g_lo, k), tile(g_hi, k), k)
            normed_c(n_cq, "mla_q", 0, 4)
            normed_c(n_ckv, "mla_kv", 4, 2)

            def rotate(st, j, i, dst, done):
                for k, table in ((0, rope_cos), (1, rope_sin)):
                    bank = arrived(dve, st, j + k, i)
                    dve.tensor_tensor(tmp[k], bank[:], table, ALU.mult).then_inc(*taken(st, j + k))
                emptied(dve, st, j + 1, i)
                dve.tensor_tensor(dst, tmp[0], tmp[1], ALU.add).then_inc(done.sem, 1)
            dve.wait_ge(*s_c.low.at(5))
            rotate(st_mla_in, 6, 0, k_rope, k_rope_ready)
            dve.wait_ge(*k_rope_ready.at(0))

            def mla_heads(i):
                rotate(st_mla, 2, i, q_rope[0], q_rope_ready)
                dve.wait_ge(*q_rope_ready.at(0, i))
                rotate(st_mla, 10, i, q_rope[1], q_rope_ready)
                at_mla.dve(dve, i, lambda t: causal("causal", t % TB), lambda hh: tile(a_lo, i * MLA_TURN + hh),
                           lambda hh: tile(a_hi, i * MLA_TURN + hh))
            turns(dve, st_mla.turns, mla_heads)
            out_mla.dve(dve, mlp[0].pre)
            mlp[0].dve(dve)

            pre_hg.dve(dve)
            dve.memset(hg_a, 0.0).then_inc(hg_cleared.sem, 1)
            dve.wait_ge(*hg_cleared.at(0))
            by_chunk = lambda t: t.rearrange("p (n c) -> p n c", n=HG_N)
            chunk_col = lambda t, c: by_chunk(t)[:, :, c:c + 1].to_broadcast([P, HG_N, HG_CHUNK])
            state = lambda n: hg_state[:, n * P:n * P + P]

            def hg_before(i):
                emptied(dve, st_hg, 1, i)
                dve.tensor_scalar(hg_f, hg_sig, lb[:, bass.ds(7 * DC + i, 1)], lb[:, bass.ds(6 * DC + i, 1)],
                                  ALU.mult, ALU.add).then_inc(hg_f_ready.sem, 1)
                dve.wait_ge(*hg_f_ready.at(0, i))
                dve.tensor_scalar(hg_k, hg_f, -1.0, 1.0, ALU.mult, ALU.add).then_inc(hg_k_ready.sem, 1)
                dve.wait_ge(*hg_logf_ready.at(0, i))
                dve.tensor_tensor_scan(hg_b, tab["scan_keep"][:], hg_logf, 0.0, ALU.mult, ALU.add).then_inc(hg_b_ready.sem, 1)
                dve.wait_ge(*hg_b_ready.at(0, i))
                dve.wait_ge(*hg_k_ready.at(0, i))
                dve.tensor_tensor(by_chunk(hg_d), by_chunk(hg_b), chunk_col(hg_b, HG_CHUNK // 2),
                                  ALU.subtract).then_inc(hg_d_ready.sem, 1)
                dve.tensor_tensor(by_chunk(hg_d2), chunk_col(hg_b, HG_CHUNK - 1), by_chunk(hg_b),
                                  ALU.subtract).then_inc(hg_d2_ready.sem, 1)
                emptied(dve, st_hg, 0, i)
                dve.wait_ge(*hg_e_ready.at(0, i))
                dve.tensor_tensor(hg_qrel, hg_e[0], hg_q, ALU.mult).then_inc(hg_rel_ready.sem, 1)
                dve.wait_ge(*hg_e_ready.at(1, i))
                dve.tensor_tensor(hg_krel, hg_e[1], hg_k, ALU.mult).then_inc(hg_rel_ready.sem, 1)
                dve.wait_ge(*hg_e_ready.at(2, i))
                if not (isinstance(i, int) and i == 0):
                    dve.wait_ge(*hg_o.at(0, i - 1))
                dve.tensor_tensor(hg_qdec, hg_e[2], hg_q, ALU.mult).then_inc(hg_dec_ready.sem, 1)
                dve.wait_ge(*hg_e_ready.at(3, i))
                dve.tensor_tensor(hg_kdec, hg_e[3], hg_k, ALU.mult).then_inc(hg_dec_ready.sem, 1)

            def hg_states(i):
                dve.wait_ge(*hg_scores.at(0, i))
                plain_wait(dve)
                dve.copy_predicated(hg_a.rearrange("p (g c) -> p g c", g=TB),
                                    hg_mask[:].rearrange("p (a c) -> p a c", a=1).to_broadcast([P, TB, P]),
                                    aux[0][:].rearrange("p (g c) -> p g c", g=TB)).then_inc(hg_masked.sem, 1)
                for n in range(HG_N - 1):
                    u = aux[n % HG_G][:, n // HG_G * P:n // HG_G * P + P]
                    if n == 0:
                        dve.wait_ge(*hg_u.at(0, i))
                        dve.tensor_copy(state(1), u).then_inc(hg_state_ready.sem, 1)
                    else:
                        dve.wait_ge(*hg_state_ready.at(n - 1, i))
                        last = (n + 1) * HG_CHUNK - 1
                        dve.scalar_tensor_tensor(state(n + 1), state(n), hg_dec[:, last:last + 1], u,
                                                 ALU.mult, ALU.add).then_inc(hg_state_ready.sem, 1)

            def hg_after(i):
                dve.wait_ge(*n_hg.ready(0, i))
                dve.scalar_tensor_tensor(tmp[1], aux[0][:], gain("hg_o", 0), rstd, ALU.mult, ALU.mult).then_inc(hg_y.sem, 1)
                dve.wait_ge(*hg_y.at(0, i))
                emptied(dve, st_hg, 3, i)
                s_hg.free(dve, 0, i)
                dve.tensor_tensor(tmp[0], tmp[1], hg_gate, ALU.mult).then_inc(s_hg.whole.sem, 1)
                s_hg.rest(dve, tile(g_lo, i), tile(g_hi, i), 0, i)
            hg_before(0)
            with dve.Fori(0, HG_HEADS - 1) as i:
                hg_states(i)
                hg_before(i + 1)
                hg_after(i)
            hg_states(HG_HEADS - 1)
            hg_after(HG_HEADS - 1)
            out_hg.dve(dve, mlp[1].pre)
            mlp[1].dve(dve)

            pre_dsa.dve(dve)
            for g in range(5):
                dst, name = (idx_q[g], "dsa_iq") if g < 4 else (idx_k, "dsa_ik")
                dve.wait_ge(*n_idx.ready(g))
                dve.scalar_tensor_tensor(dst, dst, gain(name, 0), rstd, ALU.mult, ALU.mult).then_inc(idx_ready.sem, 1)
            dve.wait_ge(*n_key.ready())
            dve.scalar_tensor_tensor(dsa_kT, dsa_cT, qk_gain[:], rstd, ALU.mult, ALU.mult).then_inc(key_ready.sem, 1)
            dve.wait_ge(*wi_ready.at(0))
            for r, (b, h) in enumerate(REL):
                w = (b + 1) * P
                score = dsa_bias[b][:, 0:w]
                dve.wait_ge(*rel_taken.at(r))
                if h:
                    dve.wait_ge(*scored.at(r - 1))
                dve.scalar_tensor_tensor(score, idx_rel[r % 2][:, 0:w], wi_tok[:, b * IDX_HEADS + h:b * IDX_HEADS + h + 1],
                                         score if h else causal("admissible", b), ALU.mult, ALU.add).then_inc(scored.sem, 1)
                if h < IDX_HEADS - 1:
                    continue
                dve.wait_ge(*scored.at(r))
                rounds = TOPK // 8
                with dve.Fori(0, rounds):
                    dve.max(top8[:], score)
                    dve.drain()
                    dve.match_replace(score, top8[:], score, GONE)
                    dve.drain()
                dve.tensor_scalar(score, score, GONE / 2, NEG, ALU.is_gt, ALU.mult).then_inc(dsa_bias_ready.sem, 1)
            dve.wait_ge(*dsa_bias_ready.at(TB - 2))

            dve.wait_ge(*n_dq.ready())

            def dsa_heads(i):
                r = q_rstds[:, bass.ds(i * (DSA_TURN * TB), DSA_TURN * TB)]
                dve.tensor_copy(q_rstd[:], r).then_inc(q_rstd_turn.sem, 1)
                dve.tensor_scalar(q_rstd_neg[:], r, -1.0, None, ALU.mult).then_inc(q_rstd_turn.sem, 1)
                dve.wait_ge(*q_rstd_turn.at(1, i))
                at_dsa.dve(dve, i, lambda t: dsa_bias[t % TB][:, 0:(t % TB + 1) * P] if t % TB else causal("admissible", 0),
                           lambda hh: tile(g_lo, i * DSA_TURN + hh), lambda hh: tile(g_hi, i * DSA_TURN + hh))
            turns(dve, DSA_HEADS // DSA_TURN, dsa_heads)
            for m in range(DC):
                bank = arrived(dve, st_dsa_o, m)
                dve.tensor_tensor(tile(hT, m), bank[:], tile(hT, m), ALU.add).then_inc(*taken(st_dsa_o, m))
            ffn[0].dve(dve)

            for c in range(DC):
                pre_ret.rest(dve, c)
            pre_ret.adds(dve)
            for table in (ret_cos, ret_sin):
                dve.tensor_tensor(table[:], table[:], rstd, ALU.mult).then_inc(ret_factors.sem, 1)
            dve.tensor_copy(ret_factor[:], rstd).then_inc(ret_factors.sem, 1)
            dve.wait_ge(*ret_factors.at(2))

            def ret_rotate(st, j, i, h):
                s_ret.free(dve, 0, h)
                for s, dst in ((0, ret_q), (1, ret_k)):
                    if s:
                        dve.wait_ge(*ret_qk_ready.at(1, h))
                    u0, u1 = j + 2 * s, j + 2 * s + 1
                    p0, p1 = arrived(dve, st, u0, i), arrived(dve, st, u1, i)
                    dve.tensor_tensor(dst[0], p0[:], ret_cos[:], ALU.mult).then_inc(ret_part.sem, 1)
                    dve.tensor_tensor(tmp[0], p1[:], ret_sin[:], ALU.mult).then_inc(ret_part.sem, 1)
                    dve.tensor_tensor(tmp[1], p0[:], ret_sin[:], ALU.mult).then_inc(*taken(st, u0))
                    dve.tensor_tensor(dst[1], p1[:], ret_cos[:], ALU.mult).then_inc(*taken(st, u1))
                    dve.wait_ge(*ret_part.at(2 * s + 1, h))
                    dve.tensor_tensor(dst[0], dst[0], tmp[0], ALU.subtract).then_inc(ret_qk_ready.sem, 1)
                    emptied(dve, st, u1, i)
                    dve.tensor_tensor(dst[1], tmp[1], dst[1], ALU.add).then_inc(ret_qk_ready.sem, 1)

            def ret_head(st, i, h):
                def take(j, dst):
                    bank = arrived(dve, st, j, i)
                    dve.tensor_tensor(dst, bank[:], ret_factor[:], ALU.mult).then_inc(*taken(st, j))

                def decay(b):
                    w = T - b * P
                    dve.wait_ge(*ret_scores.at(b, h))
                    dve.tensor_tensor(ret_s[b][:, 0:w], aux[b % 2][:, 0:w], ret_decay[:, bass.ds(h * T, w)],
                                      ALU.mult).then_inc(ret_s_ready.sem, 1)
                for m in range(RV):
                    if m >= 2:
                        dve.wait_ge(*ret_v_turned.at(m - 2, h))
                    take(m, ret_vT[m % 2])
                decay(0)
                decay(1)
                take(4, ret_gate[0])
                take(5, ret_gate[1])
                decay(2)
                take(6, ret_gate[2])
                decay(3)
                take(7, ret_gate[3])
                dve.wait_ge(*n_ret.ready(0, h))
                for m in range(RV + 1):
                    if m < RV:
                        dve.scalar_tensor_tensor(ret_raw[m], ret_raw[m], gain("ret_out", h * RV + m), rstd, ALU.mult,
                                                 ALU.mult).then_inc(ret_y.sem, 1)
                        dve.wait_ge(*ret_y.at(m, h))
                        s_ret.free(dve, m, h)
                        dve.tensor_tensor(tmp[m % 2], ret_raw[m], ret_gate[m], ALU.mult).then_inc(s_ret.whole.sem, 1)
                    if m >= 1:
                        s_ret.rest(dve, tile(g_lo, m - 1), tile(g_hi, m - 1), m - 1, h)

            def ret_out(st, j, i):
                for m in range(DC):
                    bank = arrived(dve, st, j + m, i)
                    dve.tensor_tensor(tile(hT, m), bank[:], tile(hT, m), ALU.add).then_inc(*taken(st, j + m))
            ret_rotate(st_ret_qk, 0, 0, 0)
            with dve.Fori(0, RET_HEADS - 1) as i:
                ret_head(st_ret, i, i)
                ret_rotate(st_ret, 8, i, i + 1)
                ret_out(st_ret, 12, i)
            ret_head(st_ret_end, 0, RET_HEADS - 1)
            ret_out(st_ret_end, 8, 0)
            ffn[1].dve(dve)

            for k in range(2 * TB):
                dve.wait_ge(*out_turned.at(k))
                dve.tensor_copy(acc[:, k * T:k * T + T], aux[k % 4][:]).then_inc(out_ready.sem, 1)

        @block.tensor
        def _(pe):
            pe.wait_ge(tables_in, 16 * (len(TABLE_WIDTH) + 1))
            pe.wait_ge(x_in, 16)
            for c in range(DC):
                if c >= 2:
                    pe.wait_ge(*h_ready.at(c - 2))
                for b in range(TB):
                    last = pe.transpose(aux[c % 2][:, b * P:b * P + P], acc[:, b * D + c * P:b * D + c * P + P], ident[:])
                last.then_inc(x_turned.sem, 1)
            pe.wait_ge(rows_in, 16 * len(row_loads))
            for k, (rows_t, n, c0) in enumerate(row_tiles):
                if k >= 2:
                    pe.wait_ge(*turned_out.at(k - 2))
                pe.transpose(aux[2 + k % 2][:, 0:n], rows_t[0:n, :], ident[0:n, 0:n]).then_inc(turned.sem, 1)

            pe.wait_ge(*h_ready.at(DC - 1))
            pre_mla.pe(pe)
            for j in range(8):
                unit(pe, st_mla_in, j, DC, a_hi, a_lo, ready=pre_mla.ready if j == 0 else None)
                if 1 <= j <= 6:
                    n, c = (n_cq, j - 1) if j <= 4 else (n_ckv, j - 5)
                    n.sum(pe, c)

            def mla_heads(i):
                for j in range(st_mla.per):
                    a, q = divmod(j, 8)
                    if q < 4:
                        unit(pe, st_mla, j, MLA_Q // P, g_hi, g_lo, i, ready=s_c.low.at if j == 0 else None)
                    else:
                        unit(pe, st_mla, j, MLA_KV // P, g_hi, g_lo, i, k0=4,
                             ready=(lambda k: s_c.low.at(4 + k)) if j == 4 else None)
                    if j in V_AFTER:
                        hh = V_AFTER[j]
                        emptied(pe, st_mla, 8 * (hh // 2) + 5 + 2 * (hh % 2), i)
                        if hh >= 2:
                            pe.wait_ge(*v_ready.at(hh - 2, i))
                        turn_block(pe, aux[2 + hh % 2], vT[hh % 2]).then_inc(v_turned.sem, 1)
                pe.wait_ge(*q_rope_ready.at(1, i))
                pe.wait_ge(*k_rope_ready.at(0))
                pe.wait_ge(*v_ready.at(MLA_TURN - 1, i))

                def score(t, o, w):
                    hh, b = t // TB, t % TB
                    h0 = hh % 2 * MLA_ROPE
                    pe.matmul(o[:, 0:w], qn[hh][:, b * P:b * P + P], kn[hh][:, 0:w], start=True, stop=False)
                    return pe.matmul(o[:, 0:w], q_rope[hh // 2][h0:h0 + MLA_ROPE, b * P:b * P + P],
                                     k_rope[h0:h0 + MLA_ROPE, 0:w], start=False, stop=True)
                at_mla.pe(pe, i, score, lambda hh, kb: vtok[hh][:, kb * P:kb * P + P])
            turns(pe, st_mla.turns, mla_heads)
            out_mla.pe(pe, lambda k: at_mla.out_lo.at(k))
            mlp[0].pe(pe)

            pre_hg.pe(pe)

            def hg_units(js, i, ready=None):
                for j in js:
                    unit(pe, st_hg, j, DC, a_hi, a_lo, i, ready=ready if j == 0 else None)

            def hg_recur(i):
                pe.wait_ge(*hg_rel_ready.at(1, i))
                pe.wait_ge(*hg_y.at(0, i - 1))
                for g in range(TB):
                    s = slice(g * P, g * P + P)
                    last = pe.matmul(aux[0][:, s], hg_krel[:, s], hg_qrel[:, s], start=True, stop=True)
                last.then_inc(hg_scores.sem, 1)
                emptied(pe, st_hg, 2, i)
                turn_block(pe, aux[1], hg_vT).then_inc(hg_v_turned.sem, 1)
                pe.wait_ge(*hg_dec_ready.at(1, i))
                pe.wait_ge(*hg_v_ready.at(0, i))
                turn_block(pe, aux[1], hg_kdec).then_inc(hg_k_turned.sem, 1)
                pe.wait_ge(*hg_kT_ready.at(0, i))

                def outer(g):
                    for c in range(HG_G):
                        t = slice(c * HG_CHUNK, (c + 1) * HG_CHUNK)
                        s = slice(g * P, g * P + P)
                        last = pe.matmul(aux[c][:, s], hg_kT[t, s], hg_v[t, s], start=True, stop=True)
                    return last

                pe.wait_ge(*hg_masked.at(0, i))
                for g in range(TB):
                    last = outer(g)
                last.then_inc(hg_u.sem, 1)

            def hg_output(i):
                def output(g):
                    s = slice(g * P, g * P + P)
                    last = pe.matmul(aux[0][:, s], hg_v[:, s], hg_a[:, s], start=True, stop=True,
                                     skip_group_check=True)
                    for c in range(HG_G):
                        n = g * HG_G + c
                        if n == 0:
                            continue
                        t = slice(n * HG_CHUNK, (n + 1) * HG_CHUNK)
                        last = pe.matmul(aux[0][:, t], hg_state[:, n * P:n * P + P], hg_qdec[:, t], start=False,
                                         stop=True, skip_group_check=True)
                    return last
                pe.wait_ge(*hg_state_ready.at(HG_N - 2, i))
                for g in range(TB):
                    last = output(g)
                last.then_inc(hg_o.sem, 1)
                n_hg.sum(pe, 0, 0, i)
            hg_units(range(4), 0, pre_hg.ready)
            with pe.Fori(0, HG_HEADS - 1) as i:
                hg_units((0, 1), i + 1)
                hg_recur(i)
                hg_units((2, 3), i + 1)
                hg_output(i)
            hg_recur(HG_HEADS - 1)
            hg_output(HG_HEADS - 1)
            out_hg.pe(pe, lambda k: s_hg.low.at(0, k))
            mlp[1].pe(pe)

            pre_dsa.pe(pe)
            for j in range(NG + 1):
                unit(pe, st_dsa, j, DC, a_hi, a_lo, ready=pre_dsa.ready if j == 0 else None)
                if 1 <= j <= 5:
                    n_idx.sum(pe, 0, j - 1)
            n_key.sum(pe, 0)
            emptied(pe, st_dsa, 5)
            turn_block(pe, aux[2], dsa_cT).then_inc(c_turned.sem, 1)
            emptied(pe, st_dsa, NG)
            for b in range(TB):
                last = pe.transpose(aux[3][:, b * IDX_HEADS:(b + 1) * IDX_HEADS], wiT[0:IDX_HEADS, b * P:b * P + P],
                                    ident[0:IDX_HEADS, 0:IDX_HEADS])
            last.then_inc(wi_turned.sem, 1)
            pe.wait_ge(*idx_ready.at(4))
            pe.wait_ge(*key_ready.at(0))
            for r, (b, h) in enumerate(REL):
                if r >= 2:
                    pe.wait_ge(*rel_taken.at(r - 2))
                h0, w = h % 2 * IDX_DIM, (b + 1) * P
                pe.matmul(aux[r % 2][:, 0:w], idx_q[h // 2][h0:h0 + IDX_DIM, b * P:b * P + P], idx_k[h0:h0 + IDX_DIM, 0:w],
                          start=True, stop=True).then_inc(rel_ready.sem, 1)
                if h == IDX_HEADS - 1:
                    for q in Q_AFTER[b - 1]:
                        unit(pe, st_dsa, Q0 + q, DC, a_hi, a_lo)
                        if q == 0:
                            pe.wait_ge(*c_ready.at(0))
                        else:
                            n_dq.sum_tokens(pe, q - 1)
            n_dq.sum_tokens(pe, DSA_HEADS - 1)

            pe.wait_ge(*n_dq.ready())

            def dsa_heads(i):
                def score(t, o, w):
                    hh, b = t // TB, t % TB
                    if b == 0:
                        pe.wait_ge(*dsa_q_ready.at(hh, i))
                    return pe.matmul(o[:, 0:w], dsa_q[hh][:, b * P:b * P + P], dsa_kT[:, 0:w], start=True, stop=True)
                at_dsa.pe(pe, i, score, lambda hh, kb: dsa_c[:, kb * P:kb * P + P])
            turns(pe, DSA_HEADS // DSA_TURN, dsa_heads)
            for m in range(DC):
                unit(pe, st_dsa_o, m, DC, g_hi, g_lo, ready=at_dsa.out_lo.at if m == 0 else None)
            ffn[0].pe(pe)

            for j in range(4):
                unit(pe, st_ret_qk, j, DC, a_hi, a_lo, ready=pre_ret.low.at if j == 0 else None)
                if j == 1:
                    pre_ret.norm.sum(pe)

            def ret_head(st, i, h):
                def turn(m):
                    emptied(pe, st, m, i)
                    pe.wait_ge(*(ret_v_ready.at(m - 2, h) if m >= 2 else ret_raw_ready.at(-1, h)))
                    turn_block(pe, aux[2 + m % 2], ret_vT[m % 2]).then_inc(ret_v_turned.sem, 1)

                def scores(b):
                    w = T - b * P
                    pe.wait_ge(*ret_qk_ready.at(3, h))
                    if b >= 2:
                        pe.wait_ge(*ret_s_ready.at(b - 2, h))
                    for c in range(2):
                        last = pe.matmul(aux[b % 2][:, 0:w], ret_k[c][:, b * P:b * P + P], ret_q[c][:, b * P:T],
                                         start=c == 0, stop=c == 1)
                    last.then_inc(ret_scores.sem, 1)
                for m in range(RV):
                    unit(pe, st, m, DC, a_hi, a_lo, i)
                    if m >= 1:
                        turn(m - 1)
                scores(0)
                scores(1)
                for m in range(RV):
                    unit(pe, st, RV + m, DC, a_hi, a_lo, i)
                    if m == 0:
                        turn(RV - 1)
                    elif m <= 2:
                        scores(m + 1)
                pe.wait_ge(*ret_v_ready.at(RV - 1, h))
                for m in range(RV + 1):
                    if m < RV:
                        if m >= 2:
                            pe.wait_ge(*ret_raw_ready.at(m - 2, h))
                        for b in range(TB):
                            if m == 0:
                                pe.wait_ge(*ret_s_ready.at(b, h))
                            e = b * RET_DV + m * P
                            last = pe.matmul(aux[2 + m % 2][:, b * P:T], ret_vtok[:, e:e + P], ret_s[b][:, 0:T - b * P],
                                             start=b == 0, stop=b == TB - 1, skip_group_check=True)
                        last.then_inc(ret_o.sem, 1)
                    if m >= 1:
                        n_ret.sum(pe, m - 1, 0, h)

            def ret_out(st, j, i, h):
                for m in range(DC):
                    unit(pe, st, j + m, RET_DV // P, g_hi, g_lo, i,
                         ready=(lambda k: s_ret.low.at(k, h)) if m == 0 else None)
            with pe.Fori(0, RET_HEADS - 1) as i:
                ret_head(st_ret, i, i)
                for j in range(8, 12):
                    unit(pe, st_ret, j, DC, a_hi, a_lo, i)
                ret_out(st_ret, 12, i, i)
            ret_head(st_ret_end, 0, RET_HEADS - 1)
            ret_out(st_ret_end, 8, 0, RET_HEADS - 1)
            ffn[1].pe(pe)

            for c in range(DC):
                pe.wait_ge(*ffn[1].h_at(c))
            for k in range(2 * TB):
                b = k // 2
                if k >= 4:
                    pe.wait_ge(*out_ready.at(k - 4))
                for q in range(4):
                    c = k % 2 * 4 + q
                    last = pe.transpose(aux[k % 4][:, q * P:q * P + P], hT[:, c * T + b * P:c * T + b * P + P], ident[:])
                last.then_inc(out_turned.sem, 1)


_INS = ["x", "positions", "norm_gains", "mla_w_in", "mla_q_norm", "mla_kv_norm", "mla_w_uq", "mla_w_ukv", "mla_w_o",
        "hgrn_w_in", "hgrn_lb_logits", "hgrn_o_norm", "hgrn_w_o", "mlp_w1", "mlp_w2", "norm_mix_g_2", "norm_ffn_g_2",
        "a_w_in_2", "a_q_g_2", "a_k_g_2", "a_iq_g_2", "a_ik_g_2", "a_w_out_2", "b_w_in_2", "b_out_g_2", "b_w_out_2",
        "f_w_up_2", "f_conv_w_2", "f_conv_b_2", "f_w_down_2"]


def kernel(**inputs):
    import concourse.bacc as bacc
    from concourse.bass_utils import run_bass_kernel_spmd as run

    nc = bacc.Bacc("TRN2", target_bir_lowering=False, num_devices=1)
    arrays = {}

    def given(name, a):
        arrays[name] = a
        return nc.dram_tensor(name, a.shape, mybir.dt.from_np(a.dtype), kind="ExternalInput").ap()

    args = [given(f"in_{name}", np.ascontiguousarray(inputs[name])) for name in _INS]
    tabs, hg = shape_tables()
    tables = {k: given(f"table_{k}", np.ascontiguousarray(v)) for k, v in tabs.items()}
    hg_mask = given("table_hg_mask", hg)
    out = nc.dram_tensor("out_0", (1, T, D), F32, kind="ExternalOutput").ap()
    program(nc, *args, tables, hg_mask, out)
    r = run(nc, [arrays], core_ids=[0])
    return r.results[0]["out_0"]
```

```python
from contextlib import ExitStack

import numpy as np
import concourse.bass as bass
from concourse import mybir

F32 = mybir.dt.float32
F32R = mybir.dt.float32r
I32 = mybir.dt.int32
ALU = mybir.AluOpType
ACT = mybir.ActivationFunctionType

P = 128
T = 512
TB = T // P
D = 1024
DC = D // P
RING = 4
SLAB = 2048
EPS = 1e-6
NEG = -1e30
GONE = -3e38

MLA_HEADS, MLA_Q, MLA_KV, MLA_NOPE, MLA_ROPE, MLA_V = 8, 512, 256, 128, 64, 128
MLA_SCALE = (MLA_NOPE + MLA_ROPE) ** -0.5
FF = 4096
HG_HEADS, HG_CHUNK = 8, 32
HG_N = T // HG_CHUNK
HG_G = P // HG_CHUNK
DSA_HEADS, DSA_LAT, IDX_HEADS, IDX_DIM = 8, 128, 8, 64
DSA_CHUNK, TOPK = 64, 128
DSA_SCALE = DSA_LAT ** -0.5
IDX_SCALE = IDX_HEADS ** -0.5 * IDX_DIM ** -0.5
RET_HEADS, RET_DK, RET_DV = 4, 256, 512
FF2 = 2816
FF2C = FF2 // P
CONV_W = 3
ROPE_BASE = 10000.0

TWO_PI = [6.28125, 0.00193500518798828125, 3.0199159819e-7]
ROUND = 1.5 * 2.0 ** 23


def shape_tables():
    f32 = np.float32
    p = np.arange(P)[:, None]
    t = np.arange(T)[None, :]
    tabs = {}
    tabs["ident"] = np.eye(P, dtype=f32)
    tabs["ones"] = np.ones((P, P), f32)
    tabs["ones_half"] = (p // 64 == np.arange(P)[None, :] // 64).astype(f32)
    u = t - (T - P)
    tabs["causal"] = np.where(u <= p, 0.0, NEG).astype(f32)
    tabs["admissible"] = np.where(u < (p // DSA_CHUNK + 1) * DSA_CHUNK, 0.0, NEG).astype(f32)
    tabs["scan_keep"] = np.broadcast_to((t % HG_CHUNK != 0), (P, T)).astype(f32)
    inv = np.power(f32(ROPE_BASE), -np.arange(0, MLA_ROPE, 2, dtype=f32) / f32(MLA_ROPE)).astype(f32)
    half = (np.arange(P) % MLA_ROPE) // (MLA_ROPE // 2)
    tabs["small"] = np.stack([inv[np.arange(P) % (MLA_ROPE // 2)], np.where(half == 0, -1.0, 1.0),
                              np.full(P, EPS), np.zeros(P), np.arange(P) < 64, np.arange(P) >= 64], 1).astype(f32)
    inv2 = (f32(1.0) / np.power(f32(ROPE_BASE), np.arange(0, RET_DK, 2, dtype=f32) / f32(RET_DK))).astype(f32)
    ang = (np.arange(T, dtype=f32)[None, :] * inv2[:, None]).astype(f32)
    tabs["ret_cos"] = np.cos(ang.astype(np.float64)).astype(f32)
    tabs["ret_sin"] = np.sin(ang.astype(np.float64)).astype(f32)
    dec = []
    for h in range(RET_HEADS):
        lg = np.log1p(-(2.0 ** (-5.0 - h)))
        dec.append(np.where(t >= p, np.exp(np.maximum(t - p, 0) * lg) * RET_DK ** -0.5, 0.0))
    tabs["ret_decay"] = np.concatenate(dec, 1).astype(f32)
    a, b = np.arange(P)[:, None], np.arange(P)[None, :]
    hg = ((a // HG_CHUNK == b // HG_CHUNK) & (a <= b)).astype(np.int32)
    return tabs, hg


TABLE_WIDTH = {"ident": P, "ones": P, "ones_half": P, "causal": T, "admissible": T, "scan_keep": T, "small": 6,
               "ret_cos": T, "ret_sin": T, "ret_decay": RET_HEADS * T}


class Signal:

    def __init__(self, sem, per=1, credit=0):
        self.sem, self.per, self.credit = sem, per, credit

    def at(self, j, i=0):
        return self.sem, i * self.per + (j + 1 + self.credit)


class Slab:

    def __init__(self, kc, units, parts):
        self.kc, self.units, self.parts = kc, units, parts
        self.loads = len(parts(0))


class Stage:

    def __init__(self, before, turns, slabs):
        self.turns, self.slabs = turns, slabs
        self.per = sum(s.units for s in slabs)
        assert turns == 1 or (self.per % RING == 0 and len(slabs) % 2 == 0)
        self.base = before.end if before else 0
        self.end = self.base + turns * self.per
        self.slab_base = before.slab_end if before else 0
        self.slab_end = self.slab_base + turns * len(slabs)
        self.loads_base = before.loads_end if before else [0, 0]
        self.loads_per = [0, 0]
        self.first, at = [], 0
        self.loaded_at = []
        for q, s in enumerate(slabs):
            self.first.append(at)
            at += s.units
            self.loads_per[self.slot(q)] += s.loads
            self.loaded_at.append(self.loads_per[self.slot(q)])
        self.loads_end = [b + turns * n for b, n in zip(self.loads_base, self.loads_per)]
        self.before_last = before.slabs[-1].units if before else 0

    def slot(self, q):
        return (self.slab_base + q) % 2

    def bank(self, j):
        return (self.base + j) % RING

    def done(self, j, i=0):
        return i * self.per + (self.base + j + 1)

    def uses(self, j, i=0):
        return i * (self.per // RING) + (self.base + j) // RING

    def loaded(self, q, i=0):
        s = self.slot(q)
        return i * (16 * self.loads_per[s]) + 16 * (self.loads_base[s] + self.loaded_at[q])

    def raw_free(self, q, i=0):
        if q >= 2:
            return i * self.per + self.base + self.first[q - 1]
        if q == 1:
            return i * self.per + self.base
        last = min(self.before_last, self.slabs[-1].units) if self.turns > 1 else self.before_last
        return i * self.per + self.base - last


def turns(eng, n, body):
    if n == 1:
        body(0)
    else:
        with eng.Fori(0, n) as i:
            body(i)


def turns_from(eng, n, body):
    body(0, True)
    if n == 2:
        body(1, False)
    elif n > 2:
        with eng.Fori(1, n) as i:
            body(i, False)


def program(nc, x, positions, norm_gains, mla_w_in, mla_q_norm, mla_kv_norm, mla_w_uq, mla_w_ukv, mla_w_o, hgrn_w_in,
            hgrn_lb_logits, hgrn_o_norm, hgrn_w_o, mlp_w1, mlp_w2, norm_mix_g_2, norm_ffn_g_2, a_w_in_2, a_q_g_2,
            a_k_g_2, a_iq_g_2, a_ik_g_2, a_w_out_2, b_w_in_2, b_out_g_2, b_w_out_2, f_w_up_2, f_conv_w_2, f_conv_b_2,
            f_w_down_2, tables, hg_mask_dram, out):
    with ExitStack() as ctx:
        def sb(name, width, dt=F32, parts=P):
            return ctx.enter_context(nc.sbuf_tensor(name, [parts, width], dt))

        def sem(name):
            return ctx.enter_context(nc.semaphore(name))

        def signal(name, per=1, credit=0):
            return Signal(sem(name), per, credit)

        def plain_wait(dve, s=0):
            dve.memset(carrier[:, s:s + 1], 0.0)

        shared_sems = {}

        def shared(name, per=1, turns=1):
            s, used = shared_sems.get(name) or (sem(name), 0)
            shared_sems[name] = s, used + per * turns
            return Signal(s, per, used)

        def tile(t, c, width=T):
            return t[:, bass.ds(c * width, width)]

        raw = [sb(f"raw{r}", SLAB) for r in range(2)]
        w_hi = [sb(f"w_hi{r}", DC * P, F32R) for r in range(RING)]
        w_lo = [sb(f"w_lo{r}", DC * P, F32R) for r in range(RING)]
        hT = sb("hT", DC * T)
        a_hi, a_lo = sb("a_hi", DC * T, F32R), sb("a_lo", DC * T, F32R)
        g_hi, g_lo = sb("g_hi", DC * T, F32R), sb("g_lo", DC * T, F32R)
        acc = sb("acc", DC * T)
        F = sb("F", 20 * T)
        cols = sb("cols", 128 + 16 + 4 * 88)
        tab = {k: sb(k, w) for k, w in TABLE_WIDTH.items() if not k.startswith("ret_")}
        ret_cos, ret_sin, ret_decay = sb("ret_cos", T), sb("ret_sin", T), sb("ret_decay", RET_HEADS * T)
        hg_mask = sb("hg_mask", P, I32)
        ident, ones, ones_half = tab["ident"], tab["ones"], tab["ones_half"]
        inv_freq, rope_sign, eps = (tab["small"][:, k:k + 1] for k in range(3))
        zero, halves = tab["small"][:, 3:4], tab["small"][:, 4:6]
        lb = sb("lb", 8 * DC)
        row_min, row_bias, row_sum, row_inv = (sb(n, RING) for n in ("row_min", "row_bias", "row_sum", "row_inv"))
        top8 = sb("top8", 8)
        carrier = sb("carrier", RING)
        wi_tok = sb("wi_tok", TB * IDX_HEADS)
        iq_log, iq_rstd = sb("iq_log", TB * IDX_HEADS), sb("iq_rstd", TB * IDX_HEADS)
        r_log, r_square, r_half_log = (sb(n, TB) for n in ("r_log", "r_square", "r_half_log"))
        iqk_gain = sb("iqk_gain", 1)
        q_log, q_rstds = sb("q_log", DSA_HEADS * TB), sb("q_rstds", DSA_HEADS * TB)
        q_rstd, q_rstd_neg = sb("q_rstd", DSA_HEADS * TB // 2), sb("q_rstd_neg", DSA_HEADS * TB // 2)
        qk_gain, act_warm = sb("qk_gain", 1), sb("act_warm", 2)

        sq = [tile(F, 0), tile(F, 1)]
        log_ms, rstd = tile(F, 2), tile(F, 3)
        tmp = [tile(F, 4), tile(F, 5)]

        psum = [ctx.enter_context(nc.psum_tensor(f"proj{b}", [P, T], F32)) for b in range(RING)]
        aux = [ctx.enter_context(nc.psum_tensor(f"aux{b}", [P, T], F32)) for b in range(4)]

        def rows(ap, width=P):
            return ap.rearrange("(c p) -> c p", p=width)

        vec_rows = []
        where = {}
        at = 0

        def vec(name, n, src):
            nonlocal at
            where[name] = at
            vec_rows.append((at, n, 0, P, src))
            at += n

        vec("norm", 64, norm_gains.rearrange("l k (c p) -> (l k c) p", p=P))
        vec("mix", 16, norm_mix_g_2.rearrange("l (c p) -> (l c) p", p=P))
        vec("ffn", 16, norm_ffn_g_2.rearrange("l (c p) -> (l c) p", p=P))
        vec("ret_out", 16, b_out_g_2.rearrange("l (c p) -> (l c) p", p=P))
        vec("mla_q", 4, mla_q_norm.rearrange("l (c p) -> (l c) p", p=P))
        vec("mla_kv", 2, mla_kv_norm.rearrange("l (c p) -> (l c) p", p=P))
        vec("hg_o", 1, hgrn_o_norm)
        vec("dsa_q", 1, a_q_g_2)
        vec("dsa_k", 1, a_k_g_2)
        for name, src in (("dsa_iq", a_iq_g_2), ("dsa_ik", a_ik_g_2)):
            where[name] = at
            vec_rows.append((at, 1, 0, IDX_DIM, src))
            vec_rows.append((at, 1, IDX_DIM, IDX_DIM, src))
            at += 1
        VEC = at
        CONV0 = 144
        UC = 2 * FF2C
        row_tiles = [(tile(F, 6 * TB + k, P), n, c0) for k, (n, c0) in
                     enumerate([(VEC, 0), (16, 128), (88, CONV0), (88, CONV0 + 88), (88, CONV0 + 176), (88, CONV0 + 264)])]
        row_loads = [(row_tiles[0][0][r:r + n, c:c + w], src) for r, n, c, w, src in vec_rows]
        row_loads.append((row_tiles[1][0][0:16, :], hgrn_lb_logits.rearrange("l (c p) -> (l c) p", p=P)))
        for l in range(2):
            w = f_conv_w_2[l].rearrange("k (c p) -> (k c) p", p=P)
            row_loads.append((row_tiles[2 + 2 * l][0][0:2 * UC, :], w[0:2 * UC, :]))
            row_loads.append((row_tiles[3 + 2 * l][0][0:UC, :], w[2 * UC:3 * UC, :]))
            row_loads.append((row_tiles[3 + 2 * l][0][UC:2 * UC, :], f_conv_b_2[l].rearrange("(c p) -> c p", p=P)))

        def gain(name, c, n=1):
            return cols[:, bass.ds(where[name] + c, n)]

        def conv_col(l, k, c):
            return cols[:, bass.ds(CONV0 + 176 * l + k * UC + c, 1)]

        def kpn(w):
            return w.rearrange("(k p) n -> p k n", p=P)

        def plain(w, k0=0, kc=DC, width=256, col=lambda i: 0):
            v = kpn(w)
            k = k0 if callable(k0) else (lambda i: k0)
            return Slab(kc, width // P, lambda i: [(0, width, v[:, bass.ds(k(i), kc), bass.ds(col(i), width)])])

        stages = []

        def stage(n, slabs):
            s = Stage(stages[-1] if stages else None, n, slabs)
            stages.append(s)
            return s

        w_in = kpn(mla_w_in[0])
        kr0 = MLA_Q + MLA_KV
        half = MLA_ROPE // 2
        st_mla_in = stage(1, [plain(mla_w_in[0], col=lambda i, c=c: c * 256) for c in range(3)] + [
            Slab(DC, 2, lambda i: [(64 * r, 64, w_in[:, :, kr0:kr0 + 64]) for r in range(2)]
                 + [(128 + 32 * r, 32, w_in[:, :, kr0 + 32 * (1 - r % 2):kr0 + 32 * (1 - r % 2) + 32]) for r in range(4)])])
        uq = kpn(mla_w_uq[0])
        QH = MLA_NOPE + MLA_ROPE

        MLA_TURN = 4

        def uq_parts(i, a):
            c0 = lambda h: i * (MLA_TURN * QH) + (a + h) * QH
            p = [(128 * h, 128, uq[:, :, bass.ds(c0(h), 128)]) for h in range(2)]
            p += [(256 + 64 * h, 64, uq[:, :, bass.ds(c0(h) + MLA_NOPE, 64)]) for h in range(2)]
            p += [(384 + 64 * h + 32 * r, 32, uq[:, :, bass.ds(c0(h) + MLA_NOPE + 32 * (1 - r), 32)])
                  for h in range(2) for r in range(2)]
            return p

        KVH = MLA_NOPE + MLA_V
        st_mla = stage(MLA_HEADS // MLA_TURN, [
            s for a in range(0, MLA_TURN, 2) for s in (
                Slab(MLA_Q // P, 4, lambda i, a=a: uq_parts(i, a)),
                plain(mla_w_ukv[0], kc=MLA_KV // P, width=2 * KVH, col=lambda i, a=a: i * (MLA_TURN * KVH) + a * KVH))])

        def square_out(w):
            return stage(1, [plain(w, col=lambda i, c=c: c * 256) for c in range(4)])

        st_mla_o = square_out(mla_w_o[0])

        def mlp_stage(l):
            return stage(FF // D, [plain(mlp_w1[l], col=lambda i, c=c: i * D + c * 256) for c in range(4)]
                         + [plain(mlp_w2[l], k0=lambda i: i * DC, col=lambda i, c=c: c * 256) for c in range(4)])

        st_mlp = [mlp_stage(0)]
        hg_w = kpn(hgrn_w_in[0])
        st_hg = stage(HG_HEADS, [Slab(DC, 2, lambda i, a=a: [(128 * r, 128, hg_w[:, :, bass.ds(i * P + (a + r) * D, P)])
                                                            for r in range(2)]) for a in (0, 2)])
        st_hg_o = square_out(hgrn_w_o[0])
        st_mlp.append(mlp_stage(1))

        dsa_w = kpn(a_w_in_2[0])
        o1 = DSA_HEADS * DSA_LAT
        o2 = o1 + DSA_LAT
        o3 = o2 + IDX_HEADS * IDX_DIM
        o4 = o3 + IDX_DIM
        st_dsa = stage(1, [plain(a_w_in_2[0], col=lambda i, c=c: o2 + 256 * c) for c in range(2)] + [
            Slab(DC, 2, lambda i: [(64 * r, 64, dsa_w[:, :, o3:o4]) for r in range(2)] + [(128, 128, dsa_w[:, :, o1:o2])]),
            Slab(DC, 1, lambda i: [(0, IDX_HEADS, dsa_w[:, :, o4:o4 + IDX_HEADS])])]
            + [plain(a_w_in_2[0], col=lambda i, c=c: 256 * c) for c in range(4)])
        st_dsa_o = square_out(a_w_out_2[0])

        def ffn_stages(l):
            up = kpn(f_w_up_2[l])

            def blocks(n, first, size):
                pairs = [Slab(DC, 2, lambda i, j=j: [(0, P, up[:, :, bass.ds(i * D + (first + j) * P, P)]),
                                                     (P, P, up[:, :, bass.ds(i * D + FF2 + (first + j) * P, P)])])
                         for j in range(size)]
                return stage(n, pairs + [plain(f_w_down_2[l], k0=lambda i: i * DC + first, kc=size,
                                               col=lambda i, c=c: c * 256) for c in range(4)])
            full = FF2C // DC
            return [(blocks(full, 0, DC), 0, DC), (blocks(1, full * DC, FF2C - full * DC), full * DC, FF2C - full * DC)]

        st_ffn = [ffn_stages(0)]
        dq, dv = RET_HEADS * RET_DK, RET_HEADS * RET_DV

        def ret_slabs(part, h):
            w, v0 = b_w_in_2[0], 2 * dq
            if part == "qk":
                return [plain(w, col=lambda i, c=c: h(i) * RET_DK + c) for c in (0, dq)]
            if part == "out":
                return [plain(b_w_out_2[0], k0=lambda i: h(i) * (RET_DV // P), kc=RET_DV // P, width=512,
                              col=lambda i, c=c: 512 * c) for c in range(2)]
            c0 = v0 if part == "v" else v0 + dv
            return [plain(w, col=lambda i, c=c: h(i) * RET_DV + c0 + 256 * c) for c in range(2)]

        this, following, final = (lambda i: i), (lambda i: i + 1), (lambda i: RET_HEADS - 1)
        st_ret_qk = stage(1, ret_slabs("qk", this))
        st_ret = stage(RET_HEADS - 1, ret_slabs("v", this) + ret_slabs("g", this) + ret_slabs("qk", following)
                       + ret_slabs("out", this))
        st_ret_end = stage(1, ret_slabs("v", final) + ret_slabs("g", final) + ret_slabs("out", final))
        st_ffn.append(ffn_stages(1))

        loaded = [sem("loaded0"), sem("loaded1")]
        hi_split, lo_split = sem("hi_split"), sem("lo_split")
        unit_done = sem("unit_done")
        bank_free = [sem(f"bank_free{b}") for b in range(RING)]

        def raw_view(slot, s):
            return raw[slot][:, 0:s.kc * s.units * P].rearrange("p (k n) -> p k n", k=s.kc)

        first_in, tables_in, rows_in, x_in = sem("first_in"), sem("tables_in"), sem("rows_in"), sem("x_in")
        FIRST_TABLES = ("small", "ident", "ones")
        FIRST_IN, TABLES_IN = 16 * (1 + len(FIRST_TABLES)), 16 * (len(TABLE_WIDTH) - len(FIRST_TABLES) + 1)
        stored = sem("stored")
        turned = signal("turned")
        turned_out = signal("turned_out")
        x_turned, h_ready = signal("x_turned"), signal("h_ready")
        sq_ready, sq_used = signal("sq_ready"), signal("sq_used")
        log_ready, rstd_ready = signal("log_ready"), signal("rstd_ready")
        setup = signal("setup")
        lb_exp = signal("lb_exp")
        setup_lb_diff = (sem("lb_diff"), 1)

        class Norm:
            squares = groups_done = 0

            def __init__(self, chunks, turns=1, groups=1, matrix=ones, size=None, bank=aux[0]):
                self.chunks, self.per, self.gper = chunks, chunks * groups, groups
                self.matrix, self.bank, self.size = matrix, bank, size or chunks * P
                self.base, self.gbase = Norm.squares, Norm.groups_done
                Norm.squares += turns * self.per
                Norm.groups_done += turns * groups

            def square(self, act, src, c, g=0, i=0):
                m, n = self.base + g * self.chunks + c, len(sq)
                before = m - n + 1 if c >= n else m - c
                if before > 0:
                    act.wait_ge(sq_used.sem, i * self.per + before)
                act.activation(sq[c % n], src, ACT.Square).then_inc(sq_ready.sem, 1)

            def sum(self, pe, c, g=0, i=0):
                m = self.base + g * self.chunks + c
                if c == 0 and self.gbase + g > 0:
                    pe.wait_ge(log_ready.sem, i * self.gper + self.gbase + g)
                pe.wait_ge(sq_ready.sem, i * self.per + m + 1)
                pe.matmul(self.bank[:], self.matrix[:], sq[c % len(sq)], start=c == 0,
                          stop=c == self.chunks - 1).then_inc(sq_used.sem, 1)

            def sum_tokens(self, pe, c, column, groups):
                m, n = self.base + c, groups.shape[1]
                if c == 0:
                    pe.wait_ge(log_ready.sem, self.gbase)
                pe.wait_ge(sq_ready.sem, m + 1)
                for b in range(TB):
                    k = column(b)
                    last = pe.matmul(self.bank[:, k:k + n], sq[c % 2][:, b * P:b * P + P], groups, start=True, stop=True)
                last.then_inc(sq_used.sem, 1)

            def root(self, act, g=0, i=0, users=None):
                n = self.gbase + g
                if n > 0:
                    act.wait_ge(rstd_ready.sem, i * self.gper + n)
                act.wait_ge(sq_used.sem, i * self.per + self.base + (g + 1) * self.chunks)
                act.activation(log_ms, self.bank[:], ACT.Ln, bias=eps, scale=1.0 / self.size).then_inc(log_ready.sem, 1)
                act.wait_ge(log_ready.sem, i * self.gper + n + 1)
                if users is not None:
                    act.wait_ge(*users)
                act.activation(rstd, log_ms, ACT.Exp, scale=-0.5).then_inc(rstd_ready.sem, 1)

            def ready(self, g=0, i=0):
                return rstd_ready.sem, i * self.gper + self.gbase + g + 1

        class AddedNorm(Norm):

            def __init__(self, chunks, total):
                super().__init__(chunks)
                self.total = total

            def square(self, act, src, c):
                n = len(sq)
                if c == 0:
                    act.activation(act_warm[:, self.gbase % 2:self.gbase % 2 + 1], eps, ACT.Ln)
                if self.base > 0 and c == 0:
                    act.wait_ge(sq_used.sem, self.base)
                if c > n:
                    act.wait_ge(sq_used.sem, self.base + c - n)
                act.activation(sq[c % n] if c else self.total, src, ACT.Square).then_inc(sq_ready.sem, 1)

            def add(self, dve, c):
                dve.wait_ge(sq_ready.sem, self.base + c + 1)
                if c >= 2:
                    dve.wait_ge(sq_used.sem, self.base + c - 1)
                dve.tensor_tensor(self.total, self.total, sq[c % len(sq)], ALU.add).then_inc(sq_used.sem, 1)

            def sum(self, pe):
                if self.gbase > 0:
                    pe.wait_ge(log_ready.sem, self.gbase)
                pe.wait_ge(sq_used.sem, self.base + self.chunks - 1)
                pe.matmul(self.bank[:], ones[:], self.total, start=True, stop=True).then_inc(sq_used.sem, 1)

        class Split:

            def __init__(self, per, turns=1):
                self.whole, self.high, self.low = (shared(f"split_{k}", per, turns) for k in ("whole", "hi", "lo"))

            def free(self, dve, c, i=0):
                sem, value = self.low.at(c - 2 if c >= 2 else -1, i)
                if not isinstance(value, int) or value > 0:
                    dve.wait_ge(sem, value)

            def round(self, act, dst, c, i=0):
                act.wait_ge(*self.whole.at(c, i))
                act.copy(dst, tmp[c % 2]).then_inc(self.high.sem, 1)

            def rest(self, dve, dst, hi, c, i=0):
                dve.wait_ge(*self.high.at(c, i))
                dve.tensor_tensor(dst, tmp[c % 2], hi.bitcast(F32), ALU.subtract).then_inc(self.low.sem, 1)

        def open_unit(pe, st, j, i):
            pe.wait_ge(lo_split, st.done(j, i))
            if st.base + j >= RING:
                pe.wait_ge(bank_free[st.bank(j)], st.uses(j, i))

        def unit_chunk(pe, st, j, k, kc, hi, lo, k0=0):
            r = st.bank(j)
            w = slice(k * P, k * P + P)
            xh, xl = tile(hi, k0 + k), tile(lo, k0 + k)
            pe.matmul(psum[r][:], w_hi[r][:, w], xh, start=k == 0, stop=False)
            pe.matmul(psum[r][:], w_hi[r][:, w], xl, start=False, stop=False)
            last = pe.matmul(psum[r][:], w_lo[r][:, w], xh, start=False, stop=k == kc - 1)
            if k == kc - 1:
                last.then_inc(unit_done, 1)

        def unit(pe, st, j, kc, hi, lo, i=0, k0=0, ready=None):
            open_unit(pe, st, j, i)
            for k in range(kc):
                if ready:
                    pe.wait_ge(*ready(k))
                unit_chunk(pe, st, j, k, kc, hi, lo, k0)

        def units_together(pe, st, js, kc, hi, lo, i, ready):
            for j in js:
                open_unit(pe, st, j, i)
            for k in range(kc):
                pe.wait_ge(*ready(k))
                for j in js:
                    unit_chunk(pe, st, j, k, kc, hi, lo)

        def unit_pair(pe, st, j, kc, hi, lo, i, ready):
            for u in (j, j + 1):
                open_unit(pe, st, u, i)
                for k in range(kc - 1):
                    if u == j:
                        pe.wait_ge(*ready(k))
                    unit_chunk(pe, st, u, k, kc, hi, lo)
            pe.wait_ge(*ready(kc - 1))
            for u in (j, j + 1):
                unit_chunk(pe, st, u, kc - 1, kc, hi, lo)

        def arrived(eng, st, j, i=0):
            eng.wait_ge(unit_done, st.done(j, i))
            return psum[st.bank(j)]

        def taken(st, j):
            return bank_free[st.bank(j)], 1

        def emptied(eng, st, j, i=0):
            eng.wait_ge(bank_free[st.bank(j)], st.uses(j, i) + 1)

        class PreNorm:

            def __init__(self, gain_name, gain_at):
                self.norm = Norm(DC)
                self.split = Split(DC)
                self.gain = (gain_name, gain_at)

            def act(self, act, h_at):
                for c in range(DC):
                    act.wait_ge(*h_at(c))
                    self.norm.square(act, tile(hT, c), c)
                self.norm.root(act)
                for c in range(DC):
                    self.split.round(act, tile(a_hi, c), c)

            def pe(self, pe):
                for c in range(DC):
                    self.norm.sum(pe, c)

            def dve(self, dve):
                dve.wait_ge(*self.norm.ready())
                for c in range(DC + 1):
                    if c < DC:
                        self.split.free(dve, c)
                        dve.scalar_tensor_tensor(tmp[c % 2], tile(hT, c), gain(self.gain[0], self.gain[1] + c), rstd,
                                                 ALU.mult, ALU.mult).then_inc(self.split.whole.sem, 1)
                    if c >= 1:
                        self.split.rest(dve, tile(a_lo, c - 1), tile(a_hi, c - 1), c - 1)

            def ready(self, k):
                return self.split.low.at(k)

        class LateNorm:

            def __init__(self, gain_name, gain_at, total):
                self.norm = AddedNorm(DC, total)
                self.high, self.low = shared("late_hi", DC), shared("late_lo", DC)
                self.gain = (gain_name, gain_at)

            def column(self, c):
                return gain(self.gain[0], self.gain[1] + c)

            def act(self, act, h_at):
                for c in range(DC):
                    act.wait_ge(*h_at(c))
                    act.activation(tile(a_hi, c), tile(hT, c), ACT.Identity, bias=zero,
                                   scale=self.column(c)).then_inc(self.high.sem, 1)
                for c in range(DC):
                    self.norm.square(act, tile(hT, c), c)
                self.norm.root(act)

            def rest(self, dve, c):
                dve.wait_ge(*self.high.at(c))
                dve.scalar_tensor_tensor(tile(a_lo, c), tile(hT, c), self.column(c), tile(a_hi, c).bitcast(F32),
                                         ALU.mult, ALU.subtract).then_inc(self.low.sem, 1)

            def adds(self, dve):
                for c in range(1, DC):
                    self.norm.add(dve, c)
                dve.wait_ge(*self.norm.ready())

        class PostNorm:

            def __init__(self, gain_at, total):
                self.norm = AddedNorm(DC, total)
                self.scaled, self.added = shared("post_scaled", DC), shared("post_added", DC)
                self.gain_at = gain_at

            def dve(self, dve, then=None):
                dve.wait_ge(*self.norm.ready())
                for c in range(DC + 2):
                    if c < DC:
                        if c >= 2:
                            dve.wait_ge(*self.added.at(c - 2))
                        dve.scalar_tensor_tensor(tmp[c % 2], tile(acc, c), gain("norm", self.gain_at + c), rstd,
                                                 ALU.mult, ALU.mult).then_inc(self.scaled.sem, 1)
                    if 1 <= c <= DC:
                        dve.wait_ge(*self.scaled.at(c - 1))
                        dve.tensor_tensor(tile(hT, c - 1), tile(hT, c - 1), tmp[(c - 1) % 2],
                                          ALU.add).then_inc(self.added.sem, 1)
                    if c >= 2 and then:
                        then.rest(dve, c - 2)

        class Attention:

            def __init__(self, heads, turns, scale, pr, pt, row_scale=None):
                self.heads, self.scale, self.pr, self.pt, self.row_scale = heads, scale, pr, pt, row_scale
                self.n = n = heads * TB
                s = lambda k: shared(f"attn_{k}", n, turns)
                self.scores, self.masked, self.exped, self.inverted, self.normed, self.turned, self.turned_out = (
                    s(k) for k in ("scores", "masked", "exped", "inverted", "normed", "turned", "turned_out"))
                self.biased = s("biased") if row_scale else self.masked
                self.out = shared("attn_out", heads, turns)
                self.out_hi = shared("attn_out_hi", heads, turns)
                self.out_lo = shared("attn_out_lo", heads, turns)
                self.s_bank = [aux[0], aux[1], psum[2], psum[3]]
                self.t_bank, self.o_bank = [aux[2], psum[0]], [aux[3], psum[1]]

            def keys(self, t):
                return (t % TB + 1) * P

            def pe(self, pe, i, score, values):
                for s in range(self.n + 4):
                    if s < self.n:
                        score(s, self.s_bank[s % RING], self.keys(s)).then_inc(self.scores.sem, 1)
                    t = s - 3
                    if 0 <= t < self.n:
                        pe.wait_ge(*self.normed.at(t, i))
                        for kb in range(t % TB + 1):
                            k = slice(kb * P, kb * P + P)
                            last = pe.transpose(self.t_bank[t % 2][:, k], self.pr[t % RING][:, k], ident[:])
                        last.then_inc(self.turned.sem, 1)
                    t = s - 4
                    if t >= 0:
                        hh, b = t // TB, t % TB
                        if b == 0 and hh >= 2:
                            pe.wait_ge(*self.out_lo.at(hh - 2, i))
                        pe.wait_ge(*self.turned_out.at(t, i))
                        for kb in range(b + 1):
                            last = pe.matmul(self.o_bank[hh % 2][:, b * P:b * P + P], values(hh, kb),
                                             self.pt[t % 2][:, kb * P:kb * P + P], start=kb == 0, stop=kb == b)
                        if b == TB - 1:
                            last.then_inc(self.out.sem, 1)
                pe.wait_ge(*self.out_lo.at(self.heads - 1, i))

            def dve(self, dve, i, bias, out_lo, out_hi):
                for s in range(self.n + 6):
                    if s < self.n:
                        w, r = self.keys(s), slice(s % RING, s % RING + 1)
                        dve.wait_ge(*self.scores.at(s, i))
                        plain_wait(dve, s % RING)
                        dve.tensor_tensor_reduce(self.pr[s % RING][:, 0:w], self.s_bank[s % RING][:, 0:w], bias(s), -self.scale,
                                                 -GONE, ALU.add, ALU.min, row_min[:, r]).then_inc(self.masked.sem, 1)
                        if self.row_scale:
                            dve.wait_ge(*self.masked.at(s, i))
                            dve.tensor_scalar(row_bias[:, r], row_min[:, r], self.row_scale(s)[0], None,
                                              ALU.mult).then_inc(self.biased.sem, 1)
                    t = s - 1
                    if 0 <= t < self.n:
                        w, r = self.keys(t), slice(t % RING, t % RING + 1)
                        dve.wait_ge(*self.exped.at(t, i))
                        dve.reciprocal(row_inv[:, r], row_sum[:, r]).then_inc(self.inverted.sem, 1)
                        dve.wait_ge(*self.inverted.at(t, i))
                        dve.tensor_scalar(self.pr[t % RING][:, 0:w], self.pr[t % RING][:, 0:w], row_inv[:, r], None,
                                          ALU.mult).then_inc(self.normed.sem, 1)
                    hh = (s - 6) // TB
                    if s >= 6 and s - 6 == hh * TB + TB - 1:
                        dve.wait_ge(*self.out_hi.at(hh, i))
                        dve.tensor_tensor(out_lo(hh), self.o_bank[hh % 2][:], out_hi(hh).bitcast(F32),
                                          ALU.subtract).then_inc(self.out_lo.sem, 1)

            def act(self, act, i, out_hi):
                for s in range(self.n + 5):
                    t = s - 3
                    if 0 <= t < self.n:
                        w = self.keys(t)
                        act.wait_ge(*self.turned.at(t, i))
                        act.copy(self.pt[t % 2][:, 0:w], self.t_bank[t % 2][:, 0:w]).then_inc(self.turned_out.sem, 1)
                    if s < self.n:
                        w, r = self.keys(s), slice(s % RING, s % RING + 1)
                        act.wait_ge(*self.biased.at(s, i))
                        act.activation(self.pr[s % RING][:, 0:w], self.pr[s % RING][:, 0:w], ACT.Exp,
                                       bias=(row_bias if self.row_scale else row_min)[:, r],
                                       scale=self.row_scale(s)[1] if self.row_scale else -1.0,
                                       accum_out=row_sum[:, r]).then_inc(self.exped.sem, 1)
                    hh = (s - 5) // TB
                    if s >= 5 and s - 5 == hh * TB + TB - 1:
                        act.wait_ge(*self.out.at(hh, i))
                        act.copy(out_hi(hh), self.o_bank[hh % 2][:]).then_inc(self.out_hi.sem, 1)

        def causal(table, b):
            return tab[table][:, (TB - 1 - b) * P:T]


        def turn_block(pe, bank, src):
            for b in range(TB):
                last = pe.transpose(bank[:, b * P:b * P + P], src[:, b * P:b * P + P], ident[:])
            return last

        pre_mla = PreNorm("norm", 0)
        mla_c = [tile(F, 6 + c) for c in range(6)]
        k_rope, rope_cos, rope_sin = tile(F, 12), tile(F, 13), tile(F, 14)
        pos_i, pos_f, angle, cycles, reduced = (tile(F, 15 + k) for k in range(5))
        n_cq, n_ckv = Norm(MLA_Q // P), Norm(MLA_KV // P)
        s_c = Split(6)
        angle_ready, sin_ready = signal("angle_ready"), signal("sin_ready")
        rope_part, k_rope_ready = signal("rope_part"), signal("k_rope_ready")
        qn, q_rope, kn = [tile(F, 6 + k) for k in range(4)], [tile(F, 10), tile(F, 11)], [tile(F, 15 + k) for k in range(4)]
        vT, vtok = [tile(F, 19), tile(acc, 7)], [tile(acc, k) for k in range(4)]
        q_rope_ready = signal("q_rope_ready", 2)
        v_turned, v_ready = signal("v_turned", MLA_TURN), signal("v_ready", MLA_TURN)
        V_AFTER = {6: 0, 8: 1, 14: 2, 15: 3}
        at_mla = Attention(MLA_TURN, MLA_HEADS // MLA_TURN, MLA_SCALE, [tile(acc, 4 + k) for k in range(3)] + [log_ms], sq)
        post_mla = PostNorm(8, tile(F, 6))

        class Mlp:

            def __init__(self, l):
                self.l, self.st = l, st_mlp[l]
                self.pre = LateNorm("norm", 32 * l + 16, tile(F, 8))
                self.split = Split(DC, self.st.turns)
                self.cleared = shared("mlp_cleared")
                self.post = PostNorm(32 * l + 24, tile(F, 9))
                self.relu = [tile(F, 6), tile(F, 7)]

            def pe(self, pe):
                def block(i, first):
                    if first:
                        units_together(pe, self.st, range(3), DC, a_hi, a_lo, i, self.pre.low.at)
                    for j in range(3 if first else 0, DC):
                        unit(pe, self.st, j, DC, a_hi, a_lo, i)
                        if first and j == 3:
                            self.pre.norm.sum(pe)
                    for m in range(DC):
                        unit(pe, self.st, DC + m, DC, g_hi, g_lo, i,
                             ready=(lambda k: self.split.low.at(k, i)) if m == 0 else None)
                turns_from(pe, self.st.turns, block)
                self.post.norm.sum(pe)

            def act(self, act, h_at):
                self.pre.act(act, h_at)

                def block(i):
                    for j in range(DC):
                        self.split.round(act, tile(g_hi, j), j, i)
                turns(act, self.st.turns, block)
                for c in range(DC):
                    emptied(act, self.st, DC + c, self.st.turns - 1)
                    self.post.norm.square(act, tile(acc, c), c)
                self.post.norm.root(act)

            def dve(self, dve, then=None):
                dve.memset(acc[:], 0.0).then_inc(self.cleared.sem, 1)
                dve.wait_ge(*self.cleared.at(0))
                self.pre.adds(dve)

                def block(i, last):
                    for j in range(DC + 1):
                        if j < DC:
                            bank = arrived(dve, self.st, j, i)
                            dve.scalar_tensor_tensor(self.relu[j % 2], bank[:], 0.0, rstd, ALU.max,
                                                     ALU.mult).then_inc(*taken(self.st, j))
                            emptied(dve, self.st, j, i)
                            self.split.free(dve, j, i)
                            dve.tensor_tensor(tmp[j % 2], self.relu[j % 2], self.relu[j % 2],
                                              ALU.mult).then_inc(self.split.whole.sem, 1)
                        if j >= 1:
                            self.split.rest(dve, tile(g_lo, j - 1), tile(g_hi, j - 1), j - 1, i)
                    for m in range(DC):
                        bank = arrived(dve, self.st, DC + m, i)
                        dve.tensor_tensor(tile(acc, m), bank[:], tile(acc, m), ALU.add).then_inc(*taken(self.st, DC + m))
                        if last and m >= 2:
                            self.post.norm.add(dve, m - 1)
                with dve.Fori(0, self.st.turns - 1) as i:
                    block(i, False)
                block(self.st.turns - 1, True)
                self.post.norm.add(dve, DC - 1)
                self.post.dve(dve, then)

        class OutProj:

            def __init__(self, st, hi, lo, post):
                self.st, self.hi, self.lo, self.post = st, hi, lo, post

            def early(self, pe, js, ready):
                for m in js:
                    open_unit(pe, self.st, m, 0)
                    for k in range(DC - 1):
                        if m == 0:
                            pe.wait_ge(*ready(k))
                        unit_chunk(pe, self.st, m, k, DC, self.hi, self.lo)

            def pe(self, pe, ready, begun=0):
                if begun:
                    pe.wait_ge(*ready(DC - 1))
                for m in range(begun):
                    unit_chunk(pe, self.st, m, DC - 1, DC, self.hi, self.lo)
                for m in range(begun, DC):
                    unit(pe, self.st, m, DC, self.hi, self.lo, ready=ready if m == 0 else None)
                self.post.norm.sum(pe)

            def act(self, act):
                for m in range(DC):
                    bank = arrived(act, self.st, m)
                    self.post.norm.square(act, bank[:], m)
                    act.copy(tile(acc, m), bank[:]).then_inc(*taken(self.st, m))
                self.post.norm.root(act)

            def dve(self, dve, then):
                for m in range(1, DC):
                    self.post.norm.add(dve, m)
                emptied(dve, self.st, DC - 1)
                self.post.dve(dve, then)

        out_mla = OutProj(st_mla_o, a_hi, a_lo, post_mla)
        mlp = [Mlp(0)]

        pre_hg = LateNorm("norm", 32, tile(F, 7))
        hg_factor = tile(F, 6)
        hg_sig, hg_q, hg_k, hg_f, hg_b, hg_logf = (tile(F, k) for k in (7, 9, 10, 11, 12, 13))
        hg_d, hg_d2 = tile(F, 11), tile(F, 8)
        hg_vT = tile(F, 14)
        hg_e = [tile(F, 15 + k) for k in range(4)]
        hg_qdec = tile(F, 19)
        hg_qrel, hg_krel, hg_dec, hg_kdec = hg_e
        hg_state, hg_v, hg_kT, hg_a, hg_gate = tile(acc, 0, 4 * T), tile(acc, 4), tile(acc, 5), tile(acc, 6), tile(acc, 7)
        hg_f_ready, hg_k_ready, hg_logf_ready, hg_b_ready, hg_d_ready, hg_d2_ready = (
            signal(f"hg_{n}_ready") for n in ("f", "k", "logf", "b", "d", "d2"))
        hg_e_ready = signal("hg_e_ready", 4)
        hg_factor_ready = signal("hg_factor_ready")
        hg_q_ready, hg_sig_ready, hg_gate_ready = (signal(f"hg_{n}_ready") for n in ("q", "sig", "gate"))
        hg_rel_ready, hg_dec_ready = signal("hg_rel_ready", 2), signal("hg_dec_ready", 2)
        hg_cleared = signal("hg_cleared")
        hg_scores, hg_masked = signal("hg_scores"), signal("hg_masked")
        hg_v_turned, hg_v_ready, hg_k_turned, hg_kT_ready = (
            signal(f"hg_{n}") for n in ("v_turned", "v_ready", "k_turned", "kT_ready"))
        hg_u, hg_state_ready = signal("hg_u"), signal("hg_state_ready", HG_N - 1)
        hg_o, hg_y = signal("hg_o"), signal("hg_y", credit=1)
        n_hg = Norm(1, turns=HG_HEADS, bank=aux[1])
        s_hg = Split(1, HG_HEADS)
        post_hg = PostNorm(40, tile(F, 7))
        out_hg = OutProj(st_hg_o, g_hi, g_lo, post_hg)
        mlp.append(Mlp(1))

        pre_dsa = LateNorm("mix", 0, tile(F, 14))
        dsa_factor = tile(F, 15)
        idx_q, idx_k = [tile(F, 6 + c) for c in range(4)], tile(F, 10)
        dsa_cT, dsa_kT, dsa_c = tile(F, 11), tile(F, 12), tile(F, 13)
        dsa_bias = [tile(F, 14 + b) for b in range(TB)]
        idx_rel = [tile(F, 18), tile(F, 19)]
        wiT = tile(F, 19)
        dsa_q = tile(F, 18)
        NG = 6
        n_iq = Norm(IDX_HEADS // 2, size=IDX_DIM, bank=aux[1])
        n_ik = Norm(1, matrix=ones_half, size=IDX_DIM)
        n_key = Norm(1, bank=aux[2])
        idx_ready, key_ready = signal("idx_ready"), signal("key_ready")
        c_turned, c_ready = signal("c_turned"), signal("c_ready")
        wi_turned, wi_ready, wi_scaled = signal("wi_turned"), signal("wi_ready"), signal("wi_scaled")
        dsa_factor_ready, r_sums, r_ready, r_factors = (signal(n) for n in ("dsa_factor_ready", "r_sums", "r_ready", "r_factors"))
        rel_ready, rel_taken, weighted, scored = (signal(n) for n in ("rel_ready", "rel_taken", "weighted", "scored"))
        idx_w = [tile(F, 4 * TB + k, P) for k in range(2)]
        dsa_bias_ready = signal("dsa_bias_ready")
        n_dq = Norm(DSA_HEADS, size=DSA_LAT, bank=aux[2])
        DSA_TURN = 4
        dsa_q = [tile(F, 6 + k) for k in range(DSA_TURN)]
        dsa_q_ready = signal("dsa_q_ready", DSA_TURN)
        q_rstd_turn = signal("q_rstd_turn", 2)
        at_dsa = Attention(DSA_TURN, DSA_HEADS // DSA_TURN, DSA_SCALE, [tile(F, k) for k in (10, 11, 18, 19)], sq,
                           lambda t: (q_rstd[:, t:t + 1], q_rstd_neg[:, t:t + 1]))
        REL = [(b, h) for b in range(1, TB) for h in range(IDX_HEADS)]
        Q0 = 7
        Q_AFTER = [range(0, 2), range(2, 4), range(4, 8)]

        class Ffn:

            def __init__(self, l):
                self.l = l
                self.pre = LateNorm("ffn", DC * l, tile(F, 14))
                self.u = [[tile(F, 6 + 2 * s + r) for r in range(2)] for s in range(2)]
                self.x = [[tile(F, 10 + 2 * s + r) for r in range(2)] for s in range(2)]
                self.parts = []
                for k, (st, first, size) in enumerate(st_ffn[l]):
                    self.parts.append((st, first, size, Split(size, st.turns), shared("ffn_tap2", 2 * size, st.turns),
                                       shared("ffn_tap1", 2 * size, st.turns), shared("ffn_tap0", 2 * size, st.turns),
                                       shared("ffn_silu", size, st.turns)))
                self.last = st_ffn[l][-1]

            def h_at(self, c):
                st, _, size = self.last
                return bank_free[st.bank(2 * size + c)], st.uses(2 * size + c) + 1

            def pe(self, pe):
                for st, first, size, split, *_ in self.parts:
                    def block(i, start):
                        start = start and first == 0
                        if start:
                            units_together(pe, st, range(2), DC, a_hi, a_lo, i, self.pre.low.at)
                            self.pre.norm.sum(pe)
                        for j in range(2 if start else 0, 2 * size):
                            unit(pe, st, j, DC, a_hi, a_lo, i)
                        unit_pair(pe, st, 2 * size, size, g_hi, g_lo, i, lambda c: split.low.at(c, i))
                        for m in range(2, DC):
                            unit(pe, st, 2 * size + m, size, g_hi, g_lo, i)
                    turns_from(pe, st.turns, block)

            def act(self, act, h_at):
                self.pre.act(act, h_at)
                l = self.l
                for st, first, size, split, tap2, tap1, tap0, silu in self.parts:
                    def block(i):
                        for j in range(size):
                            for s in range(2):
                                c = i * DC + first + j + s * FF2C
                                u = self.u[s][j % 2]
                                emptied(act, st, 2 * j + s, i)
                                act.activation(u, self.x[s][j % 2], ACT.Identity, bias=conv_col(l, 3, c),
                                               scale=conv_col(l, 2, c)).then_inc(tap2.sem, 1)
                                if s == 0:
                                    act.wait_ge(*tap0.at(2 * j, i))
                                    act.activation(u, u, ACT.Silu).then_inc(silu.sem, 1)
                            split.round(act, tile(g_hi, j), j, i)
                    turns(act, st.turns, block)

            def dve(self, dve):
                for c in range(DC):
                    self.pre.rest(dve, c)
                self.pre.adds(dve)
                l = self.l
                for st, first, size, split, tap2, tap1, tap0, silu in self.parts:
                    def block(i):
                        for j in range(size):
                            for s in range(2):
                                u, x, n = self.u[s][j % 2], self.x[s][j % 2], 2 * j + s
                                bank = arrived(dve, st, n, i)
                                dve.tensor_tensor(x, bank[:], rstd, ALU.mult).then_inc(*taken(st, n))
                                if s == 0 and j >= 1:
                                    split.rest(dve, tile(g_lo, j - 1), tile(g_hi, j - 1), j - 1, i)
                                for k in (1, 0):
                                    back = 2 - k
                                    dve.wait_ge(*(tap2 if k else tap1).at(n, i))
                                    dve.scalar_tensor_tensor(
                                        u[:, back:T], x[:, 0:T - back], conv_col(l, k, i * DC + first + j + s * FF2C),
                                        u[:, back:T], ALU.mult, ALU.add).then_inc((tap1 if k else tap0).sem, 1)
                            dve.wait_ge(*silu.at(j, i))
                            dve.wait_ge(*tap0.at(2 * j + 1, i))
                            split.free(dve, j, i)
                            dve.tensor_tensor(tmp[j % 2], self.u[0][j % 2], self.u[1][j % 2],
                                              ALU.mult).then_inc(split.whole.sem, 1)
                        split.rest(dve, tile(g_lo, size - 1), tile(g_hi, size - 1), size - 1, i)
                        for m in range(DC):
                            bank = arrived(dve, st, 2 * size + m, i)
                            dve.tensor_tensor(tile(hT, m), bank[:], tile(hT, m),
                                              ALU.add).then_inc(*taken(st, 2 * size + m))
                    turns(dve, st.turns, block)

        ffn = [Ffn(0)]

        pre_ret = LateNorm("mix", DC, tile(F, 14))
        ret_factor = tab["scan_keep"]
        ret_factors = signal("ret_factors", 3)
        ret_q, ret_k = [tile(F, 6), tile(F, 7)], [tile(F, 8), tile(F, 9)]
        ret_vtok = F[:, 10 * T:14 * T]
        ret_gate = [tile(F, 14 + m) for m in range(4)]
        ret_vT = [tile(F, 18), tile(F, 19)]
        ret_s = [tile(acc, j) for j in range(TB)]
        ret_raw = [tile(acc, 4 + m) for m in range(4)]
        RV = RET_DV // P
        ret_part, ret_qk_ready = signal("ret_part", 4), signal("ret_qk_ready", 4)
        ret_v_turned, ret_v_ready = signal("ret_v_turned", RV), signal("ret_v_ready", RV)
        ret_scores, ret_s_ready = signal("ret_scores", TB), signal("ret_s_ready", TB)
        ret_o, ret_raw_ready, ret_y = signal("ret_o", RV), signal("ret_raw_ready", RV, credit=1), signal("ret_y", RV)
        n_ret = Norm(RV, turns=RET_HEADS, size=RET_DV)
        s_ret = Split(RV, RET_HEADS)
        ffn.append(Ffn(1))

        out_turned, out_ready = signal("out_turned"), signal("out_ready")

        block = ctx.enter_context(nc.Block())

        @block.sync
        def _(sp):
            sp.wait_ge(x_in, 16)
            for st in stages:
                def load(i):
                    for q, s in enumerate(st.slabs):
                        if st.slab_base + q >= 2:
                            sp.wait_ge(lo_split, st.raw_free(q, i))
                        v = raw_view(st.slot(q), s)
                        for c, n, src in s.parts(i):
                            sp.dma_start(v[:, :, c:c + n], src).then_inc(loaded[st.slot(q)], 16)
                turns(sp, st.turns, load)
            for b in range(TB):
                sp.wait_ge(*out_ready.at(2 * b + 1))
                sp.dma_start(out.rearrange("a t d -> (a t) d")[b * P:b * P + P, :], acc[:, b * D:b * D + D]).then_inc(stored, 16)
            sp.wait_ge(stored, 16 * TB)

        @block.gpsimd
        def _(pool):
            pool.wait_ge(first_in, FIRST_IN)
            for st in stages:
                def split(i):
                    for q, s in enumerate(st.slabs):
                        pool.wait_ge(loaded[st.slot(q)], st.loaded(q, i))
                        v = raw_view(st.slot(q), s)
                        for m in range(s.units):
                            j = st.first[q] + m
                            r = st.bank(j)
                            if st.base + j >= RING:
                                pool.wait_ge(unit_done, st.done(j - RING, i))
                            src = v[:, :, m * P:m * P + P]
                            hi = w_hi[r][:, 0:s.kc * P].rearrange("p (k n) -> p k n", k=s.kc)
                            lo = w_lo[r][:, 0:s.kc * P].rearrange("p (k n) -> p k n", k=s.kc)
                            pool.tensor_tensor(hi, src, zero.rearrange("p (a b) -> p a b", a=1).to_broadcast([P, s.kc, P]),
                                               ALU.subtract).then_inc(hi_split, 1)
                            pool.wait_ge(hi_split, st.done(j, i))
                            pool.tensor_tensor(lo, src, hi.bitcast(F32), ALU.subtract).then_inc(lo_split, 1)
                turns(pool, st.turns, split)

        @block.scalar
        def _(act):
            act.dma_start(pos_i.bitcast(I32), positions.partition_broadcast(P)).then_inc(first_in, 16)
            for k in FIRST_TABLES:
                act.dma_start(tab[k][:], tables[k]).then_inc(first_in, 16)
            act.dma_start(acc[:].rearrange("p (t d) -> p t d", t=TB),
                          x.rearrange("a (t p) d -> p (a t) d", p=P)).then_inc(x_in, 16)
            for dst, src in row_loads:
                act.dma_start(dst, src).then_inc(rows_in, 16)
            for k in TABLE_WIDTH:
                if k not in FIRST_TABLES:
                    dst = {"ret_cos": ret_cos, "ret_sin": ret_sin, "ret_decay": ret_decay}.get(k) or tab[k]
                    act.dma_start(dst[:], tables[k]).then_inc(tables_in, 16)
            act.dma_start(hg_mask[:], hg_mask_dram).then_inc(tables_in, 16)
            act.wait_ge(first_in, FIRST_IN)

            def sine(k, dst):
                act.wait_ge(*angle_ready.at(k))
                act.activation(dst, reduced, ACT.Sin).then_inc(sin_ready.sem, 1)
            sine(0, rope_sin)

            pre_mla.act(act, lambda c: h_ready.at(c))
            sine(1, rope_cos)
            act.wait_ge(*setup_lb_diff)
            act.activation(lb[:, DC:3 * DC], lb[:, DC:3 * DC], ACT.Exp).then_inc(lb_exp.sem, 1)

            def take_c(j):
                bank = arrived(act, st_mla_in, j)
                n, c = (n_cq, j) if j < 4 else (n_ckv, j - 4)
                n.square(act, bank[:], c)
                act.copy(mla_c[j], bank[:]).then_inc(*taken(st_mla_in, j))
            for j in range(5):
                take_c(j)
            n_cq.root(act)
            take_c(5)
            for c in range(4):
                s_c.round(act, tile(g_hi, c), c)
            n_ckv.root(act)
            for c in range(4, 6):
                s_c.round(act, tile(g_hi, c), c)

            def mla_heads(i):
                for a in range(2):
                    for j, dst in ((0, qn[2 * a]), (1, qn[2 * a + 1]), (4, kn[2 * a]), (5, vT[0]), (6, kn[2 * a + 1]), (7, vT[1])):
                        j += 8 * a
                        bank = arrived(act, st_mla, j, i)
                        act.copy(dst, bank[:]).then_inc(*taken(st_mla, j))
                        if j in V_AFTER:
                            hh = V_AFTER[j]
                            act.wait_ge(*v_turned.at(hh, i))
                            act.copy(vtok[hh], aux[2 + hh % 2][:]).then_inc(v_ready.sem, 1)
                at_mla.act(act, i, lambda hh: tile(a_hi, i * MLA_TURN + hh))
            turns(act, st_mla.turns, mla_heads)
            out_mla.act(act)
            mlp[0].act(act, post_mla.added.at)

            pre_hg.act(act, mlp[0].post.added.at)

            def hg_silu(j, x, done, i, f=ACT.Silu):
                emptied(act, st_hg, j, i)
                act.activation(x, x, f).then_inc(done.sem, 1)

            def hg_gates(i):
                hg_silu(0, hg_q, hg_q_ready, i)
                hg_silu(1, hg_sig, hg_sig_ready, i, ACT.Sigmoid)
                act.wait_ge(*hg_f_ready.at(0, i))
                act.activation(hg_logf, hg_f, ACT.Ln).then_inc(hg_logf_ready.sem, 1)
                act.wait_ge(*hg_d_ready.at(0, i))
                act.activation(hg_e[0], hg_d, ACT.Exp).then_inc(hg_e_ready.sem, 1)
                act.activation(hg_e[1], hg_d, ACT.Exp, scale=-1.0).then_inc(hg_e_ready.sem, 1)
                act.activation(hg_e[2], hg_b, ACT.Exp).then_inc(hg_e_ready.sem, 1)
                act.wait_ge(*hg_d2_ready.at(0, i))
                act.activation(hg_e[3], hg_d2, ACT.Exp).then_inc(hg_e_ready.sem, 1)

            def hg_turned(i):
                act.wait_ge(*hg_v_turned.at(0, i))
                act.copy(hg_v, aux[2][:]).then_inc(hg_v_ready.sem, 1)
                act.wait_ge(*hg_k_turned.at(0, i))
                act.copy(hg_kT, aux[1][:]).then_inc(hg_kT_ready.sem, 1)

            def hg_normed(i):
                act.wait_ge(*hg_o.at(0, i))
                n_hg.square(act, aux[0][:], 0, 0, i)
                n_hg.root(act, 0, i)
                s_hg.round(act, tile(g_hi, i), 0, i)
            hg_gates(0)
            hg_silu(3, hg_gate, hg_gate_ready, 0)
            with act.Fori(0, HG_HEADS - 1) as i:
                hg_turned(i)
                hg_gates(i + 1)
                hg_normed(i)
                hg_silu(3, hg_gate, hg_gate_ready, i + 1)
            hg_turned(HG_HEADS - 1)
            hg_normed(HG_HEADS - 1)
            out_hg.act(act)
            mlp[1].act(act, post_hg.added.at)

            pre_dsa.act(act, mlp[1].post.added.at)

            act.wait_ge(*r_sums.at(0))
            act.activation(r_log[:], aux[3][:, 0:TB], ACT.Ln, bias=eps, scale=1.0 / D).then_inc(r_ready.sem, 1)
            act.wait_ge(*r_ready.at(0))
            act.activation(r_square[:], r_log[:], ACT.Exp, scale=-1.0).then_inc(r_ready.sem, 1)
            for g in range(4):
                emptied(act, st_dsa, g)
                n_iq.square(act, idx_q[g], g)
            act.wait_ge(sq_used.sem, n_iq.base + n_iq.chunks)
            act.activation(iq_log[:], aux[1][:, 0:TB * IDX_HEADS], ACT.Ln, bias=eps,
                           scale=1.0 / IDX_DIM).then_inc(log_ready.sem, 1)
            act.wait_ge(log_ready.sem, n_iq.gbase + 1)
            act.activation(iq_rstd[:], iq_log[:], ACT.Exp, scale=-0.5).then_inc(rstd_ready.sem, 1)
            emptied(act, st_dsa, 4)
            n_ik.square(act, idx_k, 0)
            n_ik.root(act)
            emptied(act, st_dsa, 5)
            n_key.square(act, dsa_cT, 0)
            act.wait_ge(*c_turned.at(0))
            act.copy(dsa_c, aux[2][:]).then_inc(c_ready.sem, 1)
            act.wait_ge(*wi_turned.at(0))
            act.copy(wi_tok[:], aux[3][:, 0:TB * IDX_HEADS]).then_inc(wi_ready.sem, 1)
            act.wait_ge(*wi_scaled.at(0))
            for r, (b, h) in enumerate(REL):
                w = (b + 1) * P
                if r >= 2:
                    act.wait_ge(*weighted.at(r - 2))
                c = b * IDX_HEADS + h
                act.activation(idx_w[r % 2], ident[:], ACT.Identity, bias=zero, scale=wi_tok[:, c:c + 1])
                act.wait_ge(*rel_ready.at(r))
                act.activation(idx_rel[r % 2][:, 0:w], aux[r % 2][:, 0:w], ACT.Relu).then_inc(rel_taken.sem, 1)
                if r == IDX_HEADS - 1:
                    n_key.root(act, users=idx_ready.at(0))
                if h == IDX_HEADS - 1:
                    for q in Q_AFTER[b - 1]:
                        bank = arrived(act, st_dsa, Q0 + q)
                        n_dq.square(act, bank[:], q)
                        act.copy(tile(acc, q), bank[:]).then_inc(*taken(st_dsa, Q0 + q))
            act.wait_ge(sq_used.sem, n_dq.base + n_dq.chunks)
            act.wait_ge(*r_factors.at(1))
            by_block = lambda t, b: t.rearrange("p (c b) -> p c b", b=TB)[:, :, b:b + 1]
            for b in range(TB):
                last = act.activation(by_block(q_log[:], b), by_block(aux[2][:, 0:DSA_HEADS * TB], b), ACT.Ln, bias=eps,
                                      scale=r_square[:, b:b + 1])
            last.then_inc(log_ready.sem, 1)
            act.wait_ge(log_ready.sem, n_dq.gbase + 1)
            for b in range(TB):
                last = act.activation(by_block(q_rstds[:], b), by_block(q_log[:], b), ACT.Exp, scale=-0.5,
                                      bias=r_half_log[:, b:b + 1])
            last.then_inc(rstd_ready.sem, 1)
            emptied(act, st_dsa, Q0 + DSA_HEADS - 1)

            def dsa_heads(i):
                for hh in range(DSA_TURN):
                    act.copy(dsa_q[hh], tile(acc, i * DSA_TURN + hh)).then_inc(dsa_q_ready.sem, 1)
                at_dsa.act(act, i, lambda hh: tile(g_hi, i * DSA_TURN + hh))
            turns(act, DSA_HEADS // DSA_TURN, dsa_heads)
            ffn[0].act(act, lambda c: (bank_free[st_dsa_o.bank(c)], st_dsa_o.uses(c) + 1))

            pre_ret.act(act, ffn[0].h_at)

            def ret_head(st, i, h):
                for m in range(RV):
                    act.wait_ge(*ret_v_turned.at(m, h))
                    act.copy(ret_vtok.rearrange("p (b e) -> p b e", b=TB)[:, :, m * P:(m + 1) * P],
                             aux[2 + m % 2][:].rearrange("p (b e) -> p b e", b=TB)).then_inc(ret_v_ready.sem, 1)
                for m in range(RV):
                    emptied(act, st, 4 + m, i)
                    act.activation(ret_gate[m], ret_gate[m], ACT.Silu)
                for m in range(RV):
                    act.wait_ge(*ret_o.at(m, h))
                    n_ret.square(act, aux[2 + m % 2][:], m, 0, h)
                    act.copy(ret_raw[m], aux[2 + m % 2][:]).then_inc(ret_raw_ready.sem, 1)
                n_ret.root(act, 0, h)
                for m in range(RV):
                    s_ret.round(act, tile(g_hi, m), m, h)
            with act.Fori(0, RET_HEADS - 1) as i:
                ret_head(st_ret, i, i)
            ret_head(st_ret_end, 0, RET_HEADS - 1)
            ffn[1].act(act, lambda c: (bank_free[st_ret_end.bank(8 + c)], st_ret_end.uses(8 + c) + 1))

        @block.vector
        def _(dve):
            count = 0

            def step(ins):
                nonlocal count
                count += 1
                ins.then_inc(setup.sem, 1)
                dve.wait_ge(setup.sem, count)

            dve.sem_inc(hg_y.sem, 1)
            dve.sem_inc(ret_raw_ready.sem, 1)
            dve.wait_ge(first_in, FIRST_IN)
            step(dve.tensor_copy(pos_f, pos_i.bitcast(I32)))
            step(dve.tensor_scalar(angle, pos_f, inv_freq, None, ALU.mult))

            def reduce_angle(quarter):
                step(dve.tensor_scalar(cycles, angle, 1.0 / (2 * np.pi), quarter, ALU.mult, ALU.add))
                step(dve.tensor_scalar(cycles, cycles, ROUND, None, ALU.add))
                step(dve.tensor_scalar(cycles, cycles, -ROUND, None, ALU.add))
                if quarter:
                    dve.wait_ge(*sin_ready.at(0))
                for n, part in enumerate(TWO_PI):
                    step(dve.scalar_tensor_tensor(reduced, cycles, -part, reduced if n else angle, ALU.mult, ALU.add))
                step(dve.tensor_scalar(reduced, reduced, quarter * 2 * np.pi, None, ALU.add))
                dve.tensor_scalar(reduced, reduced, 3.1415925, -3.1415925, ALU.min, ALU.max).then_inc(angle_ready.sem, 1)
            reduce_angle(0.0)
            for c in range(DC):
                dve.wait_ge(*x_turned.at(c))
                dve.tensor_copy(tile(hT, c), aux[c % 2][:]).then_inc(h_ready.sem, 1)
            for k, (rows_t, n, c0) in enumerate(row_tiles):
                dve.wait_ge(*turned.at(k))
                dve.tensor_copy(cols[:, c0:c0 + n], aux[2 + k % 2][:, 0:n]).then_inc(turned_out.sem, 1)
            dve.wait_ge(*turned_out.at(5))
            reduce_angle(0.25)

            pre_mla.dve(dve)
            dve.wait_ge(*sin_ready.at(1))
            step(dve.tensor_scalar(rope_sin, rope_sin, rope_sign, None, ALU.mult))
            z = [lb[:, k * DC:k * DC + DC] for k in range(8)]
            l0, l1 = cols[:, 128:128 + DC], cols[:, 128 + DC:128 + 2 * DC]
            step(dve.tensor_tensor(z[0], l0, l1, ALU.max))
            dve.tensor_tensor(z[1], l0, z[0], ALU.subtract)
            dve.tensor_tensor(z[2], l1, z[0], ALU.subtract).then_inc(setup_lb_diff[0], 1)
            dve.wait_ge(*lb_exp.at(0))
            step(dve.tensor_tensor(z[3], z[1], z[2], ALU.add))
            step(dve.reciprocal(z[4], z[3]))
            step(dve.tensor_tensor(z[5], z[1], z[4], ALU.mult))
            step(dve.tensor_tensor(z[6], z[2], z[4], ALU.mult))
            step(dve.tensor_tensor(z[6], z[5], z[6], ALU.add))
            step(dve.tensor_tensor(z[6], z[6], z[5], ALU.subtract))
            step(dve.tensor_scalar(z[7], z[6], -1.0, 1.0, ALU.mult, ALU.add))
            step(dve.tensor_tensor(qk_gain[:], gain("dsa_q", 0), gain("dsa_k", 0), ALU.mult))
            step(dve.tensor_tensor(iqk_gain[:], gain("dsa_iq", 0), gain("dsa_ik", 0), ALU.mult))


            def normed_c(n, gain_name, first, count_c):
                dve.wait_ge(*n.ready())
                for c in range(count_c + 1):
                    if c < count_c:
                        s_c.free(dve, first + c)
                        dve.scalar_tensor_tensor(tmp[(first + c) % 2], mla_c[first + c], gain(gain_name, c), rstd,
                                                 ALU.mult, ALU.mult).then_inc(s_c.whole.sem, 1)
                    if c >= 1:
                        k = first + c - 1
                        s_c.rest(dve, tile(g_lo, k), tile(g_hi, k), k)
            normed_c(n_cq, "mla_q", 0, 4)
            normed_c(n_ckv, "mla_kv", 4, 2)
            dve.wait_ge(tables_in, TABLES_IN)

            def rotate(st, j, i, dst, done):
                for k, table in ((0, rope_cos), (1, rope_sin)):
                    bank = arrived(dve, st, j + k, i)
                    dve.tensor_tensor(tmp[k], bank[:], table, ALU.mult).then_inc(*taken(st, j + k))
                emptied(dve, st, j + 1, i)
                dve.tensor_tensor(dst, tmp[0], tmp[1], ALU.add).then_inc(done.sem, 1)
            dve.wait_ge(*s_c.low.at(5))
            rotate(st_mla_in, 6, 0, k_rope, k_rope_ready)
            dve.wait_ge(*k_rope_ready.at(0))

            def mla_heads(i):
                rotate(st_mla, 2, i, q_rope[0], q_rope_ready)
                dve.wait_ge(*q_rope_ready.at(0, i))
                rotate(st_mla, 10, i, q_rope[1], q_rope_ready)
                at_mla.dve(dve, i, lambda t: causal("causal", t % TB), lambda hh: tile(a_lo, i * MLA_TURN + hh),
                           lambda hh: tile(a_hi, i * MLA_TURN + hh))
            turns(dve, st_mla.turns, mla_heads)
            out_mla.dve(dve, mlp[0].pre)
            mlp[0].dve(dve, pre_hg)

            pre_hg.adds(dve)
            dve.tensor_copy(hg_factor, rstd).then_inc(hg_factor_ready.sem, 1)
            dve.wait_ge(*hg_factor_ready.at(0))
            dve.memset(hg_a, 0.0).then_inc(hg_cleared.sem, 1)
            dve.wait_ge(*hg_cleared.at(0))
            by_chunk = lambda t: t.rearrange("p (n c) -> p n c", n=HG_N)
            chunk_col = lambda t, c: by_chunk(t)[:, :, c:c + 1].to_broadcast([P, HG_N, HG_CHUNK])
            state = lambda n: hg_state[:, n * P:n * P + P]

            def hg_take(j, dst, i):
                bank = arrived(dve, st_hg, j, i)
                dve.tensor_tensor(dst, bank[:], hg_factor, ALU.mult).then_inc(*taken(st_hg, j))

            def hg_before(i):
                hg_take(0, hg_q, i)
                hg_take(1, hg_sig, i)
                dve.wait_ge(*hg_sig_ready.at(0, i))
                dve.tensor_scalar(hg_f, hg_sig, lb[:, bass.ds(7 * DC + i, 1)], lb[:, bass.ds(6 * DC + i, 1)],
                                  ALU.mult, ALU.add).then_inc(hg_f_ready.sem, 1)
                dve.wait_ge(*hg_f_ready.at(0, i))
                dve.tensor_scalar(hg_k, hg_f, -1.0, 1.0, ALU.mult, ALU.add).then_inc(hg_k_ready.sem, 1)
                hg_take(2, hg_vT, i)
                dve.wait_ge(*hg_logf_ready.at(0, i))
                dve.tensor_tensor_scan(hg_b, tab["scan_keep"][:], hg_logf, 0.0, ALU.mult, ALU.add).then_inc(hg_b_ready.sem, 1)
                dve.wait_ge(*hg_b_ready.at(0, i))
                dve.wait_ge(*hg_k_ready.at(0, i))
                dve.tensor_tensor(by_chunk(hg_d), by_chunk(hg_b), chunk_col(hg_b, HG_CHUNK // 2),
                                  ALU.subtract).then_inc(hg_d_ready.sem, 1)
                dve.tensor_tensor(by_chunk(hg_d2), chunk_col(hg_b, HG_CHUNK - 1), by_chunk(hg_b),
                                  ALU.subtract).then_inc(hg_d2_ready.sem, 1)
                dve.wait_ge(*hg_q_ready.at(0, i))
                dve.wait_ge(*hg_e_ready.at(0, i))
                dve.tensor_tensor(hg_qrel, hg_e[0], hg_q, ALU.mult).then_inc(hg_rel_ready.sem, 1)
                dve.wait_ge(*hg_e_ready.at(1, i))
                dve.tensor_tensor(hg_krel, hg_e[1], hg_k, ALU.mult).then_inc(hg_rel_ready.sem, 1)
                dve.wait_ge(*hg_e_ready.at(2, i))
                if not (isinstance(i, int) and i == 0):
                    dve.wait_ge(*hg_o.at(0, i - 1))
                dve.tensor_tensor(hg_qdec, hg_e[2], hg_q, ALU.mult).then_inc(hg_dec_ready.sem, 1)
                dve.wait_ge(*hg_e_ready.at(3, i))
                dve.tensor_tensor(hg_kdec, hg_e[3], hg_k, ALU.mult).then_inc(hg_dec_ready.sem, 1)

            def hg_states(i):
                dve.wait_ge(*hg_scores.at(0, i))
                plain_wait(dve)
                dve.copy_predicated(hg_a.rearrange("p (g c) -> p g c", g=TB),
                                    hg_mask[:].rearrange("p (a c) -> p a c", a=1).to_broadcast([P, TB, P]),
                                    aux[3][:].rearrange("p (g c) -> p g c", g=TB)).then_inc(hg_masked.sem, 1)
                for n in range(HG_N - 1):
                    u = aux[n % HG_G][:, n // HG_G * P:n // HG_G * P + P]
                    if n == 0:
                        dve.wait_ge(*hg_u.at(0, i))
                        dve.tensor_copy(state(1), u).then_inc(hg_state_ready.sem, 1)
                    else:
                        dve.wait_ge(*hg_state_ready.at(n - 1, i))
                        last = (n + 1) * HG_CHUNK - 1
                        dve.scalar_tensor_tensor(state(n + 1), state(n), hg_dec[:, last:last + 1], u,
                                                 ALU.mult, ALU.add).then_inc(hg_state_ready.sem, 1)

            def hg_after(i):
                dve.wait_ge(*n_hg.ready(0, i))
                dve.scalar_tensor_tensor(tmp[1], aux[0][:], gain("hg_o", 0), rstd, ALU.mult, ALU.mult).then_inc(hg_y.sem, 1)
                dve.wait_ge(*hg_y.at(0, i))
                dve.wait_ge(*hg_gate_ready.at(0, i))
                s_hg.free(dve, 0, i)
                dve.tensor_tensor(tmp[0], tmp[1], hg_gate, ALU.mult).then_inc(s_hg.whole.sem, 1)
                s_hg.rest(dve, tile(g_lo, i), tile(g_hi, i), 0, i)
            hg_before(0)
            hg_take(3, hg_gate, 0)
            with dve.Fori(0, HG_HEADS - 1) as i:
                hg_states(i)
                hg_before(i + 1)
                hg_after(i)
                hg_take(3, hg_gate, i + 1)
            hg_states(HG_HEADS - 1)
            hg_after(HG_HEADS - 1)
            out_hg.dve(dve, mlp[1].pre)
            mlp[1].dve(dve, pre_dsa)

            pre_dsa.adds(dve)
            dve.tensor_copy(dsa_factor, rstd).then_inc(dsa_factor_ready.sem, 1)
            dve.wait_ge(*dsa_factor_ready.at(0))
            for g, dst in enumerate(idx_q + [idx_k, dsa_cT]):
                bank = arrived(dve, st_dsa, g)
                dve.tensor_tensor(dst, bank[:], dsa_factor, ALU.mult).then_inc(*taken(st_dsa, g))
            dve.wait_ge(*r_ready.at(1))
            dve.tensor_scalar(r_square[:], r_square[:], 1.0 / DSA_LAT, None, ALU.mult).then_inc(r_factors.sem, 1)
            dve.tensor_scalar(r_half_log[:], r_log[:], -0.5, None, ALU.mult).then_inc(r_factors.sem, 1)
            dve.wait_ge(*n_ik.ready())
            dve.scalar_tensor_tensor(idx_k, idx_k, iqk_gain[:], rstd, ALU.mult, ALU.mult).then_inc(idx_ready.sem, 1)
            bank = arrived(dve, st_dsa, NG)
            dve.scalar_tensor_tensor(wiT[0:IDX_HEADS, :], bank[0:IDX_HEADS, :], IDX_SCALE, dsa_factor[0:IDX_HEADS, :],
                                     ALU.mult, ALU.mult).then_inc(*taken(st_dsa, NG))
            dve.wait_ge(*wi_ready.at(0))
            dve.wait_ge(*n_iq.ready())
            dve.tensor_tensor(wi_tok[:], wi_tok[:], iq_rstd[:], ALU.mult).then_inc(wi_scaled.sem, 1)
            for b in range(1, TB):
                w = (b + 1) * P
                score = dsa_bias[b][:, 0:w]
                dve.wait_ge(*weighted.at(b * IDX_HEADS - 1))
                dve.tensor_tensor(score, aux[3][:, 0:w], causal("admissible", b), ALU.add).then_inc(scored.sem, 1)
                dve.wait_ge(*scored.at(b - 1))
                rounds = TOPK // 8
                with dve.Fori(0, rounds):
                    dve.max(top8[:], score)
                    dve.drain()
                    dve.match_replace(score, top8[:], score, GONE)
                    dve.drain()
                dve.tensor_scalar(score, score, GONE / 2, NEG, ALU.is_gt, ALU.mult).then_inc(dsa_bias_ready.sem, 1)
                if b == 1:
                    dve.wait_ge(*n_key.ready())
                    dve.scalar_tensor_tensor(dsa_kT, dsa_cT, qk_gain[:], rstd, ALU.mult, ALU.mult).then_inc(key_ready.sem, 1)
            dve.wait_ge(*dsa_bias_ready.at(TB - 2))

            dve.wait_ge(*n_dq.ready())

            def dsa_heads(i):
                r = q_rstds[:, bass.ds(i * (DSA_TURN * TB), DSA_TURN * TB)]
                dve.tensor_copy(q_rstd[:], r).then_inc(q_rstd_turn.sem, 1)
                dve.tensor_scalar(q_rstd_neg[:], r, -1.0, None, ALU.mult).then_inc(q_rstd_turn.sem, 1)
                dve.wait_ge(*q_rstd_turn.at(1, i))
                at_dsa.dve(dve, i, lambda t: dsa_bias[t % TB][:, 0:(t % TB + 1) * P] if t % TB else causal("admissible", 0),
                           lambda hh: tile(g_lo, i * DSA_TURN + hh), lambda hh: tile(g_hi, i * DSA_TURN + hh))
            turns(dve, DSA_HEADS // DSA_TURN, dsa_heads)
            for m in range(DC):
                bank = arrived(dve, st_dsa_o, m)
                dve.tensor_tensor(tile(hT, m), bank[:], tile(hT, m), ALU.add).then_inc(*taken(st_dsa_o, m))
            ffn[0].dve(dve)

            for c in range(DC):
                pre_ret.rest(dve, c)
            pre_ret.adds(dve)
            for table in (ret_cos, ret_sin):
                dve.tensor_tensor(table[:], table[:], rstd, ALU.mult).then_inc(ret_factors.sem, 1)
            dve.tensor_copy(ret_factor[:], rstd).then_inc(ret_factors.sem, 1)
            dve.wait_ge(*ret_factors.at(2))

            def ret_rotate(st, j, i, h):
                s_ret.free(dve, 0, h)
                for s, dst in ((0, ret_q), (1, ret_k)):
                    if s:
                        dve.wait_ge(*ret_qk_ready.at(1, h))
                    u0, u1 = j + 2 * s, j + 2 * s + 1
                    p0, p1 = arrived(dve, st, u0, i), arrived(dve, st, u1, i)
                    dve.tensor_tensor(dst[0], p0[:], ret_cos[:], ALU.mult).then_inc(ret_part.sem, 1)
                    dve.tensor_tensor(tmp[0], p1[:], ret_sin[:], ALU.mult).then_inc(ret_part.sem, 1)
                    dve.tensor_tensor(tmp[1], p0[:], ret_sin[:], ALU.mult).then_inc(*taken(st, u0))
                    dve.tensor_tensor(dst[1], p1[:], ret_cos[:], ALU.mult).then_inc(*taken(st, u1))
                    dve.wait_ge(*ret_part.at(2 * s + 1, h))
                    dve.tensor_tensor(dst[0], dst[0], tmp[0], ALU.subtract).then_inc(ret_qk_ready.sem, 1)
                    emptied(dve, st, u1, i)
                    dve.tensor_tensor(dst[1], tmp[1], dst[1], ALU.add).then_inc(ret_qk_ready.sem, 1)

            def ret_head(st, i, h):
                def take(j, dst):
                    bank = arrived(dve, st, j, i)
                    dve.tensor_tensor(dst, bank[:], ret_factor[:], ALU.mult).then_inc(*taken(st, j))

                def decay(b):
                    w = T - b * P
                    dve.wait_ge(*ret_scores.at(b, h))
                    dve.tensor_tensor(ret_s[b][:, 0:w], aux[b % 2][:, 0:w], ret_decay[:, bass.ds(h * T, w)],
                                      ALU.mult).then_inc(ret_s_ready.sem, 1)
                for m in range(RV):
                    if m >= 2:
                        dve.wait_ge(*ret_v_turned.at(m - 2, h))
                    take(m, ret_vT[m % 2])
                decay(0)
                decay(1)
                take(4, ret_gate[0])
                take(5, ret_gate[1])
                decay(2)
                take(6, ret_gate[2])
                decay(3)
                take(7, ret_gate[3])
                dve.wait_ge(*n_ret.ready(0, h))
                for m in range(RV + 1):
                    if m < RV:
                        dve.scalar_tensor_tensor(ret_raw[m], ret_raw[m], gain("ret_out", h * RV + m), rstd, ALU.mult,
                                                 ALU.mult).then_inc(ret_y.sem, 1)
                        dve.wait_ge(*ret_y.at(m, h))
                        s_ret.free(dve, m, h)
                        dve.tensor_tensor(tmp[m % 2], ret_raw[m], ret_gate[m], ALU.mult).then_inc(s_ret.whole.sem, 1)
                    if m >= 1:
                        s_ret.rest(dve, tile(g_lo, m - 1), tile(g_hi, m - 1), m - 1, h)

            def ret_out(st, j, i):
                for m in range(DC):
                    bank = arrived(dve, st, j + m, i)
                    dve.tensor_tensor(tile(hT, m), bank[:], tile(hT, m), ALU.add).then_inc(*taken(st, j + m))
            ret_rotate(st_ret_qk, 0, 0, 0)
            with dve.Fori(0, RET_HEADS - 1) as i:
                ret_head(st_ret, i, i)
                ret_rotate(st_ret, 8, i, i + 1)
                ret_out(st_ret, 12, i)
            ret_head(st_ret_end, 0, RET_HEADS - 1)
            ret_out(st_ret_end, 8, 0)
            ffn[1].dve(dve)

            for k in range(2 * TB):
                dve.wait_ge(*out_turned.at(k))
                dve.tensor_copy(acc[:, k * T:k * T + T], aux[k % 4][:]).then_inc(out_ready.sem, 1)

        @block.tensor
        def _(pe):
            pe.wait_ge(first_in, FIRST_IN)
            pe.wait_ge(x_in, 16)
            for c in range(DC):
                if c >= 2:
                    pe.wait_ge(*h_ready.at(c - 2))
                for b in range(TB):
                    last = pe.transpose(aux[c % 2][:, b * P:b * P + P], acc[:, b * D + c * P:b * D + c * P + P], ident[:])
                last.then_inc(x_turned.sem, 1)
            pe.wait_ge(rows_in, 16 * len(row_loads))
            for k, (rows_t, n, c0) in enumerate(row_tiles):
                if k >= 2:
                    pe.wait_ge(*turned_out.at(k - 2))
                pe.transpose(aux[2 + k % 2][:, 0:n], rows_t[0:n, :], ident[0:n, 0:n]).then_inc(turned.sem, 1)

            pe.wait_ge(*h_ready.at(DC - 1))
            pre_mla.pe(pe)
            units_together(pe, st_mla_in, range(2), DC, a_hi, a_lo, 0, pre_mla.ready)
            for j in range(2, 8):
                unit(pe, st_mla_in, j, DC, a_hi, a_lo)
                for u in (0, 1) if j == 2 else (j - 1,):
                    if u < 6:
                        n, c = (n_cq, u) if u < 4 else (n_ckv, u - 4)
                        n.sum(pe, c)

            def mla_heads(i):
                for j in range(st_mla.per):
                    a, q = divmod(j, 8)
                    if q < 4:
                        unit(pe, st_mla, j, MLA_Q // P, g_hi, g_lo, i, ready=s_c.low.at if j == 0 else None)
                    else:
                        unit(pe, st_mla, j, MLA_KV // P, g_hi, g_lo, i, k0=4,
                             ready=(lambda k: s_c.low.at(4 + k)) if j == 4 else None)
                    if j in V_AFTER:
                        hh = V_AFTER[j]
                        emptied(pe, st_mla, 8 * (hh // 2) + 5 + 2 * (hh % 2), i)
                        if hh >= 2:
                            pe.wait_ge(*v_ready.at(hh - 2, i))
                        turn_block(pe, aux[2 + hh % 2], vT[hh % 2]).then_inc(v_turned.sem, 1)
                pe.wait_ge(*q_rope_ready.at(1, i))
                pe.wait_ge(*k_rope_ready.at(0))
                pe.wait_ge(*v_ready.at(MLA_TURN - 1, i))

                def score(t, o, w):
                    hh, b = t // TB, t % TB
                    h0 = hh % 2 * MLA_ROPE
                    pe.matmul(o[:, 0:w], qn[hh][:, b * P:b * P + P], kn[hh][:, 0:w], start=True, stop=False)
                    return pe.matmul(o[:, 0:w], q_rope[hh // 2][h0:h0 + MLA_ROPE, b * P:b * P + P],
                                     k_rope[h0:h0 + MLA_ROPE, 0:w], start=False, stop=True)
                at_mla.pe(pe, i, score, lambda hh, kb: vtok[hh][:, kb * P:kb * P + P])
            turns(pe, st_mla.turns, mla_heads)
            pe.wait_ge(tables_in, TABLES_IN)
            out_mla.pe(pe, lambda k: at_mla.out_lo.at(k))
            mlp[0].pe(pe)


            def hg_units(js, i):
                for j in js:
                    unit(pe, st_hg, j, DC, a_hi, a_lo, i)

            def hg_inside(i):
                pe.wait_ge(*hg_rel_ready.at(1, i))
                for g in range(TB):
                    s = slice(g * P, g * P + P)
                    last = pe.matmul(aux[3][:, s], hg_krel[:, s], hg_qrel[:, s], start=True, stop=True)
                last.then_inc(hg_scores.sem, 1)
                emptied(pe, st_hg, 2, i)
                turn_block(pe, aux[2], hg_vT).then_inc(hg_v_turned.sem, 1)
                pe.wait_ge(*hg_dec_ready.at(1, i))
                pe.wait_ge(log_ready.sem, i + n_hg.gbase)
                turn_block(pe, aux[1], hg_kdec).then_inc(hg_k_turned.sem, 1)

            def hg_outer(i):
                pe.wait_ge(*hg_v_ready.at(0, i))
                pe.wait_ge(*hg_kT_ready.at(0, i))
                pe.wait_ge(*hg_y.at(0, i - 1))

                def outer(g):
                    for c in range(HG_G):
                        t = slice(c * HG_CHUNK, (c + 1) * HG_CHUNK)
                        s = slice(g * P, g * P + P)
                        last = pe.matmul(aux[c][:, s], hg_kT[t, s], hg_v[t, s], start=True, stop=True)
                    return last

                pe.wait_ge(*hg_masked.at(0, i))
                for g in range(TB):
                    last = outer(g)
                last.then_inc(hg_u.sem, 1)

            def hg_output(i):
                def output(g):
                    s = slice(g * P, g * P + P)
                    last = pe.matmul(aux[0][:, s], hg_v[:, s], hg_a[:, s], start=True, stop=True,
                                     skip_group_check=True)
                    for c in range(HG_G):
                        n = g * HG_G + c
                        if n == 0:
                            continue
                        t = slice(n * HG_CHUNK, (n + 1) * HG_CHUNK)
                        last = pe.matmul(aux[0][:, t], hg_state[:, n * P:n * P + P], hg_qdec[:, t], start=False,
                                         stop=True, skip_group_check=True)
                    return last
                pe.wait_ge(*hg_state_ready.at(HG_N - 2, i))
                for g in range(TB):
                    last = output(g)
                last.then_inc(hg_o.sem, 1)
                n_hg.sum(pe, 0, 0, i)
            units_together(pe, st_hg, range(3), DC, a_hi, a_lo, 0, pre_hg.low.at)
            hg_units((3,), 0)
            pre_hg.norm.sum(pe)
            with pe.Fori(0, HG_HEADS - 1) as i:
                hg_units((0,), i + 1)
                hg_inside(i)
                hg_units((1,), i + 1)
                hg_outer(i)
                hg_units((2, 3), i + 1)
                hg_output(i)
            hg_ready = lambda k: s_hg.low.at(0, k)
            hg_inside(HG_HEADS - 1)
            out_hg.early(pe, (0, 1), hg_ready)
            hg_outer(HG_HEADS - 1)
            out_hg.early(pe, (2,), hg_ready)
            hg_output(HG_HEADS - 1)
            out_hg.early(pe, (3,), hg_ready)
            out_hg.pe(pe, hg_ready, 4)
            mlp[1].pe(pe)

            units_together(pe, st_dsa, range(3), DC, a_hi, a_lo, 0, pre_dsa.low.at)
            unit(pe, st_dsa, 3, DC, a_hi, a_lo)
            pre_dsa.norm.sum(pe)
            for b in range(TB):
                last = pe.matmul(aux[3][:, b:b + 1], pre_dsa.norm.total[:, b * P:b * P + P], ones[:, 0:1], start=True, stop=True)
            last.then_inc(r_sums.sem, 1)

            def iq_sums(cs):
                for c in cs:
                    n_iq.sum_tokens(pe, c, lambda b: b * IDX_HEADS + 2 * c, halves)
            unit(pe, st_dsa, 4, DC, a_hi, a_lo)
            iq_sums((0, 1))
            unit(pe, st_dsa, 5, DC, a_hi, a_lo)
            iq_sums((2, 3))
            n_ik.sum(pe, 0)
            unit(pe, st_dsa, 6, DC, a_hi, a_lo)
            pe.wait_ge(*r_ready.at(0))
            emptied(pe, st_dsa, 5)
            turn_block(pe, aux[2], dsa_cT).then_inc(c_turned.sem, 1)
            emptied(pe, st_dsa, NG)
            for b in range(TB):
                last = pe.transpose(aux[3][:, b * IDX_HEADS:(b + 1) * IDX_HEADS], wiT[0:IDX_HEADS, b * P:b * P + P],
                                    ident[0:IDX_HEADS, 0:IDX_HEADS])
            last.then_inc(wi_turned.sem, 1)
            pe.wait_ge(*idx_ready.at(0))
            def q_sums(c):
                n_dq.sum_tokens(pe, c, lambda b: c * TB + b, ones[:, 0:1])

            def weigh(r):
                b, h = REL[r]
                w = (b + 1) * P
                pe.wait_ge(*rel_taken.at(r))
                if h == 0 and b >= 2:
                    pe.wait_ge(*scored.at(b - 2))
                pe.matmul(aux[3][:, 0:w], idx_w[r % 2], idx_rel[r % 2][:, 0:w], start=h == 0,
                          stop=h == IDX_HEADS - 1).then_inc(weighted.sem, 1)

            for r, (b, h) in enumerate(REL):
                h0, w = h % 2 * IDX_DIM, (b + 1) * P
                pe.matmul(aux[r % 2][:, 0:w], idx_q[h // 2][h0:h0 + IDX_DIM, b * P:b * P + P], idx_k[h0:h0 + IDX_DIM, 0:w],
                          start=True, stop=True).then_inc(rel_ready.sem, 1)
                if h:
                    weigh(r - 1)
                if h == IDX_HEADS - 1:
                    weigh(r)
                if r == IDX_HEADS - 1:
                    pe.wait_ge(*c_ready.at(0))
                    n_key.sum(pe, 0)
                if h == IDX_HEADS - 1:
                    for q in Q_AFTER[b - 1]:
                        unit(pe, st_dsa, Q0 + q, DC, a_hi, a_lo)
                        if q:
                            q_sums(q - 1)
            q_sums(DSA_HEADS - 1)

            pe.wait_ge(*n_dq.ready())
            pe.wait_ge(*key_ready.at(0))

            def dsa_heads(i):
                def score(t, o, w):
                    hh, b = t // TB, t % TB
                    if b == 0:
                        pe.wait_ge(*dsa_q_ready.at(hh, i))
                    return pe.matmul(o[:, 0:w], dsa_q[hh][:, b * P:b * P + P], dsa_kT[:, 0:w], start=True, stop=True)
                at_dsa.pe(pe, i, score, lambda hh, kb: dsa_c[:, kb * P:kb * P + P])
            turns(pe, DSA_HEADS // DSA_TURN, dsa_heads)
            for m in range(DC):
                unit(pe, st_dsa_o, m, DC, g_hi, g_lo, ready=at_dsa.out_lo.at if m == 0 else None)
            ffn[0].pe(pe)

            units_together(pe, st_ret_qk, range(2), DC, a_hi, a_lo, 0, pre_ret.low.at)
            pre_ret.norm.sum(pe)
            for j in (2, 3):
                unit(pe, st_ret_qk, j, DC, a_hi, a_lo)

            def ret_head(st, i, h):
                def turn(m):
                    emptied(pe, st, m, i)
                    pe.wait_ge(*(ret_v_ready.at(m - 2, h) if m >= 2 else ret_raw_ready.at(-1, h)))
                    turn_block(pe, aux[2 + m % 2], ret_vT[m % 2]).then_inc(ret_v_turned.sem, 1)

                def scores(b):
                    w = T - b * P
                    pe.wait_ge(*ret_qk_ready.at(3, h))
                    if b >= 2:
                        pe.wait_ge(*ret_s_ready.at(b - 2, h))
                    for c in range(2):
                        last = pe.matmul(aux[b % 2][:, 0:w], ret_k[c][:, b * P:b * P + P], ret_q[c][:, b * P:T],
                                         start=c == 0, stop=c == 1)
                    last.then_inc(ret_scores.sem, 1)
                for m in range(RV):
                    unit(pe, st, m, DC, a_hi, a_lo, i)
                    if m >= 1:
                        turn(m - 1)
                scores(0)
                scores(1)
                for m in range(RV):
                    unit(pe, st, RV + m, DC, a_hi, a_lo, i)
                    if m == 0:
                        turn(RV - 1)
                    elif m <= 2:
                        scores(m + 1)
                pe.wait_ge(*ret_v_ready.at(RV - 1, h))
                for m in range(RV + 1):
                    if m < RV:
                        if m >= 2:
                            pe.wait_ge(*ret_raw_ready.at(m - 2, h))
                        for b in range(TB):
                            if m == 0:
                                pe.wait_ge(*ret_s_ready.at(b, h))
                            e = b * RET_DV + m * P
                            last = pe.matmul(aux[2 + m % 2][:, b * P:T], ret_vtok[:, e:e + P], ret_s[b][:, 0:T - b * P],
                                             start=b == 0, stop=b == TB - 1, skip_group_check=True)
                        last.then_inc(ret_o.sem, 1)
                    if m >= 1:
                        n_ret.sum(pe, m - 1, 0, h)

            def ret_out(st, j, i, h):
                for m in range(DC):
                    unit(pe, st, j + m, RET_DV // P, g_hi, g_lo, i,
                         ready=(lambda k: s_ret.low.at(k, h)) if m == 0 else None)
            with pe.Fori(0, RET_HEADS - 1) as i:
                ret_head(st_ret, i, i)
                for j in range(8, 12):
                    unit(pe, st_ret, j, DC, a_hi, a_lo, i)
                ret_out(st_ret, 12, i, i)
            ret_head(st_ret_end, 0, RET_HEADS - 1)
            ret_out(st_ret_end, 8, 0, RET_HEADS - 1)
            ffn[1].pe(pe)

            for c in range(DC):
                pe.wait_ge(*ffn[1].h_at(c))
            for k in range(2 * TB):
                b = k // 2
                if k >= 4:
                    pe.wait_ge(*out_ready.at(k - 4))
                for q in range(4):
                    c = k % 2 * 4 + q
                    last = pe.transpose(aux[k % 4][:, q * P:q * P + P], hT[:, c * T + b * P:c * T + b * P + P], ident[:])
                last.then_inc(out_turned.sem, 1)


_INS = ["x", "positions", "norm_gains", "mla_w_in", "mla_q_norm", "mla_kv_norm", "mla_w_uq", "mla_w_ukv", "mla_w_o",
        "hgrn_w_in", "hgrn_lb_logits", "hgrn_o_norm", "hgrn_w_o", "mlp_w1", "mlp_w2", "norm_mix_g_2", "norm_ffn_g_2",
        "a_w_in_2", "a_q_g_2", "a_k_g_2", "a_iq_g_2", "a_ik_g_2", "a_w_out_2", "b_w_in_2", "b_out_g_2", "b_w_out_2",
        "f_w_up_2", "f_conv_w_2", "f_conv_b_2", "f_w_down_2"]


def kernel(**inputs):
    import concourse.bacc as bacc
    from concourse.bass_utils import run_bass_kernel_spmd as run

    nc = bacc.Bacc("TRN2", target_bir_lowering=False, num_devices=1)
    arrays = {}

    def given(name, a):
        arrays[name] = a
        return nc.dram_tensor(name, a.shape, mybir.dt.from_np(a.dtype), kind="ExternalInput").ap()

    args = [given(f"in_{name}", np.ascontiguousarray(inputs[name])) for name in _INS]
    tabs, hg = shape_tables()
    tables = {k: given(f"table_{k}", np.ascontiguousarray(v)) for k, v in tabs.items()}
    hg_mask = given("table_hg_mask", hg)
    out = nc.dram_tensor("out_0", (1, T, D), F32, kind="ExternalOutput").ap()
    program(nc, *args, tables, hg_mask, out)
    r = run(nc, [arrays], core_ids=[0])
    return r.results[0]["out_0"]
```
